# Optimizing a Trainium2 kernel written in Bass

```python
import math
import jax, jax.numpy as jnp
from jax import lax
import numpy as np

D_MODEL = 1024
BATCH = 1
SEQ = 256
DEPTH = 1

MIX_WIDTH = D_MODEL
DN_HEADS = 4
DN_HEAD_DIM = MIX_WIDTH // 2 // DN_HEADS
DN_WIDTH = DN_HEADS * DN_HEAD_DIM
CONV_WIDTH = 4
CHUNK = 64
POOL_WINDOWS = (2, 4, 8, 16)
POOL_GROUPS = len(POOL_WINDOWS)
POOL_WIDTH = MIX_WIDTH - DN_WIDTH
POOL_GROUP_DIM = POOL_WIDTH // POOL_GROUPS
IN_WIDTH = 4 * DN_WIDTH + 2 * DN_HEADS + POOL_WIDTH
PEER_HEADS = 8
N_KEYS = 128
N_EXPERTS = N_KEYS * N_KEYS
PEER_QUERY_DIM = 256
PEER_HALF = PEER_QUERY_DIM // 2
PEER_TOPK = 16
PEER_TOKEN_BLOCK = 128
EPS = 1e-6


def _rmsnorm(x, w):
    xf = x.astype(jnp.float32)
    y = xf * lax.rsqrt(jnp.mean(xf * xf, axis=-1, keepdims=True) + EPS)
    return (y * w.astype(jnp.float32)).astype(x.dtype)

def _l2norm(x):
    return x * lax.rsqrt(jnp.sum(x * x, axis=-1, keepdims=True) + EPS)

def _causal_conv(x, w):
    c = x.shape[-1]
    return lax.conv_general_dilated(
        x, w[:, None, :].astype(x.dtype), window_strides=(1,),
        padding=((CONV_WIDTH - 1, 0),),
        dimension_numbers=("NWC", "WIO", "NWC"), feature_group_count=c)

def _chunk_gated_delta_rule(q, k, v, g, beta):
    b, s, h, dk = q.shape
    dv = v.shape[-1]
    n = s // CHUNK
    q = q * (dk ** -0.5)

    def to_chunks(t):
        return t.reshape(b, n, CHUNK, h, -1).transpose(0, 3, 1, 2, 4)

    q, k, v = to_chunks(q), to_chunks(k), to_chunks(v)
    g = g.reshape(b, n, CHUNK, h).transpose(0, 3, 1, 2)
    beta = beta.reshape(b, n, CHUNK, h).transpose(0, 3, 1, 2)
    g = jnp.cumsum(g, axis=-1)
    k_beta = k * beta[..., None]
    v_beta = v * beta[..., None]
    causal = jnp.tril(jnp.ones((CHUNK, CHUNK), dtype=bool))
    strict = jnp.tril(jnp.ones((CHUNK, CHUNK), dtype=bool), -1)
    decay = jnp.exp(jnp.where(causal, g[..., :, None] - g[..., None, :], -jnp.inf))
    a_mat = jnp.where(strict, jnp.einsum("bhnid,bhnjd->bhnij", k_beta, k) * decay, 0.0)
    eye = jnp.eye(CHUNK, dtype=q.dtype)
    t_mat = lax.linalg.triangular_solve(eye + a_mat, jnp.broadcast_to(eye, a_mat.shape),
                                        left_side=True, lower=True)
    w_vals = jnp.einsum("bhnij,bhnjd->bhnid", t_mat, v_beta)
    k_cumdecay = jnp.einsum("bhnij,bhnjd->bhnid", t_mat, k_beta * jnp.exp(g)[..., None])
    attn_intra = jnp.where(causal, jnp.einsum("bhnid,bhnjd->bhnij", q, k) * decay, 0.0)
    g_last = g[..., -1]
    k_decay = k * jnp.exp(g_last[..., None] - g)[..., None]
    q_decay = q * jnp.exp(g)[..., None]
    xs = (jnp.moveaxis(q_decay, 2, 0), jnp.moveaxis(k_cumdecay, 2, 0), jnp.moveaxis(w_vals, 2, 0),
          jnp.moveaxis(attn_intra, 2, 0), jnp.moveaxis(k_decay, 2, 0), jnp.moveaxis(g_last, 2, 0))

    def step(state, inp):
        qd, kcd, wv, attn_c, kd, gl = inp
        v_new = wv - jnp.einsum("bhcd,bhde->bhce", kcd, state)
        o = jnp.einsum("bhcd,bhde->bhce", qd, state) + jnp.einsum("bhij,bhje->bhie", attn_c, v_new)
        state = state * jnp.exp(gl)[..., None, None] + jnp.einsum("bhcd,bhce->bhde", kd, v_new)
        return state, o

    state0 = jnp.zeros((b, h, dk, dv), dtype=q.dtype)
    _, o = lax.scan(step, state0, xs)
    return o.transpose(1, 0, 3, 2, 4).reshape(b, s, h, dv)

def _multiscale_pool(p, w_pool, pool_scale):
    b, s, _ = p.shape
    pf = p.astype(jnp.float32).reshape(b, s, POOL_GROUPS, POOL_GROUP_DIM)
    cs = jnp.cumsum(pf, axis=1)
    pos = jnp.arange(1, s + 1, dtype=jnp.int32)
    outs = []
    for gi, w in enumerate(POOL_WINDOWS):
        c = cs[:, :, gi]
        lower = jnp.pad(c, ((0, 0), (w, 0), (0, 0)))[:, :s]
        count = jnp.minimum(pos, w).astype(jnp.float32)[None, :, None]
        outs.append((c - lower) / count - pf[:, :, gi])
    pooled = jnp.stack(outs, axis=2)
    mixed = jnp.einsum("bsgc,gcd->bsgd", pooled, w_pool.astype(jnp.float32))
    return mixed.reshape(b, s, POOL_WIDTH) * pool_scale.astype(jnp.float32)

def _peer(xn, w_query, sub_keys, expert_down, expert_up):
    b, s, d = xn.shape
    blocks = xn.reshape(-1, PEER_TOKEN_BLOCK, d)
    sk = sub_keys.astype(jnp.float32)

    def block(xb):
        t = xb.shape[0]
        q = (xb @ w_query).astype(jnp.float32).reshape(t, PEER_HEADS, 2, PEER_HALF)
        scores = jnp.einsum("thpc,hpkc->thpk", q, sk)
        s1, i1 = lax.top_k(scores[:, :, 0], PEER_TOPK)
        s2, i2 = lax.top_k(scores[:, :, 1], PEER_TOPK)
        cand = (s1[..., :, None] + s2[..., None, :]).reshape(t, PEER_HEADS, PEER_TOPK * PEER_TOPK)
        cand_idx = (i1[..., :, None] * N_KEYS + i2[..., None, :]).reshape(t, PEER_HEADS, PEER_TOPK * PEER_TOPK)
        top_s, top_pos = lax.top_k(cand, PEER_TOPK)
        idx = jnp.take_along_axis(cand_idx, top_pos, axis=-1)
        gate = jax.nn.softmax(top_s, axis=-1)
        u = expert_down[idx]
        v = expert_up[idx]
        act = jax.nn.gelu(jnp.einsum("td,thkd->thk", xb, u).astype(jnp.float32), approximate=False)
        return jnp.einsum("thk,thkd->td", (gate * act).astype(v.dtype), v)

    return lax.map(block, blocks).reshape(b, s, d).astype(xn.dtype)

def first_inputs(seed: int = 0) -> dict:
    key = jax.random.key(seed)
    ks = jax.random.split(key, 16)
    f32 = jnp.float32
    L = DEPTH

    def gain(k, shape):
        return 1.0 + 0.02 * jax.random.normal(k, shape, f32)

    x = jax.random.normal(ks[0], (BATCH, SEQ, D_MODEL), f32)
    norm_mix_w = gain(ks[1], (L, D_MODEL))
    w_in = jax.random.normal(ks[2], (L, D_MODEL, IN_WIDTH), f32) * D_MODEL ** -0.5
    conv_w = jax.random.normal(ks[3], (L, CONV_WIDTH, 3 * DN_WIDTH), f32) * CONV_WIDTH ** -0.5
    a_log = jnp.log(jax.random.uniform(ks[4], (L, DN_HEADS), f32, 1.0, 16.0))
    dt = jnp.exp(jax.random.uniform(ks[5], (L, DN_HEADS), f32, math.log(1e-3), math.log(1e-1)))
    dt_bias = dt + jnp.log(-jnp.expm1(-dt))
    dn_norm_w = gain(ks[6], (L, DN_HEAD_DIM))
    w_pool = jax.random.normal(ks[7], (L, POOL_GROUPS, POOL_GROUP_DIM, POOL_GROUP_DIM), f32) * POOL_GROUP_DIM ** -0.5
    pool_scale = gain(ks[8], (L, POOL_WIDTH))
    w_out = jax.random.normal(ks[9], (L, MIX_WIDTH, D_MODEL), f32) * MIX_WIDTH ** -0.5
    norm_ffn_w = gain(ks[10], (L, D_MODEL))
    w_query = jax.random.normal(ks[11], (L, D_MODEL, PEER_HEADS * PEER_QUERY_DIM), f32) * D_MODEL ** -0.5
    sub_keys = jax.random.normal(ks[12], (L, PEER_HEADS, 2, N_KEYS, PEER_HALF), f32) * PEER_HALF ** -0.5
    expert_down = jax.random.normal(ks[13], (L, N_EXPERTS, D_MODEL), f32) * D_MODEL ** -0.5
    expert_up = jax.random.normal(ks[14], (L, N_EXPERTS, D_MODEL), f32) * PEER_HEADS ** -0.5
    norm_final_w = gain(ks[15], (D_MODEL,))
    return {"x": x, "norm_mix_w": norm_mix_w, "w_in": w_in, "conv_w": conv_w, "a_log": a_log,
            "dt_bias": dt_bias, "dn_norm_w": dn_norm_w, "w_pool": w_pool, "pool_scale": pool_scale,
            "w_out": w_out, "norm_ffn_w": norm_ffn_w, "w_query": w_query, "sub_keys": sub_keys,
            "expert_down": expert_down, "expert_up": expert_up, "norm_final_w": norm_final_w}

def first_block(x, norm_mix_w, w_in, conv_w, a_log, dt_bias, dn_norm_w, w_pool, pool_scale,
              w_out, norm_ffn_w, w_query, sub_keys, expert_down, expert_up, norm_final_w):
    b, s, _ = x.shape
    for l in range(DEPTH):
        h = _rmsnorm(x, norm_mix_w[l])
        proj = h @ w_in[l]
        qkv = proj[..., :3 * DN_WIDTH]
        z = proj[..., 3 * DN_WIDTH:4 * DN_WIDTH]
        b_gate = proj[..., 4 * DN_WIDTH:4 * DN_WIDTH + DN_HEADS]
        a_dec = proj[..., 4 * DN_WIDTH + DN_HEADS:4 * DN_WIDTH + 2 * DN_HEADS]
        p = proj[..., 4 * DN_WIDTH + 2 * DN_HEADS:]
        qkv = jax.nn.silu(_causal_conv(qkv, conv_w[l])).astype(jnp.float32)
        q = _l2norm(qkv[..., :DN_WIDTH].reshape(b, s, DN_HEADS, DN_HEAD_DIM))
        k = _l2norm(qkv[..., DN_WIDTH:2 * DN_WIDTH].reshape(b, s, DN_HEADS, DN_HEAD_DIM))
        v = qkv[..., 2 * DN_WIDTH:].reshape(b, s, DN_HEADS, DN_HEAD_DIM)
        beta = jax.nn.sigmoid(b_gate.astype(jnp.float32))
        g = -jnp.exp(a_log[l].astype(jnp.float32)) * jax.nn.softplus(
            a_dec.astype(jnp.float32) + dt_bias[l].astype(jnp.float32))
        o = _chunk_gated_delta_rule(q, k, v, g, beta)
        o = _rmsnorm(o, dn_norm_w[l]) * jax.nn.silu(
            z.astype(jnp.float32).reshape(b, s, DN_HEADS, DN_HEAD_DIM))
        o = o.reshape(b, s, DN_WIDTH).astype(x.dtype)
        pool_out = _multiscale_pool(p, w_pool[l], pool_scale[l]).astype(x.dtype)
        x = x + jnp.concatenate([o, pool_out], axis=-1) @ w_out[l]
        x = x + _peer(_rmsnorm(x, norm_ffn_w[l]), w_query[l], sub_keys[l], expert_down[l], expert_up[l])
    return _rmsnorm(x, norm_final_w)


PLE_DIM = 256
MOBA_HEADS = 8
MOBA_HEAD_DIM = D_MODEL // 16
MOBA_WIDTH = MOBA_HEADS * MOBA_HEAD_DIM
MOBA_BLOCK = 256
MOBA_TOPK = 3
MOBA_Q_CHUNK = 64
RET_HEADS = 4
RET_HEAD_DIM = D_MODEL // 8
RET_WIDTH = RET_HEADS * RET_HEAD_DIM
RET_CHUNK = 256
MIX_WIDTH_2 = MOBA_WIDTH + RET_WIDTH
IN_PROJ_WIDTH = 3 * MOBA_WIDTH + 4 * RET_WIDTH
SEQ_PAD_MULTIPLE = 256
D_FF = 2816
CONV_WIDTH_2 = 3
RMS_EPS = 1e-6
GN_EPS = 1e-5


def rmsnorm(x, g):
    xf = x.astype(jnp.float32)
    ms = jnp.mean(xf * xf, axis=-1, keepdims=True)
    return (xf * lax.rsqrt(ms + RMS_EPS)).astype(x.dtype) * g

def alibi_slopes(n_heads):
    return jnp.exp2(-8.0 * jnp.arange(1, n_heads + 1, dtype=jnp.float32) / n_heads)

def to_heads(t, n_heads, head_dim):
    b, s, _ = t.shape
    return t.reshape(b, s, n_heads, head_dim).transpose(0, 2, 1, 3)

def from_heads(t):
    b, h, s, d = t.shape
    return t.transpose(0, 2, 1, 3).reshape(b, s, h * d)

def moba_attention(q, k, v):
    B, H, S, Dh = q.shape
    nb = S // MOBA_BLOCK
    k_eff = min(MOBA_TOPK, nb)
    n_sel = k_eff * MOBA_BLOCK
    scale = Dh ** -0.5
    slopes = alibi_slopes(H)[:, None, None]
    kb = k.reshape(B, H, nb, MOBA_BLOCK, Dh)
    vb = v.reshape(B, H, nb, MOBA_BLOCK, Dh)
    kmean = jnp.mean(kb.astype(jnp.float32), axis=3).astype(k.dtype)
    kb_flat = kb.reshape(B * H * nb, MOBA_BLOCK, Dh)
    vb_flat = vb.reshape(B * H * nb, MOBA_BLOCK, Dh)
    head_base = (jnp.arange(B * H, dtype=jnp.int32) * nb).reshape(B, H, 1, 1)
    chunks_per_block = MOBA_BLOCK // MOBA_Q_CHUNK
    blk_pos = jnp.arange(MOBA_BLOCK, dtype=jnp.int32)
    blk_ids = jnp.arange(nb, dtype=jnp.int32)

    def one_chunk(c):
        start = c * MOBA_Q_CHUNK
        qc = lax.dynamic_slice_in_dim(q, start, MOBA_Q_CHUNK, axis=2)
        own = c // chunks_per_block
        q_pos = start + jnp.arange(MOBA_Q_CHUNK, dtype=jnp.int32)
        gate = jnp.einsum('bhqd,bhnd->bhqn', qc, kmean).astype(jnp.float32)
        gate = jnp.where(blk_ids < own, gate, -jnp.inf)
        gate_val, sel = lax.top_k(gate, k_eff)
        sel_valid = jnp.isfinite(gate_val)
        flat = head_base + sel
        k_sel = kb_flat[flat].reshape(B, H, MOBA_Q_CHUNK, n_sel, Dh)
        v_sel = vb_flat[flat].reshape(B, H, MOBA_Q_CHUNK, n_sel, Dh)
        s_sel = jnp.einsum('bhqd,bhqkd->bhqk', qc, k_sel).astype(jnp.float32) * scale
        key_pos_sel = (sel[..., None] * MOBA_BLOCK + blk_pos).reshape(B, H, MOBA_Q_CHUNK, n_sel)
        dist_sel = (q_pos[:, None] - key_pos_sel).astype(jnp.float32)
        s_sel = jnp.where(jnp.repeat(sel_valid, MOBA_BLOCK, axis=-1),
                          s_sel - slopes * dist_sel, -jnp.inf)
        k_own = lax.dynamic_index_in_dim(kb, own, axis=2, keepdims=False)
        v_own = lax.dynamic_index_in_dim(vb, own, axis=2, keepdims=False)
        s_own = jnp.einsum('bhqd,bhkd->bhqk', qc, k_own).astype(jnp.float32) * scale
        dist_own = q_pos[:, None] - (own * MOBA_BLOCK + blk_pos)[None, :]
        s_own = jnp.where(dist_own >= 0, s_own - slopes * dist_own.astype(jnp.float32), -jnp.inf)
        probs = jax.nn.softmax(jnp.concatenate([s_sel, s_own], axis=-1), axis=-1).astype(v.dtype)
        out = (jnp.einsum('bhqk,bhqkd->bhqd', probs[..., :n_sel], v_sel)
               + jnp.einsum('bhqk,bhkd->bhqd', probs[..., n_sel:], v_own))
        return out

    outs = lax.map(one_chunk, jnp.arange(S // MOBA_Q_CHUNK, dtype=jnp.int32))
    return jnp.moveaxis(outs, 0, 2).reshape(B, H, S, Dh)

def retention_chunkwise(q, k, v):
    B, H, S, Dh = q.shape
    C = RET_CHUNK
    nc = S // C
    gamma = 1.0 - jnp.exp2(-5.0 - jnp.arange(H, dtype=jnp.float32))
    log_g = jnp.log(gamma)
    idx = jnp.arange(C, dtype=jnp.float32)
    diff = idx[:, None] - idx[None, :]
    decay_intra = jnp.where(diff >= 0, jnp.exp(log_g[:, None, None] * jnp.maximum(diff, 0.0)), 0.0)
    q_decay = jnp.exp(log_g[:, None] * (idx + 1.0))[..., None]
    k_decay = jnp.exp(log_g[:, None] * (C - 1.0 - idx))[..., None]
    chunk_decay = jnp.exp(log_g * C)[:, None, None]
    k = k * (Dh ** -0.5)

    def chunks(t):
        return jnp.moveaxis(t.reshape(B, H, nc, C, Dh), 2, 0)

    def step(state, inp):
        qc, kc, vc = inp
        s = jnp.einsum('bhqd,bhkd->bhqk', qc, kc) * decay_intra
        inner = jnp.einsum('bhqk,bhkd->bhqd', s, vc)
        cross = jnp.einsum('bhqd,bhde->bhqe', qc * q_decay, state)
        new_state = chunk_decay * state + jnp.einsum('bhkd,bhke->bhde', kc * k_decay, vc)
        return new_state, inner + cross

    state0 = jnp.zeros((B, H, Dh, Dh), jnp.float32)
    _, outs = lax.scan(step, state0, (chunks(q), chunks(k), chunks(v)))
    return jnp.moveaxis(outs, 0, 2).reshape(B, H, S, Dh)

def head_groupnorm(o, g):
    mu = jnp.mean(o, axis=-1, keepdims=True)
    var = jnp.mean(jnp.square(o - mu), axis=-1, keepdims=True)
    return from_heads((o - mu) * lax.rsqrt(var + GN_EPS)) * g

def causal_dwconv(u, w, b):
    S = u.shape[1]
    up = jnp.pad(u, ((0, 0), (CONV_WIDTH_2 - 1, 0), (0, 0)))
    out = b
    for j in range(CONV_WIDTH_2):
        out = out + w[j] * up[:, j:j + S]
    return out

def second_inputs(seed: int = 0) -> dict:
    key = jax.random.key(seed)
    ks = jax.random.split(key, 17)
    f32 = jnp.float32

    def nrm(k, shape, scale):
        return jax.random.normal(k, shape, f32) * scale

    def gain(k, shape):
        return 1.0 + 0.02 * jax.random.normal(k, shape, f32)

    return {
        "x": nrm(ks[0], (BATCH, SEQ, D_MODEL), 1.0),
        "p": nrm(ks[1], (DEPTH, BATCH, SEQ, PLE_DIM), 1.0),
        "attn_norm": gain(ks[2], (DEPTH, D_MODEL)),
        "w_in": nrm(ks[3], (DEPTH, D_MODEL, IN_PROJ_WIDTH), D_MODEL ** -0.5),
        "ret_norm": gain(ks[4], (DEPTH, RET_WIDTH)),
        "w_out": nrm(ks[5], (DEPTH, MIX_WIDTH_2, D_MODEL), MIX_WIDTH_2 ** -0.5),
        "ffn_norm": gain(ks[6], (DEPTH, D_MODEL)),
        "w_up": nrm(ks[7], (DEPTH, D_MODEL, D_FF), D_MODEL ** -0.5),
        "w_gate": nrm(ks[8], (DEPTH, D_MODEL, D_FF), D_MODEL ** -0.5),
        "conv_w": nrm(ks[9], (DEPTH, CONV_WIDTH_2, D_FF), CONV_WIDTH_2 ** -0.5),
        "conv_b": nrm(ks[10], (DEPTH, D_FF), 0.01),
        "w_down": nrm(ks[11], (DEPTH, D_FF, D_MODEL), D_FF ** -0.5),
        "ple_norm": gain(ks[12], (DEPTH, D_MODEL)),
        "w_ple": nrm(ks[13], (DEPTH, PLE_DIM, D_MODEL), PLE_DIM ** -0.5),
        "w_ple_gate": nrm(ks[14], (DEPTH, D_MODEL, D_MODEL), D_MODEL ** -0.5),
        "final_norm": gain(ks[15], (D_MODEL,)),
    }

def second_block(x, p, attn_norm, w_in, ret_norm, w_out, ffn_norm, w_up, w_gate, conv_w,
              conv_b, w_down, ple_norm, w_ple, w_ple_gate, final_norm):
    B, S, _ = x.shape
    S_pad = -(-S // SEQ_PAD_MULTIPLE) * SEQ_PAD_MULTIPLE
    split_points = [MOBA_WIDTH, 2 * MOBA_WIDTH, 3 * MOBA_WIDTH,
                    3 * MOBA_WIDTH + RET_WIDTH, 3 * MOBA_WIDTH + 2 * RET_WIDTH,
                    3 * MOBA_WIDTH + 3 * RET_WIDTH]
    for i in range(DEPTH):
        h = rmsnorm(x, attn_norm[i])
        proj = h @ w_in[i]
        proj = jnp.pad(proj, ((0, 0), (0, S_pad - S), (0, 0)))
        mq, mk, mv, rq, rk, rv, rg = jnp.split(proj, split_points, axis=-1)
        moba_out = from_heads(moba_attention(to_heads(mq, MOBA_HEADS, MOBA_HEAD_DIM),
                                             to_heads(mk, MOBA_HEADS, MOBA_HEAD_DIM),
                                             to_heads(mv, MOBA_HEADS, MOBA_HEAD_DIM)))
        ret = retention_chunkwise(to_heads(rq, RET_HEADS, RET_HEAD_DIM),
                                  to_heads(rk, RET_HEADS, RET_HEAD_DIM),
                                  to_heads(rv, RET_HEADS, RET_HEAD_DIM))
        ret_out = (head_groupnorm(ret, ret_norm[i]) * jax.nn.silu(rg)).astype(x.dtype)
        mix = jnp.concatenate([moba_out, ret_out], axis=-1)[:, :S]
        x = x + mix @ w_out[i]
        h = rmsnorm(x, ffn_norm[i])
        u = causal_dwconv(h @ w_up[i], conv_w[i], conv_b[i])
        x = x + (jax.nn.gelu(u) * (h @ w_gate[i])) @ w_down[i]
        g = jax.nn.sigmoid(rmsnorm(x, ple_norm[i]) @ w_ple_gate[i])
        x = x + (p[i] @ w_ple[i]) * g
    return rmsnorm(x, final_norm)


def setup_inputs(seed=0):
    out = dict(first_inputs(seed))
    for name, value in second_inputs(seed + 1).items():
        if name != "x":
            out[name + "_2"] = value
    return out


def reference(
    x, norm_mix_w, w_in, conv_w, a_log, dt_bias, dn_norm_w, w_pool, pool_scale, w_out,
    norm_ffn_w, w_query, sub_keys, expert_down, expert_up, norm_final_w, p_2, attn_norm_2,
    w_in_2, ret_norm_2, w_out_2, ffn_norm_2, w_up_2, w_gate_2, conv_w_2, conv_b_2, w_down_2,
    ple_norm_2, w_ple_2, w_ple_gate_2, final_norm_2,
):
    x = first_block(
        x, norm_mix_w, w_in, conv_w, a_log, dt_bias, dn_norm_w, w_pool, pool_scale, w_out,
        norm_ffn_w, w_query, sub_keys, expert_down, expert_up, norm_final_w,
    )
    return second_block(
        x, p_2, attn_norm_2, w_in_2, ret_norm_2, w_out_2, ffn_norm_2, w_up_2, w_gate_2,
        conv_w_2, conv_b_2, w_down_2, ple_norm_2, w_ple_2, w_ple_gate_2, final_norm_2,
    )


_drawn_inputs = setup_inputs


def setup_inputs(seed=0):
    import zlib

    import numpy as np

    out = dict(_drawn_inputs(seed))
    spreads = {}
    factors = {'dn_norm_w': 3.133,
     'attn_norm_2': 3.216,
     'ret_norm_2': 7.194,
     'ffn_norm_2': 11.895,
     'conv_b_2': 31.267,
     'ple_norm_2': 200.0,
     'final_norm_2': 23.887,
     'p_2': 8.0,
     'w_ple_2': 8.0,
     'w_ple_gate_2': 8.0}
    for name, (base, spread) in spreads.items():
        noise = np.random.default_rng([zlib.crc32(name.encode()), seed]).standard_normal(out[name].shape)
        drawn = base * np.exp(spread * noise) if base else spread * noise
        out[name] = __import__('jax').numpy.asarray(drawn.astype(out[name].dtype))
    for name, factor in factors.items():
        out[name] = (out[name] * factor).astype(out[name].dtype)
    return out
```

```python
import concourse.bass as bass
from concourse import mybir
from contextlib import ExitStack
import numpy as np

F32 = mybir.dt.float32
F32R = mybir.dt.float32r
U32 = mybir.dt.uint32
ALU = mybir.AluOpType
ACT = mybir.ActivationFunctionType
AX = mybir.AxisListType

P = 128
T = 256
TB = T // P
D = 1024
KT = D // P
TW = KT * P
DH = 4
NI = TB * DH
PG = 4
NH = 8
TOPK = 16
NEG = -3.0e38
EPS = 1e-6
MH, MD = 8, 64
RH = 4
FF = 2816 // P
PAD = 16

W_PROJ1 = 0
N_PROJ1 = 20
W_OUT1 = W_PROJ1 + N_PROJ1
W_QUERY = W_OUT1 + KT
N_QUERY = 2 * NH
W_EXP = W_QUERY + N_QUERY
N_EXP = P
W_PROJ2 = W_EXP + 2 * N_EXP
N_PROJ2 = 20
W_V2 = W_PROJ2 + N_PROJ2
W_OUT2 = W_V2 + KT
W_FF = W_OUT2 + KT
W_PLEG = W_FF + 3 * FF
W_PLE = W_PLEG + KT
N_TILES = W_PLE + 2
RING = 4
LEAD = 3
assert N_TILES % 4 == 0

CV = {}
_c = 0
for _n, _w in (("norm_mix", KT), ("conv", 48), ("dn_norm", 1), ("pool_scale", PG), ("norm_ffn", KT), ("norm_mid", KT),
               ("attn_norm", KT), ("ret_norm", RH), ("ffn_norm", KT), ("conv2", 3 * FF), ("conv2_b", FF),
               ("ple_norm", KT), ("final_norm", KT)):
    CV[_n] = _c
    _c += _w
N_CV = _c

SEMS = """x_in vec_in c1_in gate_w_in row_in wpool_in keys_in c2_in ple_in out_done dve act pe pool
w_hi w_lo w_used raw0 raw1 x_sq ssq norm_ms norm_sqrt norm_h src_hi operand
evac conv_raw conv_done silu_done z_done p_done
qk_sq qk_ss qk_ms qk_sqrt qk_norm ba gate_in gate_sig gate_e gate_l gate_ea g_ready gb gsub gexp
kk qkt kvt kv_ready An_ready AnT AnT_sb T0 amt U U_sb Tp inverse w_ps w_sb kcd_ps kcd_sb s1_ps s1_sb vn_ps vn_sb o_ps
o_sq o_ss o_ms o_sqrt mix_dn pooled pool_ps mix_pool
q_ps q_sb sc_ps scores seeded cv_ready cv_exp topk idxT idxT_sb onehot g_ps g_sb
gelu p_mul p_hi p_split x2 s_ps s_max s_exp s_norm pt_ps pt_sb ao_ps ao_sb v_ps v_sb
rs_ps rs_sb ro_ps ro_sb rmu rxc r_sq r_ss r_ms r_sqrt mix_ret evac2 rg_done
ff_conv ff_gelu ff_mul ff_hi ff_split ff_done ff_seed x4 ple_gate ple_hi ple_op ple_ps ple_add""".split()


def program(nc, x_t, vecs, wts, c1, gate_w, rows, w_pool, keys, c2, ple_t, out):
    ctx = ExitStack()
    with ctx:
        s = {n: ctx.enter_context(nc.semaphore("s_" + n)) for n in SEMS}

        top = [-(-nc.sbuf_base // 32) * 32]
        slab = ctx.enter_context(nc.sbuf_tensor("slab", [P, (nc.sbuf_bytes_remaining - 64) // 4], F32))

        def place(name, shape, dt=F32, at=None):
            size = int(np.prod(shape)) * 4
            size = -(-size // 32) * 32
            if at is None:
                at, top[0] = top[0], top[0] + size
            else:
                at[0], at = at[0] + size, at[0]
            return nc.alloc_sbuf_tensor_at(name, [P] + list(shape), dt, offset=at)

        raw = place("raw", [2, 2 * TW])
        whi = place("whi", [RING, TW], F32R)
        wlo = place("wlo", [RING, TW], F32R)
        ahi = place("ahi", [KT, T], F32R)
        alo = place("alo", [KT, T], F32R)
        ident = place("ident", [P])
        ones = place("ones", [P])
        vec = place("vec", [N_CV])
        small = top[0]
        x = place("x", [KT, T])
        pf = place("pf", [2, T])
        phi = place("phi", [2, T], F32R)
        plo = place("plo", [2, T], F32R)
        aux = [small]
        iT = place("iT", [3, T], at=aux)
        iota = place("iota", [P], at=aux)
        oh1 = place("oh1", [2, 4, P], at=aux)
        oh2 = place("oh2", [2, 4, P], at=aux)
        assert aux[0] <= top[0]
        arena = top[0]
        G = place("G", [N_EXP, T])
        end = top[0]
        assert end <= nc.sbuf_usable_end, end

        a = [arena]
        h32 = place("h32", [KT, T], at=a)
        sq = place("sq", [KT, T], at=a)
        rstd = place("rstd", [T], at=a)
        rtmp = place("rtmp", [T], at=a)
        common = a[0]
        cst = place("cst", [10 * P + PG * T], at=a)
        U1 = cst[:, 0:P]
        SL = cst[:, P:2 * P]
        LM0 = cst[:, 2 * P:3 * P]
        LMT = [cst[:, (3 + l) * P:(4 + l) * P] for l in range(7)]
        invc = cst[:, 10 * P:10 * P + PG * T].rearrange("p (g t) -> p g t", g=PG)
        gw = place("gw", [KT, 8], at=a)
        row = place("row", [8], at=a)
        wp = place("wp", [PG, P], at=a)
        keep = a[0]
        qraw = place("qraw", [12, T + 3], at=a)
        b = [keep]
        rn = place("rn", [8, T], at=b)
        qkv = place("qkv", [12, T], at=a)
        zs = place("zs", [DH, T], at=a)
        pp = place("pp", [PG, PAD + T], at=a)
        pa = place("pa", [PG, PAD + T], at=a)
        pb = place("pb", [PG, PAD + T], at=a)
        I8 = [NI, P]
        gbc = place("gbc", I8, at=a)
        AmT = gbc
        Dm = place("Dm", I8, at=a)
        Tm = Dm
        DT = place("DT", I8, at=a)
        X = place("X", I8, at=a)
        Us = X
        attnT = DT
        An = place("An", I8, at=a)
        AnT = place("AnT", I8, at=a)
        TT = place("TT", I8, at=a)
        eGb = place("eGb", [DH, P], at=a)
        kbg = place("kbg", [DH, P], at=a)
        kdec = place("kdec", [DH, P], at=a)
        vb = place("vb", I8, at=a)
        Wv = place("Wv", I8, at=a)
        kcdT = place("kcdT", [DH, P], at=a)
        S1 = place("S1", [DH, P], at=a)
        qd = kcdT_q = place("qd", [DH, P], at=a)
        tok = place("tok", [160], at=a)
        assert a[0] <= end, a[0] - end
        col = {}
        c = 0
        for n, w in (("ba", 16), ("beta", 8), ("nbeta", 8), ("t1", 8), ("t2", 8), ("e", 8), ("l", 8), ("ea", 4),
                     ("g", 8), ("gc", 8), ("egc", 4), ("bg", 4), ("kd", 4)):
            col[n] = tok[:, c:c + w]
            c += w
        a = [common]
        qs = place("qs", [4, T], at=a)
        kk = place("kk", [2 * NH, P], at=a)
        sc = place("sc", [TB, 2 * NH, P], at=a)
        v16 = place("v16", [TB, 2 * NH, TOPK], at=a)
        i16 = place("i16", [TB, 2 * NH, TOPK], U32, at=a)
        i16f = place("i16f", [TB, 2 * NH, TOPK], at=a)
        cand = place("cand", [TB * NH, TOPK * TOPK], at=a)
        cv = place("cv", [TB * NH, TOPK], at=a)
        ci = place("ci", [TB * NH, TOPK], U32, at=a)
        cj = place("cj", [2, TB * NH * TOPK], U32, at=a)
        cf = place("cf", [2, TB * NH * TOPK], at=a)
        gates = place("gates", [3, TB, P], at=a)
        gsum = place("gsum", [2, TB * NH], at=a)
        iota16 = place("iota16", [P], at=a)
        eq = place("eq", [TB * NH, TOPK, TOPK], at=a)
        assert a[0] <= end
        a = [common]
        qk2 = place("qk2", [16, T], at=a)
        rgs = place("rgs", [RH, T], at=a)
        vv = place("vv", [TB, D], at=a)
        cs2 = place("cs2", [RH * 3 * P + 3 * P], at=a)
        rdec = cs2[:, 0:RH * 3 * P].rearrange("p (r n) -> p r n", r=RH)
        dist = cs2[:, RH * 3 * P:]
        sS = place("sS", [2, 3 * P], at=a)
        pr = place("pr", [2, 3 * P], at=a)
        pT = place("pT", [2, 3 * P], at=a)
        mx = place("mx", [MH, 4], at=a)
        sums = place("sums", [MH, 4], at=a)
        rS = place("rS", [RH, 3 * P], at=a)
        ro = place("ro", [RH, T], at=a)
        rr = place("rr", [RH, T], at=a)
        mix2 = place("mix2", [KT, T], at=a)
        fu = place("fu", [2, T], at=a)
        fg = place("fg", [2, T], at=a)
        gs = place("gs", [KT, T], at=a)
        pt = place("pt", [2, T], at=a)
        pthi = place("pthi", [2, T], F32R, at=a)
        ptlo = place("ptlo", [2, T], F32R, at=a)
        assert a[0] <= end

        ps = ctx.enter_context(nc.psum_tensor("ps", [P, 8, 512], F32))
        flat = ps[:, :, :].rearrange("p b n -> p (b n)")

        def bank(b0, n, shape=None, base=0):
            v = flat[:, b0 * 512 + base:b0 * 512 + base + n]
            return v

        def vcol(name, j=0):
            return vec[:, CV[name] + j:CV[name] + j + 1]

        def b3(ap, n):
            return ap.unsqueeze(2).to_broadcast([P, ap.shape[1], n])

        def m3(ap, n):
            return ap.unsqueeze(1).to_broadcast([P, n, ap.shape[1]])

        block = ctx.enter_context(nc.Block())

        def raw_tile(half, k):
            return raw[:, half, k * TW:(k + 1) * TW]

        @block.sync
        def _(sp):
            sp.dma_start(x[:, :, :], x_t).then_inc(s["x_in"], 16)
            sp.dma_start(vec[:, :], vecs).then_inc(s["vec_in"], 16)
            rs = (s["raw0"], s["raw1"])
            for p in range(2):
                sp.dma_start(raw[:, p, :], wts[p]).then_inc(rs[p], 16)
            with sp.Fori(1, N_TILES // 4) as i:
                for p in range(2):
                    sp.wait_ge(s["w_hi"], i * 4 + (2 * p - 2))
                    sp.wait_ge(s["w_lo"], i * 4 + (2 * p - 2))
                    sp.dma_start(raw[:, p, :], wts[bass.ds(i * 2 + p, 1), :, :].rearrange("a p n -> p (a n)"))\
                      .then_inc(rs[p], 16)
            sp.wait_ge(s["norm_h"], 7)
            sp.dma_start(out, h32[:, :, :]).then_inc(s["out_done"], 16)
            sp.wait_ge(s["out_done"], 16)

        @block.gpsimd
        def _(pl):
            pl.dma_start(gw[:, :, :], gate_w).then_inc(s["gate_w_in"], 16)
            pl.dma_start(row[:, :], rows.partition_broadcast(P)).then_inc(s["row_in"], 16)
            pl.dma_start(ident[:, :], c1[:, 10 * P + PG * T:11 * P + PG * T]).then_inc(s["c1_in"], 16)
            pl.dma_start(cst[:, :], c1[:, 0:10 * P + PG * T]).then_inc(s["c1_in"], 16)
            pl.dma_start(wp[:, :, :], w_pool).then_inc(s["wpool_in"], 16)
            pl.wait_ge(s["operand"], 2)
            pl.dma_start(kk[:, :, :], keys).then_inc(s["keys_in"], 16)
            pl.dma_start(iota16[:, :], c1[:, 11 * P + PG * T:12 * P + PG * T]).then_inc(s["keys_in"], 16)
            pl.wait_ge(s["seeded"], 1)
            pl.wait_ge(s["operand"], 3)
            pl.dma_start(iota[:, :], c1[:, 11 * P + PG * T:12 * P + PG * T]).then_inc(s["keys_in"], 16)
            pl.wait_ge(s["p_mul"], N_EXP)
            pl.dma_start(cs2[:, :], c2).then_inc(s["c2_in"], 16)
            pl.dma_start(pt[:, :, :], ple_t).then_inc(s["ple_in"], 16)

        def split_hi(act, u, j, quad=None):
            if quad is None:
                if u >= N_TILES:
                    return
                act.wait_ge((s["raw0"], s["raw1"])[j // 2], 16 * (u // 4 + 1))
                if u >= RING:
                    act.wait_ge(s["w_used"], u - RING + 1)
            else:
                act.wait_ge((s["raw0"], s["raw1"])[j // 2], quad * 16 + 16)
                act.wait_ge(s["w_used"], quad * 4 + (j - RING + 1))
            nc.scalar.activation(whi[:, j, :], raw_tile(j // 2, j % 2), ACT.Copy).then_inc(s["w_hi"], 1)

        def split_lo(dve, u, j, quad=None):
            if quad is None:
                if u >= N_TILES:
                    return
                dve.wait_ge(s["w_hi"], u + 1)
                if u >= RING:
                    dve.wait_ge(s["w_used"], u - RING + 1)
            else:
                dve.wait_ge(s["w_hi"], quad * 4 + (j + 1))
                dve.wait_ge(s["w_used"], quad * 4 + (j - RING + 1))
            nc.vector.tensor_tensor(wlo[:, j, :], raw_tile(j // 2, j % 2), whi[:, j, :].bitcast(F32),
                                    ALU.subtract).then_inc(s["w_lo"], 1)

        def products(out_ap, wh, wl, xh, xl, first, last):
            nc.tensor.matmul(out_ap, wh, xh, start=first, stop=False, skip_group_check=True)
            nc.tensor.matmul(out_ap, wh, xl, start=False, stop=False, skip_group_check=True)
            return nc.tensor.matmul(out_ap, wl, xh, start=False, stop=last, skip_group_check=True)

        def w_k(j, k):
            return whi[:, j, k * P:(k + 1) * P], wlo[:, j, k * P:(k + 1) * P]

        def gemm_tile(pe, j, dst):
            for k in range(KT):
                m = products(dst, *w_k(j, k), ahi[:, k, :], alo[:, k, :], k == 0, k == KT - 1)
            m.then_inc(s["w_used"], 1)

        class Chain:

            def __init__(self, eng, sem):
                self.eng, self.sem, self.n = eng, sem, 0

            def __call__(self, ins):
                ins.then_inc(self.sem, 1)
                self.n += 1
                self.eng.wait_ge(self.sem, self.n)

        X_READY = [(s["x_in"], 16), (s["evac"], W_QUERY), (s["x2"], 1), (s["norm_h"], 3), (s["evac2"], N_PROJ2 + KT), (s["x4"], 1), (s["ple_add"], KT)]
        NORM_W = ["norm_mix", "norm_ffn", "norm_mid", "attn_norm", "ffn_norm", "ple_norm", "final_norm"]
        NORM_OP = [0, 2, None, 3, 5, 6, None]
        USED_BEFORE = [0, W_OUT1, W_QUERY, W_PROJ2, W_OUT2, W_FF, W_PLEG]

        def norm_act(act, i):
            act.wait_ge(*X_READY[i])
            if i == 4:
                act.wait_ge(s["mix_ret"], 1)
            nc.scalar.activation(sq[:, :, :], x[:, :, :], ACT.Square).then_inc(s["x_sq"], 1)
            act.wait_ge(s["norm_ms"], i + 1)
            nc.scalar.activation(rstd[:, :], rtmp[:, :], ACT.Sqrt).then_inc(s["norm_sqrt"], 1)
            if NORM_OP[i] is not None:
                operand_act(act, NORM_OP[i], h32)

        def norm_pe(pe, i):
            pe.wait_ge(s["x_sq"], i + 1)
            if i == 0:
                pe.wait_ge(s["pool"], 1)
            for k in range(KT):
                m = nc.tensor.matmul(bank(2, T), ones[:, :], sq[:, k, :], start=k == 0, stop=k == KT - 1)
            m.then_inc(s["ssq"], 1)

        def norm_dve(dve, ch, i):
            if i == 0:
                dve.wait_ge(s["x_in"], 16)
                dve.wait_ge(s["vec_in"], 16)
            dve.wait_ge(s["ssq"], i + 1)
            nc.vector.tensor_scalar(rtmp[:, :], bank(2, T), 1.0 / D, EPS, ALU.mult, ALU.add).then_inc(s["norm_ms"], 1)
            dve.wait_ge(s["norm_sqrt"], i + 1)
            ch(nc.vector.reciprocal(rtmp[:, :], rstd[:, :]))
            for k in range(KT):
                m = nc.vector.scalar_tensor_tensor((x if i == 2 else h32)[:, k, :], x[:, k, :], vcol(NORM_W[i], k), rtmp[:, :],
                                                   ALU.mult, ALU.mult)
            m.then_inc(s["norm_h"], 1)
            dve.wait_ge(s["norm_h"], i + 1)
            if NORM_OP[i] is not None:
                operand_dve(dve, NORM_OP[i], h32)

        def operand_act(act, n, src):
            if n in NORM_OP:
                act.wait_ge(s["norm_h"], NORM_OP.index(n) + 1)
            if n:
                act.wait_ge(s["w_used"], USED_BEFORE[n])
            nc.scalar.activation(ahi[:, :, :], src[:, :, :], ACT.Copy).then_inc(s["src_hi"], 1)

        def operand_dve(dve, n, src):
            dve.wait_ge(s["src_hi"], n + 1)
            nc.vector.tensor_tensor(alo[:, :, :], src[:, :, :], ahi[:, :, :].bitcast(F32), ALU.subtract)\
              .then_inc(s["operand"], 1)

        i4 = lambda b0, n=NI: bank(b0, n * P).rearrange("p (i n) -> p i n", n=P)

        @block.tensor
        def _(pe):
            tm = nc.tensor.matmul
            norm_pe(pe, 0)

            pe.wait_ge(s["operand"], 1)
            for u in range(2):
                pe.wait_ge(s["w_lo"], u + 1)
                gemm_tile(pe, u % RING, bank(u % 2, T))
            for u in range(2, 4):
                pe.wait_ge(s["w_lo"], u + 1)
                pe.wait_ge(s["evac"], u - 1)
                gemm_tile(pe, u % RING, bank(u % 2, T))
            with pe.Fori(1, N_PROJ1 // 4) as i:
                for j in range(4):
                    pe.wait_ge(s["w_lo"], i * 4 + (j + 1))
                    pe.wait_ge(s["evac"], i * 4 + (j - 1))
                    gemm_tile(pe, j, bank(j % 2, T))
            pe.wait_ge(s["gate_w_in"], 16)
            pe.wait_ge(s["norm_h"], 1)
            for n in range(TB):
                for k in range(KT):
                    m = tm(bank(3, 8, base=8 * n), h32[:, k, n * P:(n + 1) * P], gw[:, k, :],
                           start=k == 0, stop=k == KT - 1)
            m.then_inc(s["ba"], 1)
            pe.wait_ge(s["qk_sq"], 1)
            for b0 in range(4):
                m = tm(bank(4 + b0, 512), ones[:, :], sq[:, 2 * b0:2 * b0 + 2, :], start=True, stop=True)
            m.then_inc(s["qk_ss"], 1)
            pe.wait_ge(s["c1_in"], 32)
            pe.wait_ge(s["g_ready"], 1)
            for n in range(TB):
                tm(bank(3, DH, base=16 + DH * n), U1, col["g"][:, n * DH:(n + 1) * DH], start=True, stop=True)
            pe.wait_ge(s["evac"], N_PROJ1)
            for i in range(NI):
                m = tm(i4(0)[:, i, :], gbc[:, i, :], U1, start=True, stop=True)
            m.then_inc(s["gb"], 1)
            pe.wait_ge(s["qk_norm"], 1)
            for n in range(TB):
                for h in range(DH):
                    kc = qkv[:, DH + h, n * P:(n + 1) * P]
                    m = tm(i4(4)[:, n * DH + h, :], kc, kc, start=True, stop=True)
            m.then_inc(s["kk"], 1)
            for n in range(TB):
                for h in range(DH):
                    m = tm(i4(6)[:, n * DH + h, :], qkv[:, DH + h, n * P:(n + 1) * P],
                           qkv[:, h, n * P:(n + 1) * P], start=True, stop=True)
            m.then_inc(s["qkt"], 1)
            pe.wait_ge(s["gexp"], 1)
            for n in range(TB):
                for h in range(DH):
                    m = nc.tensor.transpose(i4(0)[:, n * DH + h, :], qkv[:, DH + h, n * P:(n + 1) * P], ident[:, :])
            m.then_inc(s["kvt"], 1)
            pe.wait_ge(s["norm_ms"], 1)
            pe.wait_ge(s["gate_l"], 1)
            pe.wait_ge(s["gsub"], 1)
            for n in range(TB):
                for h in range(DH):
                    m = nc.tensor.transpose(i4(2)[:, n * DH + h, :], qkv[:, 2 * DH + h, n * P:(n + 1) * P],
                                            ident[:, :])
            m.then_inc(s["kvt"], 1)
            pe.wait_ge(s["An_ready"], 1)
            for i in range(NI):
                m = nc.tensor.transpose(i4(4)[:, i, :], An[:, i, :], ident[:, :])
            m.then_inc(s["AnT"], 1)
            pe.wait_ge(s["kv_ready"], 1)
            for l in range(1, 7):
                pe.wait_ge(s["amt"], l)
                for i in range(NI):
                    m = tm(i4(0)[:, i, :], AmT[:, i, :], Tm[:, i, :], start=True, stop=True)
                m.then_inc(s["U"], 1)
                pe.wait_ge(s["U_sb"], l)
                for i in range(NI):
                    m = tm(i4(2)[:, i, :], Us[:, i, :], TT[:, i, :], start=True, stop=True)
                if l < 6:
                    for i in range(NI):
                        m = tm(i4(4)[:, i, :], TT[:, i, :], Us[:, i, :], start=True, stop=True)
                m.then_inc(s["Tp"], 1)
            pe.wait_ge(s["inverse"], 1)
            for i in range(NI):
                m = tm(i4(0)[:, i, :], TT[:, i, :], vb[:, i, :], start=True, stop=True)
            m.then_inc(s["w_ps"], 1)
            for h in range(DH):
                m = tm(i4(2)[:, h, :], kbg[:, h, :], TT[:, DH + h, :], start=True, stop=True)
            m.then_inc(s["kcd_ps"], 1)
            pe.wait_ge(s["w_sb"], 1)
            for h in range(DH):
                m = tm(i4(3)[:, h, :], kdec[:, h, :], Wv[:, h, :], start=True, stop=True)
            m.then_inc(s["s1_ps"], 1)
            pe.wait_ge(s["kcd_sb"], 1)
            pe.wait_ge(s["s1_sb"], 1)
            for h in range(DH):
                m = tm(i4(4)[:, h, :], kcdT[:, h, :], S1[:, h, :], start=True, stop=True)
            m.then_inc(s["vn_ps"], 1)
            pe.wait_ge(s["vn_sb"], 1)
            for h in range(DH):
                o = bank(6, T, base=h * T)
                tm(o[:, 0:P], Wv[:, h, :], attnT[:, h, :], start=True, stop=True)
                tm(o[:, P:T], S1[:, h, :], qd[:, h, :], start=True, stop=False)
                m = tm(o[:, P:T], Wv[:, DH + h, :], attnT[:, DH + h, :], start=False, stop=True)
            m.then_inc(s["o_ps"], 1)
            pe.wait_ge(s["o_sq"], 1)
            for b0 in range(2):
                m = tm(bank(4 + b0, 512), ones[:, :], sq[:, 2 * b0:2 * b0 + 2, :], start=True, stop=True)
            m.then_inc(s["o_ss"], 1)
            pe.wait_ge(s["wpool_in"], 16)
            pe.wait_ge(s["pooled"], 1)
            for g in range(PG):
                m = tm(bank(2, T, base=g * T), wp[:, g, :], pa[:, g, PAD:], start=True, stop=True)
            m.then_inc(s["pool_ps"], 1)

            pe.wait_ge(s["operand"], 2)
            def plain_stage(first, n, sem, base):
                assert first % 4 == 0
                for j in range(4):
                    pe.wait_ge(s["w_lo"], first + j + 1)
                    if base + j >= 2:
                        pe.wait_ge(sem, base + j - 1)
                    gemm_tile(pe, j, bank(j % 2, T))
                if n > 4:
                    with pe.Fori(1, n // 4) as i:
                        for j in range(4):
                            pe.wait_ge(s["w_lo"], i * 4 + (first + j + 1))
                            pe.wait_ge(sem, i * 4 + (base + j - 1))
                            gemm_tile(pe, j, bank(j % 2, T))
            plain_stage(W_OUT1, KT, s["evac"], N_PROJ1)
            norm_pe(pe, 1)

            pe.wait_ge(s["operand"], 3)
            pe.wait_ge(s["keys_in"], 32)

            def scores(m_idx, slot, key):
                for tb in range(TB):
                    m = tm(bank(2 + slot % 2, P, base=tb * P), qs[:, slot, tb * P:(tb + 1) * P], key,
                           start=True, stop=True)
                m.then_inc(s["sc_ps"], 1)

            for j in range(4):
                pe.wait_ge(s["w_lo"], W_QUERY + j + 1)
                pe.wait_ge(s["evac"], W_QUERY + j - 1)
                gemm_tile(pe, j, bank(j % 2, T))
                if j >= 1:
                    pe.wait_ge(s["evac"], W_QUERY + j)
                    if j >= 3:
                        pe.wait_ge(s["scores"], j - 2)
                    scores(j - 1, j - 1, kk[:, j - 1, :])
            with pe.Fori(1, N_QUERY // 4) as i:
                for j in range(4):
                    pe.wait_ge(s["w_lo"], i * 4 + (W_QUERY + j + 1))
                    pe.wait_ge(s["evac"], i * 4 + (W_QUERY + j - 1))
                    gemm_tile(pe, j, bank(j % 2, T))
                    pe.wait_ge(s["evac"], i * 4 + (W_QUERY + j))
                    pe.wait_ge(s["scores"], i * 4 + (j - 2))
                    scores(None, (j - 1) % 4, kk[:, bass.ds(i * 4 + (j - 1), 1), :].rearrange("p a n -> p (a n)"))
            pe.wait_ge(s["evac"], W_EXP)
            pe.wait_ge(s["scores"], N_QUERY - 2)
            scores(None, 3, kk[:, N_QUERY - 1, :])

            for b0 in range(4):
                m = tm(bank(4 + b0, 512), ident[:, :], x[:, 2 * b0:2 * b0 + 2, :],
                       start=True, stop=False, skip_group_check=True)
            m.then_inc(s["seeded"], 1)

            pe.wait_ge(s["topk"], 1)
            pe.wait_ge(s["scores"], N_QUERY)
            for q in range(3):
                for tb in range(TB):
                    m = nc.tensor.transpose(bank(2, P, base=q * T + tb * P), gates[:, q, tb, :], ident[:, :])
            m.then_inc(s["idxT"], 1)
            pe.wait_ge(s["idxT_sb"], 1)

            def gate_group(j):
                for t in range(4):
                    m = tm(bank(2 + j, P, base=t * P), oh2[:, j, t, :], oh1[:, j, t, :], start=True, stop=True)
                m.then_inc(s["g_ps"], 1)

            for j in range(2):
                pe.wait_ge(s["onehot"], j + 1)
                gate_group(j)
            with pe.Fori(1, T // 8) as i:
                for j in range(2):
                    pe.wait_ge(s["onehot"], i * 2 + (j + 1))
                    pe.wait_ge(s["g_sb"], i * 2 + (j - 1))
                    gate_group(j)

            def expert_out(j, r, last=False):
                for k in range(KT):
                    m = products(bank(4, T, base=k * T), *w_k(j, k), phi[:, r, :], plo[:, r, :], False, last)
                m.then_inc(s["w_used"], 1)

            pe.wait_ge(s["w_lo"], W_EXP + 1)
            gemm_tile(pe, 0, bank(0, T))
            pe.wait_ge(s["w_lo"], W_EXP + 2)
            gemm_tile(pe, 1, bank(1, T))
            pe.wait_ge(s["w_lo"], W_EXP + 3)
            pe.wait_ge(s["p_split"], 1)
            expert_out(2, 0)
            with pe.Fori(1, N_EXP // 2) as i:
                for v in range(2):
                    pe.wait_ge(s["w_lo"], i * 4 + (W_EXP + 2 * v))
                    pe.wait_ge(s["gelu"], i * 2 + (v - 1))
                    gemm_tile(pe, (2 * v - 1) % 4, bank(v, T))
                    pe.wait_ge(s["w_lo"], i * 4 + (W_EXP + 2 * v + 1))
                    pe.wait_ge(s["p_split"], i * 2 + v)
                    expert_out(2 * v, 1 - v)
            pe.wait_ge(s["w_lo"], W_PROJ2)
            pe.wait_ge(s["p_split"], N_EXP)
            expert_out(3, 1, last=True)
            norm_pe(pe, 2)
            norm_pe(pe, 3)

            pe.wait_ge(s["operand"], 4)
            plain_stage(W_PROJ2, N_PROJ2, s["evac2"], 0)
            for k in range(KT):
                u = W_V2 + k
                pe.wait_ge(s["w_lo"], u + 1)
                j = u % 4
                for tb in range(TB):
                    for half in range(2):
                        m = products(bank(4 + 2 * tb + half, 512), ahi[:, k, tb * P:(tb + 1) * P],
                                     alo[:, k, tb * P:(tb + 1) * P], whi[:, j, half * 512:(half + 1) * 512],
                                     wlo[:, j, half * 512:(half + 1) * 512], k == 0, k == KT - 1)
                m.then_inc(s["w_used"], 1)

            pe.wait_ge(s["evac2"], N_PROJ2)

            def att_scores(h):
                r0, jt = MD * (h % 2), h // 2
                rows_ = slice(r0, r0 + MD)
                if h >= 2:
                    pe.wait_ge(s["s_max"], h - 1)
                tm(bank(h % 2, P), qk2[rows_, jt, 0:P], qk2[rows_, 4 + jt, 0:P], start=True, stop=True)
                tm(bank(h % 2, T, base=P), qk2[rows_, jt, P:T], qk2[rows_, 4 + jt, 0:T], start=True, stop=True)\
                    .then_inc(s["s_ps"], 1)

            def att_transposed(h):
                pe.wait_ge(s["s_norm"], h + 1)
                if h >= 2:
                    pe.wait_ge(s["pt_sb"], h - 1)
                for q in range(3):
                    m = nc.tensor.transpose(bank(2 + h % 2, P, base=q * P), pr[:, h % 2, q * P:(q + 1) * P],
                                            ident[:, :])
                m.then_inc(s["pt_ps"], 1)

            def att_out(h):
                r0, jt = MD * (h % 2), h // 2
                pe.wait_ge(s["pt_sb"], h + 1)
                if h == 0:
                    pe.wait_ge(s["v_sb"], 1)
                if h >= 2:
                    pe.wait_ge(s["ao_sb"], h - 1)
                o = bank(4 + h % 2, T)[r0:r0 + MD, :]
                vh = lambda tb: vv[:, tb, h * MD:(h + 1) * MD]
                tm(o[:, 0:P], vh(0), pT[:, h % 2, 0:P], start=True, stop=True)
                tm(o[:, P:T], vh(0), pT[:, h % 2, P:2 * P], start=True, stop=False)
                tm(o[:, P:T], vh(1), pT[:, h % 2, 2 * P:3 * P], start=False, stop=True).then_inc(s["ao_ps"], 1)

            att_scores(0)
            for h in range(MH):
                if h + 1 < MH:
                    att_scores(h + 1)
                att_transposed(h)
                if h:
                    att_out(h - 1)
            att_out(MH - 1)

            pe.wait_ge(s["s_max"], MH)
            for r in range(RH):
                if r >= 2:
                    pe.wait_ge(s["rs_sb"], r - 1)
                tm(bank(r % 2, T), qk2[:, 12 + r, 0:P], qk2[:, 8 + r, 0:T], start=True, stop=True)
                tm(bank(r % 2, P, base=T), qk2[:, 12 + r, P:T], qk2[:, 8 + r, P:T], start=True, stop=True)\
                    .then_inc(s["rs_ps"], 1)
            for r in range(RH):
                pe.wait_ge(s["rs_sb"], r + 1)
                o = bank(6, T, base=r * T)
                vr = lambda tb: vv[:, tb, 512 + r * P:512 + (r + 1) * P]
                tm(o[:, 0:P], vr(0), rS[:, r, 0:P], start=True, stop=True)
                tm(o[:, P:T], vr(0), rS[:, r, P:T], start=True, stop=False)
                m = tm(o[:, P:T], vr(1), rS[:, r, T:T + P], start=False, stop=True)
            m.then_inc(s["ro_ps"], 1)
            pe.wait_ge(s["ro_sb"], 1)
            pe.wait_ge(s["pt_sb"], MH)
            for b0 in range(2):
                m = tm(bank(2 + b0, 512), ones[:, :], ro[:, 2 * b0:2 * b0 + 2, :], start=True, stop=True)
            m.then_inc(s["rmu"], 1)
            pe.wait_ge(s["r_sq"], 1)
            pe.wait_ge(s["ao_sb"], MH)
            for b0 in range(2):
                m = tm(bank(4 + b0, 512), ones[:, :], sq[:, 2 * b0:2 * b0 + 2, :], start=True, stop=True)
            m.then_inc(s["r_ss"], 1)

            pe.wait_ge(s["operand"], 5)
            plain_stage(W_OUT2, KT, s["evac2"], N_PROJ2)
            norm_pe(pe, 4)

            pe.wait_ge(s["operand"], 6)
            for b0 in range(4):
                tm(bank(4 + b0, 512), ident[:, :], x[:, 2 * b0:2 * b0 + 2, :],
                   start=True, stop=False, skip_group_check=True)
            for f in range(FF):
                u = W_FF + (3 * f - 1 if f else 0)
                v = f % 2
                for n in range(2):
                    pe.wait_ge(s["w_lo"], u + n + 1)
                    if f >= 2 and n == 0:
                        pe.wait_ge(s["ff_conv"], f - 1)
                    if f >= 2 and n == 1:
                        pe.wait_ge(s["ff_mul"], f - 1)
                    gemm_tile(pe, (u + n) % 4, bank(2 * n + v, T))
                if f:
                    pe.wait_ge(s["w_lo"], u + 3)
                    pe.wait_ge(s["ff_split"], f)
                    expert_out((u + 2) % 4, (f - 1) % 2)
            pe.wait_ge(s["w_lo"], W_PLEG)
            pe.wait_ge(s["ff_split"], FF)
            expert_out((W_PLEG - 1) % 4, (FF - 1) % 2, last=True)
            norm_pe(pe, 5)

            pe.wait_ge(s["operand"], 7)
            for n in range(KT):
                u = W_PLEG + n
                pe.wait_ge(s["w_lo"], u + 1)
                if n >= 2:
                    pe.wait_ge(s["ple_gate"], n - 1)
                gemm_tile(pe, u % 4, bank(n % 2, T))
            pe.wait_ge(s["ple_op"], 1)
            for n in range(KT):
                u = W_PLE + n // 4
                if n % 4 == 0:
                    pe.wait_ge(s["w_lo"], u + 1)
                if n >= 4:
                    pe.wait_ge(s["ple_add"], n - 3)
                for k in range(2):
                    m = products(bank(3 + n % 4, T), *w_k(u % 4, 2 * (n % 4) + k), pthi[:, k, :], ptlo[:, k, :],
                                 k == 0, k == 1)
                m.then_inc(s["ple_ps"], 1)
            norm_pe(pe, 6)

        @block.scalar
        def _(act):
            A = nc.scalar.activation
            for u in range(LEAD):
                split_hi(act, u, u % 4)
            norm_act(act, 0)

            def hi_for(u):
                split_hi(act, u + LEAD, (u + LEAD) % 4)

            for u in range(4):
                hi_for(u)
                act.wait_ge(s["w_used"], u + 1)
                A(qraw[:, u, 3:], bank(u % 2, T), ACT.Copy).then_inc(s["evac"], 1)
            with act.Fori(1, 3) as i:
                for j in range(4):
                    split_hi(act, None, (j + LEAD) % 4, i + (1 if j + LEAD >= 4 else 0))
                    act.wait_ge(s["w_used"], i * 4 + (j + 1))
                    A(qraw[:, bass.ds(i * 4 + j, 1), 3:], bank(j % 2, T).unsqueeze(1), ACT.Copy).then_inc(s["evac"], 1)
            for u in range(12, 16):
                hi_for(u)
                act.wait_ge(s["w_used"], u + 1)
                A(zs[:, u - 12, :], bank(u % 2, T), ACT.Silu).then_inc(s["evac"], 1)
            for u in range(16, 20):
                hi_for(u)
                act.wait_ge(s["w_used"], u + 1)
                A(pp[:, u - 16, PAD:], bank(u % 2, T), ACT.Copy).then_inc(s["evac"], 1)
            act.wait_ge(s["conv_done"], 12)
            A(qkv[:, :, :], qkv[:, :, :], ACT.Silu).then_inc(s["silu_done"], 1)
            act.wait_ge(s["silu_done"], 1)
            A(sq[:, :, :], qkv[:, 0:8, :], ACT.Square).then_inc(s["qk_sq"], 1)
            act.wait_ge(s["gate_in"], 1)
            A(col["beta"].rearrange("p (n h) -> p n h", n=TB), col["ba"].rearrange("p (n c) -> p n c", n=TB)[:, :, 0:4],
              ACT.Sigmoid).then_inc(s["gate_sig"], 1)
            act.wait_ge(s["gate_in"], 2)
            A(col["e"], col["t2"], ACT.Exp, scale=-1.0).then_inc(s["gate_e"], 1)
            act.wait_ge(s["gate_e"], 1)
            act.wait_ge(s["row_in"], 16)
            A(col["ea"], row[:, 4:8], ACT.Exp).then_inc(s["gate_ea"], 1)
            A(col["l"], col["e"], ACT.Ln, bias=1.0).then_inc(s["gate_l"], 1)
            act.wait_ge(s["qk_ms"], 1)
            A(rn[:, :, :], rn[:, :, :], ACT.Sqrt).then_inc(s["qk_sqrt"], 1)
            act.wait_ge(s["gsub"], 1)
            A(Dm[:, :, :], Dm[:, :, :], ACT.Exp)
            A(DT[:, :, :], DT[:, :, :], ACT.Exp)
            A(eGb[:, :, :], i4(0)[:, DH:NI, :], ACT.Exp)
            A(col["egc"], col["gc"][:, DH:NI], ACT.Exp)
            A(col["kd"], X[:, 0:DH, P - 1:P].rearrange("p h n -> p (h n)"), ACT.Exp).then_inc(s["gexp"], 1)
            act.wait_ge(s["AnT"], 1)
            A(AnT[:, :, :], i4(4), ACT.Copy).then_inc(s["AnT_sb"], 1)
            for l in range(1, 7):
                act.wait_ge(s["U"], l)
                A(Us[:, :, :], i4(0), ACT.Copy).then_inc(s["U_sb"], 1)
            act.wait_ge(s["w_ps"], 1)
            A(Wv[:, :, :], i4(0), ACT.Copy).then_inc(s["w_sb"], 1)
            act.wait_ge(s["kcd_ps"], 1)
            A(kcdT[:, :, :], i4(2)[:, 0:DH, :], ACT.Copy).then_inc(s["kcd_sb"], 1)
            act.wait_ge(s["s1_ps"], 1)
            A(S1[:, :, :], i4(3)[:, 0:DH, :], ACT.Copy).then_inc(s["s1_sb"], 1)
            act.wait_ge(s["o_ps"], 1)
            A(sq[:, 0:DH, :], bank(6, DH * T).rearrange("p (h t) -> p h t", h=DH), ACT.Square).then_inc(s["o_sq"], 1)
            act.wait_ge(s["o_ms"], 1)
            A(rn[:, 0:DH, :], rn[:, 0:DH, :], ACT.Sqrt).then_inc(s["o_sqrt"], 1)
            act.wait_ge(s["pool_ps"], 1)
            for g in range(PG):
                m = A(h32[:, DH + g, :], bank(2, T, base=g * T), ACT.Copy, scale=vcol("pool_scale", g))
            m.then_inc(s["mix_pool"], 1)
            act.wait_ge(s["mix_pool"], 1)
            act.wait_ge(s["mix_dn"], 1)
            operand_act(act, 1, h32)
            for u in range(W_OUT1, W_QUERY):
                hi_for(u)
            norm_act(act, 1)

            for j in range(4):
                hi_for(W_QUERY + j)
                act.wait_ge(s["w_used"], W_QUERY + j + 1)
                A(qs[:, j, :], bank(j % 2, T), ACT.Copy).then_inc(s["evac"], 1)
                if j:
                    act.wait_ge(s["sc_ps"], j)
                    A(sc[:, :, j - 1, :], bank(2 + (j - 1) % 2, T).rearrange("p (b n) -> p b n", b=TB), ACT.Copy)\
                        .then_inc(s["scores"], 1)
            with act.Fori(1, N_QUERY // 4) as i:
                for j in range(4):
                    split_hi(act, None, (j + LEAD) % 4, i + (W_QUERY // 4 + (1 if j + LEAD >= 4 else 0)))
                    act.wait_ge(s["w_used"], i * 4 + (W_QUERY + j + 1))
                    act.wait_ge(s["sc_ps"], i * 4 + (j - 3))
                    A(qs[:, j, :], bank(j % 2, T), ACT.Copy).then_inc(s["evac"], 1)
                    act.wait_ge(s["sc_ps"], i * 4 + j)
                    A(sc[:, :, bass.ds(i * 4 + (j - 1), 1), :].rearrange("p b a n -> p b (a n)"),
                      bank(2 + (j - 1) % 2, T).rearrange("p (b n) -> p b n", b=TB), ACT.Copy).then_inc(s["scores"], 1)
            act.wait_ge(s["sc_ps"], N_QUERY)
            A(sc[:, :, N_QUERY - 1, :], bank(3, T).rearrange("p (b n) -> p b n", b=TB), ACT.Copy).then_inc(s["scores"], 1)
            act.wait_ge(s["cv_ready"], 1)
            A(cv[:, :, :], cv[:, :, :], ACT.Exp).then_inc(s["cv_exp"], 1)
            act.wait_ge(s["seeded"], 1)
            act.wait_ge(s["idxT"], 1)
            A(iT[:, :, :], bank(2, 3 * T).rearrange("p (q t) -> p q t", q=3), ACT.Copy).then_inc(s["idxT_sb"], 1)
            gv = G[:, :, :].rearrange("p i t -> p t i")
            act.wait_ge(s["topk"], 1)
            with act.Fori(0, T // 8) as i:
                for j in range(2):
                    act.wait_ge(s["g_ps"], i * 2 + (j + 1))
                    A(gv[:, bass.ds(i * 8 + 4 * j, 4), :], bank(2 + j, 512).rearrange("p (t n) -> p t n", t=4),
                      ACT.Copy).then_inc(s["g_sb"], 1)
            geo = lambda v: bank(2 + v, T)

            hi_for(W_EXP)
            act.wait_ge(s["g_sb"], T // 4)
            act.wait_ge(s["w_used"], W_EXP + 1)
            A(geo(0), bank(0, T), ACT.Gelu).then_inc(s["gelu"], 1)
            hi_for(W_EXP + 1)
            act.wait_ge(s["w_used"], W_EXP + 2)
            A(geo(1), bank(1, T), ACT.Gelu).then_inc(s["gelu"], 1)
            act.wait_ge(s["p_mul"], 1)
            A(phi[:, 0, :], pf[:, 0, :], ACT.Copy).then_inc(s["p_hi"], 1)
            hi_for(W_EXP + 2)
            with act.Fori(1, N_EXP // 2) as i:
                for v in range(2):
                    dj = W_EXP + 2 * v + 2
                    split_hi(act, None, dj % 4, i + dj // 4)
                    act.wait_ge(s["w_used"], i * 4 + (W_EXP + 2 * v))
                    act.wait_ge(s["p_mul"], i * 2 + (v - 1))
                    A(geo(v), bank(v, T), ACT.Gelu).then_inc(s["gelu"], 1)
                    act.wait_ge(s["p_mul"], i * 2 + v)
                    act.wait_ge(s["w_used"], i * 4 + (W_EXP + 2 * v - 1))
                    A(phi[:, 1 - v, :], pf[:, 1 - v, :], ACT.Copy).then_inc(s["p_hi"], 1)
                    split_hi(act, None, (dj + 1) % 4, i + (dj + 1) // 4)
            act.wait_ge(s["p_mul"], N_EXP)
            act.wait_ge(s["w_used"], W_PROJ2 - 3)
            A(phi[:, 1, :], pf[:, 1, :], ACT.Copy).then_inc(s["p_hi"], 1)
            hi_for(W_PROJ2 - 1)
            act.wait_ge(s["w_used"], W_PROJ2)
            act.wait_ge(s["p_split"], N_EXP)
            for b0 in range(4):
                m = A(x[:, 2 * b0:2 * b0 + 2, :], bank(4 + b0, 512).rearrange("p (k t) -> p k t", k=2), ACT.Copy)
            m.then_inc(s["x2"], 1)
            norm_act(act, 2)
            norm_act(act, 3)

            for n in range(N_PROJ2):
                u = W_PROJ2 + n
                hi_for(u)
                act.wait_ge(s["w_used"], u + 1)
                if n < 16:
                    A(qk2[:, n, :], bank(n % 2, T), ACT.Copy).then_inc(s["evac2"], 1)
                else:
                    A(rgs[:, n - 16, :], bank(n % 2, T), ACT.Silu).then_inc(s["evac2"], 1)
            for u in range(W_V2, W_OUT2):
                hi_for(u)
            act.wait_ge(s["w_used"], W_OUT2)
            for b0 in range(4):
                m = A(vv[:, b0 // 2, (b0 % 2) * 512:(b0 % 2 + 1) * 512], bank(4 + b0, 512), ACT.Copy)
            m.then_inc(s["v_sb"], 1)
            def att_pt(h):
                act.wait_ge(s["pt_ps"], h + 1)
                if h >= 2:
                    act.wait_ge(s["ao_ps"], h - 1)
                A(pT[:, h % 2, :], bank(2 + h % 2, 3 * P), ACT.Copy).then_inc(s["pt_sb"], 1)

            for h in range(MH):
                act.wait_ge(s["s_max"], h + 1)
                if h >= 2:
                    act.wait_ge(s["pt_ps"], h - 1)
                A(pr[:, h % 2, 0:P], sS[:, h % 2, 0:P], ACT.Exp, bias=mx[:, h, 2:3], scale=MD ** -0.5,
                  accum_out=sums[:, h, 0:1])
                A(pr[:, h % 2, P:3 * P], sS[:, h % 2, P:3 * P], ACT.Exp, bias=mx[:, h, 3:4], scale=MD ** -0.5,
                  accum_out=sums[:, h, 1:2]).then_inc(s["s_exp"], 1)
                if h:
                    att_pt(h - 1)
            att_pt(MH - 1)
            act.wait_ge(s["ro_ps"], 1)
            A(ro[:, :, :], bank(6, RH * T).rearrange("p (r t) -> p r t", r=RH), ACT.Copy).then_inc(s["ro_sb"], 1)
            act.wait_ge(s["rxc"], 1)
            A(sq[:, 0:RH, :], ro[:, :, :], ACT.Square).then_inc(s["r_sq"], 1)
            act.wait_ge(s["r_ms"], 1)
            A(rr[:, :, :], rr[:, :, :], ACT.Sqrt).then_inc(s["r_sqrt"], 1)
            act.wait_ge(s["mix_ret"], 1)
            operand_act(act, 4, mix2)
            for u in range(W_OUT2, W_FF):
                hi_for(u)
            norm_act(act, 4)
            for f in range(FF):
                u = W_FF + (3 * f - 1 if f else 0)
                hi_for(u)
                act.wait_ge(s["ff_conv"], f + 1)
                if f >= 2:
                    act.wait_ge(s["ff_mul"], f - 1)
                A(fg[:, f % 2, :], fu[:, f % 2, :], ACT.Gelu_apprx_tanh).then_inc(s["ff_gelu"], 1)
                hi_for(u + 1)
                act.wait_ge(s["ff_mul"], f + 1)
                if f >= 2:
                    act.wait_ge(s["w_used"], W_FF + 3 * (f - 1) + 2)
                A(phi[:, f % 2, :], pf[:, f % 2, :], ACT.Copy).then_inc(s["ff_hi"], 1)
                if f:
                    hi_for(u + 2)
            hi_for(W_PLEG - 1)
            act.wait_ge(s["w_used"], W_PLEG)
            for b0 in range(4):
                m = A(x[:, 2 * b0:2 * b0 + 2, :], bank(4 + b0, 512).rearrange("p (k t) -> p k t", k=2), ACT.Copy)
            m.then_inc(s["x4"], 1)
            norm_act(act, 5)
            act.wait_ge(s["ple_in"], 16)
            A(pthi[:, :, :], pt[:, :, :], ACT.Copy).then_inc(s["ple_hi"], 1)
            for n in range(KT):
                hi_for(W_PLEG + n)
                act.wait_ge(s["w_used"], W_PLEG + n + 1)
                A(gs[:, n, :], bank(n % 2, T), ACT.Sigmoid).then_inc(s["ple_gate"], 1)
            norm_act(act, 6)

        @block.vector
        def _(dve):
            V = nc.vector
            ch = Chain(dve, s["dve"])
            V.memset(ones[:, :], 1.0).then_inc(s["pool"], 1)
            V.memset(qraw[:, :, 0:3], 0.0)
            ch(V.memset(pp[:, :, 0:PAD], 0.0))
            for u in range(LEAD):
                split_lo(dve, u, u % 4)
            norm_dve(dve, ch, 0)

            def lo_for(u):
                split_lo(dve, u + LEAD, (u + LEAD) % 4)

            for n in range(N_PROJ1):
                lo_for(n)
                if n < 12:
                    dve.wait_ge(s["evac"], n + 1)
                    ch(V.tensor_scalar(qkv[:, n, :], qraw[:, n, 3:3 + T], vcol("conv", 3 * 12 + n), None, ALU.mult))
                    for tap in (2, 1):
                        ch(V.scalar_tensor_tensor(qkv[:, n, :], qraw[:, n, tap:tap + T], vcol("conv", tap * 12 + n),
                                                  qkv[:, n, :], ALU.mult, ALU.add))
                    V.scalar_tensor_tensor(qkv[:, n, :], qraw[:, n, 0:T], vcol("conv", n), qkv[:, n, :],
                                           ALU.mult, ALU.add).then_inc(s["conv_done"], 1)
            bv = lambda n: col[n].rearrange("p (n h) -> p n h", n=TB)
            bav = col["ba"].rearrange("p (n c) -> p n c", n=TB)
            dve.wait_ge(s["ba"], 1)
            V.tensor_copy(col["ba"], bank(3, 16)).then_inc(s["gate_in"], 1)
            dve.wait_ge(s["gate_in"], 1)
            dve.wait_ge(s["row_in"], 16)
            ch(V.tensor_tensor(bv("t1"), bav[:, :, 4:8], m3(row[:, 0:4], TB), ALU.add))
            ch(V.tensor_scalar(col["t2"], col["t1"], -1.0, None, ALU.mult))
            V.tensor_tensor(col["t2"], col["t1"], col["t2"], ALU.max).then_inc(s["gate_in"], 1)
            dve.wait_ge(s["gate_l"], 1)
            dve.wait_ge(s["gate_ea"], 1)
            ch(V.scalar_tensor_tensor(col["l"], col["t1"], 0.0, col["l"], ALU.max, ALU.add))
            ch(V.scalar_tensor_tensor(bv("g"), bv("l"), -1.0, m3(col["ea"], TB), ALU.mult, ALU.mult))
            V.tensor_copy(gbc[:, :, :], b3(col["g"], P)).then_inc(s["g_ready"], 1)
            dve.wait_ge(s["gate_sig"], 1)
            ch(V.tensor_scalar(col["nbeta"], col["beta"], -1.0, None, ALU.mult))
            dve.wait_ge(s["qk_ss"], 1)
            dve.wait_ge(s["evac"], N_PROJ1)
            V.tensor_scalar(rn[:, 0:4, :], bank(4, 4 * T).rearrange("p (k t) -> p k t", k=4), EPS, float(P),
                            ALU.add, ALU.mult)
            V.tensor_scalar(rn[:, 4:8, :], bank(6, 4 * T).rearrange("p (k t) -> p k t", k=4), EPS, None,
                            ALU.add).then_inc(s["qk_ms"], 1)
            dve.wait_ge(s["gb"], 1)
            ch(V.tensor_copy(col["gc"], bank(3, NI, base=16)))
            ch(V.tensor_tensor(X[:, :, :], i4(0), b3(col["gc"], P), ALU.subtract))
            V.tensor_scalar(DT[:, :, :], X[:, :, :], 0.0, None, ALU.min)
            V.tensor_scalar(Dm[:, :, :], X[:, :, :], -1.0, 0.0, ALU.mult, ALU.min).then_inc(s["gsub"], 1)
            dve.wait_ge(s["qk_sqrt"], 1)
            ch(V.reciprocal(rn[:, :, :], rn[:, :, :]))
            V.tensor_tensor(qkv[:, 0:8, :], qkv[:, 0:8, :], rn[:, :, :], ALU.mult).then_inc(s["qk_norm"], 1)
            dve.wait_ge(s["gexp"], 1)
            dve.wait_ge(s["c1_in"], 32)
            dve.wait_ge(s["qk_norm"], 1)
            V.tensor_tensor(Dm[:, :, :], Dm[:, :, :], m3(SL, NI), ALU.mult)
            V.tensor_tensor(DT[:, :, :], DT[:, :, :], m3(U1, NI), ALU.mult)
            V.tensor_tensor(qd[:, :, :], qkv[:, 0:DH, P:T], eGb[:, :, :], ALU.mult)
            ch(V.tensor_tensor(col["bg"], col["beta"][:, DH:NI], col["egc"], ALU.mult))
            dve.wait_ge(s["kk"], 1)
            ch(V.tensor_tensor(An[:, :, :], i4(4), Dm[:, :, :], ALU.mult))
            V.tensor_tensor(An[:, :, :], An[:, :, :], b3(col["nbeta"], P), ALU.mult).then_inc(s["An_ready"], 1)
            dve.wait_ge(s["qkt"], 1)
            V.tensor_tensor(attnT[:, :, :], i4(6), DT[:, :, :], ALU.mult)
            dve.wait_ge(s["kvt"], 1)
            V.tensor_tensor(kdec[:, :, :], i4(0)[:, 0:DH, :], b3(col["kd"], P), ALU.mult)
            V.tensor_tensor(kbg[:, :, :], i4(0)[:, DH:NI, :], b3(col["bg"], P), ALU.mult)
            dve.wait_ge(s["kvt"], 2)
            V.tensor_tensor(vb[:, :, :], i4(2), b3(col["beta"], P), ALU.mult).then_inc(s["kv_ready"], 1)
            dve.wait_ge(s["An_ready"], 1)
            ch(V.tensor_tensor(Tm[:, :, :], An[:, :, :], m3(LM0, NI), ALU.mult))
            ch(V.tensor_tensor(Tm[:, :, :], Tm[:, :, :], m3(ident[:, :], NI), ALU.add))
            dve.wait_ge(s["AnT_sb"], 1)
            ch(V.tensor_tensor(TT[:, :, :], AnT[:, :, :], m3(LMT[0], NI), ALU.mult))
            ch(V.tensor_tensor(TT[:, :, :], TT[:, :, :], m3(ident[:, :], NI), ALU.add))
            V.tensor_tensor(AmT[:, :, :], AnT[:, :, :], m3(LMT[1], NI), ALU.mult).then_inc(s["amt"], 1)
            for l in range(1, 7):
                dve.wait_ge(s["Tp"], l)
                m = V.tensor_tensor(TT[:, :, :], TT[:, :, :], i4(2), ALU.add)
                if l < 6:
                    ch(V.tensor_tensor(Tm[:, :, :], Tm[:, :, :], i4(4), ALU.add))
                    V.tensor_tensor(AmT[:, :, :], AnT[:, :, :], m3(LMT[l + 1], NI), ALU.mult).then_inc(s["amt"], 1)
            m.then_inc(s["inverse"], 1)
            dve.wait_ge(s["vn_ps"], 1)
            V.tensor_tensor(Wv[:, DH:NI, :], Wv[:, DH:NI, :], i4(4)[:, 0:DH, :], ALU.subtract).then_inc(s["vn_sb"], 1)
            dve.wait_ge(s["evac"], N_PROJ1)
            N = PAD + T
            ch(V.tensor_tensor(pa[:, :, 1:N], pp[:, :, 1:N], pp[:, :, 0:N - 1], ALU.add))
            ch(V.tensor_tensor(pb[:, 1:, 3:N], pa[:, 1:, 3:N], pa[:, 1:, 1:N - 2], ALU.add))
            ch(V.tensor_tensor(pa[:, 2:, 7:N], pb[:, 2:, 7:N], pb[:, 2:, 3:N - 4], ALU.add))
            ch(V.tensor_tensor(pb[:, 3, 15:N], pa[:, 3, 15:N], pa[:, 3, 7:N - 8], ALU.add))
            for g in range(PG):
                m = V.tensor_tensor(pa[:, g, PAD:], (pa, pb)[g % 2][:, g, PAD:], invc[:, g, :], ALU.mult)
            ch(m)
            V.tensor_tensor(pa[:, :, PAD:], pa[:, :, PAD:], pp[:, :, PAD:], ALU.subtract).then_inc(s["pooled"], 1)
            dve.wait_ge(s["o_ss"], 1)
            V.tensor_scalar(rn[:, 0:DH, :], bank(4, DH * T).rearrange("p (h t) -> p h t", h=DH), 1.0 / P, EPS,
                            ALU.mult, ALU.add).then_inc(s["o_ms"], 1)
            dve.wait_ge(s["o_sqrt"], 1)
            ch(V.reciprocal(rn[:, 0:DH, :], rn[:, 0:DH, :]))
            ch(V.tensor_tensor(rn[:, 0:DH, :], rn[:, 0:DH, :], zs[:, :, :], ALU.mult))
            V.scalar_tensor_tensor(h32[:, 0:DH, :], bank(6, DH * T).rearrange("p (h t) -> p h t", h=DH),
                                   vcol("dn_norm"), rn[:, 0:DH, :], ALU.mult, ALU.mult).then_inc(s["mix_dn"], 1)
            dve.wait_ge(s["mix_dn"], 1)
            operand_dve(dve, 1, h32)
            for n in range(KT):
                u = W_OUT1 + n
                lo_for(u)
                dve.wait_ge(s["w_used"], u + 1)
                V.tensor_tensor(x[:, n, :], x[:, n, :], bank(n % 2, T), ALU.add).then_inc(s["evac"], 1)
            norm_dve(dve, ch, 1)
            for u in range(W_QUERY, W_EXP):
                lo_for(u)
            dve.wait_ge(s["scores"], N_QUERY)
            sets = [(tb, m) for tb in range(TB) for m in range(2 * NH)]

            def top16(vals, idx, data, keys_):
                for k in keys_:
                    m = V.max(out=vals(k)[:, 0:8], in_=data(k))
                ch(m)
                for k in keys_:
                    m = V.max_index(out=idx(k)[:, 0:8], in_max=vals(k)[:, 0:8], in_values=data(k))
                ch(m)
                for k in keys_:
                    m = V.match_replace(out=data(k), in_to_replace=vals(k)[:, 0:8], in_values=data(k), imm_value=NEG)
                ch(m)
                for k in keys_:
                    m = V.max(out=vals(k)[:, 8:16], in_=data(k))
                ch(m)
                for k in keys_:
                    m = V.max_index(out=idx(k)[:, 8:16], in_max=vals(k)[:, 8:16], in_values=data(k))
                ch(m)

            top16(lambda k: v16[:, k[0], k[1], :], lambda k: i16[:, k[0], k[1], :], lambda k: sc[:, k[0], k[1], :], sets)
            V.tensor_copy(i16f[:, :, :, :], i16[:, :, :, :])
            v16s = v16[:, :, :, :].rearrange("p b (h c) k -> p (b h) c k", c=2)
            for k in range(TB * NH):
                m = V.tensor_tensor(cand[:, k, :].rearrange("p (a b) -> p a b", b=TOPK),
                                    b3(v16s[:, k, 0, :], TOPK), m3(v16s[:, k, 1, :], TOPK), ALU.add)
            ch(m)
            top16(lambda k: cv[:, k, :], lambda k: ci[:, k, :], lambda k: cand[:, k, :], range(TB * NH))
            ch(V.tensor_copy(gsum[:, 0, :], cv[:, :, 0]))
            V.tensor_tensor(cv[:, :, :], cv[:, :, :], b3(gsum[:, 0, :], TOPK), ALU.subtract).then_inc(s["cv_ready"], 1)
            civ = ci[:, :, :].rearrange("p g k -> p (g k)")
            V.tensor_scalar(cj[:, 0, :], civ, 4, None, ALU.logical_shift_right)
            ch(V.tensor_scalar(cj[:, 1, :], civ, 15, None, ALU.bitwise_and))
            ch(V.tensor_copy(cf[:, :, :], cj[:, :, :]))
            i16s = i16f[:, :, :, :].rearrange("p b (h c) k -> p (b h) c k", c=2)
            dve.wait_ge(s["keys_in"], 32)
            eqf = eq[:, :, :, :].rearrange("p g k j -> p (g k) j")
            for half in range(2):
                ch(V.tensor_tensor(eqf, b3(cf[:, half, :], TOPK), m3(iota16[:, 0:TOPK], TB * NH * TOPK), ALU.is_equal))
                ch(V.tensor_tensor(eq[:, :, :, :], eq[:, :, :, :],
                                   i16s[:, :, half, :].unsqueeze(2).to_broadcast([P, TB * NH, TOPK, TOPK]), ALU.mult))
                ch(V.tensor_reduce(out=gates[:, half, :, :].rearrange("p b n -> p (b n)"), in_=eqf, op=ALU.add,
                                   axis=AX.X))
            dve.wait_ge(s["cv_exp"], 1)
            ch(V.tensor_reduce(out=gsum[:, 0, :], in_=cv[:, :, :], op=ALU.add, axis=AX.X))
            ch(V.reciprocal(gsum[:, 1, :], gsum[:, 0, :]))
            V.tensor_tensor(gates[:, 2, :, :].rearrange("p b (g k) -> p (b g) k", k=TOPK), cv[:, :, :],
                            b3(gsum[:, 1, :], TOPK), ALU.mult).then_inc(s["topk"], 1)
            dve.wait_ge(s["idxT_sb"], 1)
            dve.wait_ge(s["keys_in"], 48)

            def onehots(t, j):
                for n in range(4):
                    c1_, c2_, cg = (iT[:, q, bass.ds(t + n, 1)] if not isinstance(t, int) else iT[:, q, t + n:t + n + 1]
                                    for q in range(3))
                    V.tensor_scalar(oh1[:, j, n, :], iota[:, :], c1_, None, ALU.is_equal)
                    m = V.tensor_scalar(oh2[:, j, n, :], iota[:, :], c2_, cg, ALU.is_equal, ALU.mult)
                m.then_inc(s["onehot"], 1)

            for j in range(2):
                onehots(4 * j, j)
            with dve.Fori(1, T // 8) as i:
                for j in range(2):
                    dve.wait_ge(s["g_ps"], i * 2 + (j - 1))
                    onehots(i * 8 + 4 * j, j)
            geo = lambda v: bank(2 + v, T)
            gcol = lambda e: G[:, bass.ds(e, 1), :].rearrange("p a t -> p (a t)") if not isinstance(e, int) else G[:, e, :]

            lo_for(W_EXP)
            dve.wait_ge(s["g_sb"], T // 4)
            dve.wait_ge(s["gelu"], 1)
            V.tensor_tensor(pf[:, 0, :], geo(0), gcol(0), ALU.mult).then_inc(s["p_mul"], 1)
            lo_for(W_EXP + 1)
            dve.wait_ge(s["gelu"], 2)
            V.tensor_tensor(pf[:, 1, :], geo(1), gcol(1), ALU.mult).then_inc(s["p_mul"], 1)
            dve.wait_ge(s["p_hi"], 1)
            V.tensor_tensor(plo[:, 0, :], pf[:, 0, :], phi[:, 0, :].bitcast(F32), ALU.subtract).then_inc(s["p_split"], 1)
            lo_for(W_EXP + 2)
            with dve.Fori(1, N_EXP // 2) as i:
                for v in range(2):
                    dj = W_EXP + 2 * v + 2
                    split_lo(dve, None, dj % 4, i + dj // 4)
                    dve.wait_ge(s["gelu"], i * 2 + (v + 1))
                    dve.wait_ge(s["p_split"], i * 2 + (v - 1))
                    V.tensor_tensor(pf[:, v, :], geo(v), gcol(i * 2 + v), ALU.mult).then_inc(s["p_mul"], 1)
                    dve.wait_ge(s["p_hi"], i * 2 + v)
                    V.tensor_tensor(plo[:, 1 - v, :], pf[:, 1 - v, :], phi[:, 1 - v, :].bitcast(F32),
                                    ALU.subtract).then_inc(s["p_split"], 1)
                    split_lo(dve, None, (dj + 1) % 4, i + (dj + 1) // 4)
            dve.wait_ge(s["p_hi"], N_EXP)
            V.tensor_tensor(plo[:, 1, :], pf[:, 1, :], phi[:, 1, :].bitcast(F32), ALU.subtract).then_inc(s["p_split"], 1)
            lo_for(W_PROJ2 - 1)
            norm_dve(dve, ch, 2)
            norm_dve(dve, ch, 3)

            for u in range(W_PROJ2, W_OUT2):
                lo_for(u)
            dve.wait_ge(s["c2_in"], 16)
            slopes = [2.0 ** (-8.0 * (h + 1) / MH) for h in range(MH)]
            norm_p = lambda h: (pr[:, h % 2, 0:P], pr[:, h % 2, P:3 * P])

            def att_norm(h):
                dve.wait_ge(s["s_exp"], h + 1)
                ch(V.reciprocal(sums[:, h, 2:4], sums[:, h, 0:2]))
                V.tensor_scalar(norm_p(h)[0], norm_p(h)[0], sums[:, h, 2:3], None, ALU.mult)
                V.tensor_scalar(norm_p(h)[1], norm_p(h)[1], sums[:, h, 3:4], None, ALU.mult).then_inc(s["s_norm"], 1)

            def att_evac(h):
                r0 = MD * (h % 2)
                dve.wait_ge(s["ao_ps"], h + 1)
                V.tensor_copy(mix2[r0:r0 + MD, h // 2, :], bank(4 + h % 2, T)[r0:r0 + MD, :]).then_inc(s["ao_sb"], 1)

            for h in range(MH):
                dve.wait_ge(s["s_ps"], h + 1)
                if h >= 2:
                    dve.wait_ge(s["s_exp"], h - 1)
                ch(V.scalar_tensor_tensor(sS[:, h % 2, :], dist, slopes[h] * MD ** 0.5, bank(h % 2, 3 * P),
                                          ALU.mult, ALU.add))
                V.tensor_reduce(out=mx[:, h, 0:1], in_=sS[:, h % 2, 0:P], op=ALU.max, axis=AX.X)
                ch(V.tensor_reduce(out=mx[:, h, 1:2], in_=sS[:, h % 2, P:3 * P], op=ALU.max, axis=AX.X))
                V.tensor_scalar(mx[:, h, 2:4], mx[:, h, 0:2], -(MD ** -0.5), None, ALU.mult).then_inc(s["s_max"], 1)
                if h:
                    att_norm(h - 1)
                if h >= 3:
                    att_evac(h - 3)
            att_norm(MH - 1)
            for h in range(MH - 3, MH):
                att_evac(h)
            for r in range(RH):
                dve.wait_ge(s["rs_ps"], r + 1)
                V.tensor_tensor(rS[:, r, :], bank(r % 2, 3 * P), rdec[:, r, :], ALU.mult).then_inc(s["rs_sb"], 1)
            dve.wait_ge(s["ro_sb"], 1)
            dve.wait_ge(s["rmu"], 1)
            V.scalar_tensor_tensor(ro[:, :, :], bank(2, RH * T).rearrange("p (r t) -> p r t", r=RH), -1.0 / P,
                                   ro[:, :, :], ALU.mult, ALU.add).then_inc(s["rxc"], 1)
            dve.wait_ge(s["r_ss"], 1)
            V.tensor_scalar(rr[:, :, :], bank(4, RH * T).rearrange("p (r t) -> p r t", r=RH), 1.0 / P, 1e-5,
                            ALU.mult, ALU.add).then_inc(s["r_ms"], 1)
            dve.wait_ge(s["r_sqrt"], 1)
            ch(V.reciprocal(rr[:, :, :], rr[:, :, :]))
            ch(V.tensor_tensor(rr[:, :, :], rr[:, :, :], rgs[:, :, :], ALU.mult))
            for r in range(RH):
                m = V.scalar_tensor_tensor(mix2[:, RH + r, :], ro[:, r, :], vcol("ret_norm", r), rr[:, r, :],
                                           ALU.mult, ALU.mult)
            m.then_inc(s["mix_ret"], 1)
            dve.wait_ge(s["mix_ret"], 1)
            operand_dve(dve, 4, mix2)
            for n in range(KT):
                u = W_OUT2 + n
                lo_for(u)
                dve.wait_ge(s["w_used"], u + 1)
                V.tensor_tensor(x[:, n, :], x[:, n, :], bank(n % 2, T), ALU.add).then_inc(s["evac2"], 1)
            norm_dve(dve, ch, 4)
            for f in range(FF):
                u = W_FF + (3 * f - 1 if f else 0)
                v = f % 2
                lo_for(u)
                dve.wait_ge(s["w_used"], u + 1)
                if f >= 2:
                    dve.wait_ge(s["ff_gelu"], f - 1)
                up = bank(v, T)
                ch(V.tensor_scalar(fu[:, v, :], up, vcol("conv2", 2 * FF + f), vcol("conv2_b", f), ALU.mult, ALU.add))
                ch(V.scalar_tensor_tensor(fu[:, v, 1:T], up[:, 0:T - 1], vcol("conv2", FF + f), fu[:, v, 1:T],
                                          ALU.mult, ALU.add))
                V.scalar_tensor_tensor(fu[:, v, 2:T], up[:, 0:T - 2], vcol("conv2", f), fu[:, v, 2:T],
                                       ALU.mult, ALU.add).then_inc(s["ff_conv"], 1)
                lo_for(u + 1)
                dve.wait_ge(s["w_used"], u + 2)
                dve.wait_ge(s["ff_gelu"], f + 1)
                if f >= 2:
                    dve.wait_ge(s["ff_split"], f - 1)
                V.tensor_tensor(pf[:, v, :], fg[:, v, :], bank(2 + v, T), ALU.mult).then_inc(s["ff_mul"], 1)
                if f:
                    dve.wait_ge(s["w_hi"], u + 2 + LEAD + 1)
                dve.wait_ge(s["ff_hi"], f + 1)
                V.tensor_tensor(plo[:, v, :], pf[:, v, :], phi[:, v, :].bitcast(F32), ALU.subtract)\
                 .then_inc(s["ff_split"], 1)
                if f:
                    lo_for(u + 2)
            lo_for(W_PLEG - 1)
            norm_dve(dve, ch, 5)
            dve.wait_ge(s["ple_hi"], 1)
            V.tensor_tensor(ptlo[:, :, :], pt[:, :, :], pthi[:, :, :].bitcast(F32), ALU.subtract).then_inc(s["ple_op"], 1)
            for n in range(KT):
                lo_for(W_PLEG + n)
            for n in range(KT):
                dve.wait_ge(s["ple_gate"], n + 1)
                dve.wait_ge(s["ple_ps"], n + 1)
                ch(V.tensor_tensor(gs[:, n, :], gs[:, n, :], bank(3 + n % 4, T), ALU.mult))
                V.tensor_tensor(x[:, n, :], x[:, n, :], gs[:, n, :], ALU.add).then_inc(s["ple_add"], 1)
            norm_dve(dve, ch, 6)


def columns(w):
    n = w.shape[1] // P
    return np.ascontiguousarray(w.reshape(KT, P, n, P).transpose(2, 1, 0, 3)).reshape(n, P, TW)


def rows_of(w):
    return w.reshape(-1, P, TW)


def interleaved(first, second, third=None):
    last = third if third is not None else second
    head = [first] if third is None else [first, second]
    out = []
    for e in range(len(first) + 1):
        if e < len(first):
            out += [h[e] for h in head]
        if e:
            out.append(last[e - 1])
    return np.stack(out)


def pack(v):
    return np.ascontiguousarray(v.reshape(-1, P).T)


def constants():
    i = np.arange(P)
    blk = lambda l: ((i[:, None] >> (l + 1)) == (i[None, :] >> (l + 1))) & (((i[:, None] >> l) & 1) == 1) \
        & (((i[None, :] >> l) & 1) == 0)
    c1 = [i[:, None] <= i[None, :], i[:, None] > i[None, :], blk(0)] + [blk(l).T for l in range(7)]
    t = np.arange(T)
    inv = [np.broadcast_to(np.float32(1) / np.minimum(t + 1, 2 << g).astype(np.float32), (P, T)) for g in range(PG)]
    c1 = np.concatenate([np.asarray(m, np.float32) for m in c1 + inv + [np.eye(P), np.broadcast_to(i, (P, P))]], axis=1)
    q, k = np.arange(T)[None, :], np.arange(T)[:, None]
    ret = []
    for r in range(RH):
        log_g = np.log(1.0 - 2.0 ** (-5.0 - r))
        d = np.where(q >= k, np.exp(log_g * np.maximum(q - k, 0)), 0.0) * P ** -0.5
        ret += [d[0:P, :], d[P:, P:]]
    dist = np.where(q <= k, (q - k).astype(np.float64), -1e30)
    c2 = np.concatenate(ret + [dist[0:P, 0:P], dist[P:, :]], axis=1).astype(np.float32)
    return c1, c2


def kernel(**a):
    import concourse.bacc as bacc
    from concourse.bass_utils import run_bass_kernel_spmd as run

    a = {k: np.asarray(v) for k, v in a.items()}
    w_in, w_in2 = a["w_in"][0], a["w_in_2"][0]
    c1, c2 = constants()
    m, r = 512, 512
    tiles = [
        columns(w_in[:, 0:4 * 512]), columns(w_in[:, 4 * 512 + 8:]),
        columns(a["w_out"][0]), columns(a["w_query"][0]),
        interleaved(np.ascontiguousarray(a["expert_down"][0].reshape(N_EXP, P, KT, P).transpose(0, 3, 2, 1)).reshape(N_EXP, P, TW),
                    rows_of(a["expert_up"][0])),
        columns(np.concatenate([w_in2[:, 0:2 * m], w_in2[:, 3 * m:3 * m + 2 * r], w_in2[:, 3 * m + 3 * r:]], axis=1)),
        rows_of(np.concatenate([w_in2[:, 2 * m:3 * m], w_in2[:, 3 * m + 2 * r:3 * m + 3 * r]], axis=1)),
        columns(a["w_out_2"][0]),
        interleaved(columns(a["w_up_2"][0]), columns(a["w_gate_2"][0]), rows_of(a["w_down_2"][0])),
        columns(a["w_ple_gate_2"][0]),
        a["w_ple_2"][0].reshape(2, P, 2, 4, P).transpose(2, 1, 3, 0, 4).reshape(2, P, TW),
    ]
    w = np.concatenate(tiles)
    assert w.shape[0] == N_TILES
    w = np.ascontiguousarray(w.reshape(N_TILES // 2, 2, P, TW).transpose(0, 2, 1, 3)).reshape(N_TILES // 2, P, 2 * TW)
    vecs = np.concatenate([
        pack(a["norm_mix_w"][0]), np.concatenate([pack(a["conv_w"][0, j]) for j in range(4)], axis=1),
        pack(a["dn_norm_w"][0]), pack(a["pool_scale"][0]), pack(a["norm_ffn_w"][0]), pack(a["norm_final_w"]), pack(a["attn_norm_2"][0]),
        pack(a["ret_norm_2"][0]), pack(a["ffn_norm_2"][0]),
        np.concatenate([pack(a["conv_w_2"][0, j]) for j in range(3)], axis=1), pack(a["conv_b_2"][0]),
        pack(a["ple_norm_2"][0]), pack(a["final_norm_2"])], axis=1)
    feature_major = lambda t: np.ascontiguousarray(t.T.reshape(-1, P, T).transpose(1, 0, 2))
    arrays = {
        "x_t": feature_major(a["x"][0]), "vecs": np.ascontiguousarray(vecs), "wts": w, "c1": c1,
        "gate_w": np.ascontiguousarray(w_in[:, 4 * 512:4 * 512 + 8].reshape(KT, P, 8).transpose(1, 0, 2)),
        "rows": np.concatenate([a["dt_bias"][0], a["a_log"][0]]),
        "w_pool": np.ascontiguousarray(a["w_pool"][0].transpose(1, 0, 2)),
        "keys": np.ascontiguousarray(a["sub_keys"][0].reshape(2 * NH, P, P).transpose(2, 0, 1)),
        "c2": c2, "ple_t": feature_major(a["p_2"][0, 0]),
    }
    nc = bacc.Bacc("TRN2", target_bir_lowering=False, num_devices=1)
    args = [nc.dram_tensor("in_" + n, v.shape, mybir.dt.from_np(v.dtype), kind="ExternalInput").ap()
            for n, v in arrays.items()]
    args.append(nc.dram_tensor("out_0_dram", (P, KT, T), F32, kind="ExternalOutput").ap())
    program(nc, *args)
    got = run(nc, [{"in_" + n: v for n, v in arrays.items()}], core_ids=[0]).results[0]["out_0_dram"]
    return np.ascontiguousarray(got.transpose(1, 0, 2).reshape(D, T).T).reshape(1, T, D)
```

```python
import concourse.bass as bass
from concourse import mybir
from contextlib import ExitStack
import numpy as np

F32 = mybir.dt.float32
F32R = mybir.dt.float32r
BF16 = mybir.dt.bfloat16
U32 = mybir.dt.uint32
ALU = mybir.AluOpType
ACT = mybir.ActivationFunctionType
AX = mybir.AxisListType

P = 128
T = 256
TB = T // P
D = 1024
KT = D // P
TW = KT * P
DH = 4
NI = TB * DH
PG = 4
NH = 8
TOPK = 16
NEG = -3.0e38
EPS = 1e-6
MH, MD = 8, 64
RH = 4
EVERY_A, EVERY_B = 8, 4
CV_AT = 48
GT = 4
N_GROUPS = T // GT
FF = 2816 // P
PAD = 16

W_PROJ1 = 0
N_PROJ1 = 20
W_OUT1 = W_PROJ1 + N_PROJ1
W_QUERY = W_OUT1 + KT
N_QUERY = 2 * NH
W_EXP = W_QUERY + N_QUERY
N_EXP = P
W_UP = W_EXP + N_EXP
W_PROJ2 = W_UP + N_EXP
N_PROJ2 = 20
W_V2 = W_PROJ2 + N_PROJ2
W_OUT2 = W_V2 + KT
W_FF = W_OUT2 + KT
W_PLEG = W_FF + 3 * FF
W_PLE = W_PLEG + KT
N_TILES = W_PLE + 2
RING = 4
LEAD = 3
assert N_TILES % 4 == 0

CV = {}
_c = 0
for _n, _w in (("norm_mix", KT), ("conv", 48), ("dn_norm", 1), ("pool_scale", PG), ("norm_ffn", KT), ("norm_mid", KT),
               ("attn_norm", KT), ("ret_norm", RH), ("ffn_norm", KT), ("conv2", 3 * FF), ("conv2_b", FF),
               ("ple_norm", KT), ("final_norm", KT)):
    CV[_n] = _c
    _c += _w
N_CV = _c

SEMS = """x_in vec_in c1_in gate_w_in row_in wpool_in keys_in c2_in ple_in out_done dve act pe pool
w_hi w_lo w_used raw0 raw1 x_sq ssq norm_ms norm_sqrt norm_h src_hi operand
evac conv_raw conv_done silu_done z_done p_done
qk_sq qk_ss qk_ms qk_sqrt qk_norm ba gate_in gate_sig gate_e gate_l gate_ea g_ready gb gsub gexp
kk qkt kvt kv_ready An_ready AnT AnT_sb T0 amt U U_sb Tp inverse w_ps w_sb kcd_ps kcd_sb s1_ps s1_sb vn_ps vn_sb o_ps
o_sq o_ss o_ms o_sqrt mix_dn pooled pool_ps mix_pool
q_ps q_sb sc_ps scores seeded cv_ready cv_exp cf_ready topk idxT idxT_sb gate_parts oh_eq oh1 g_ps g_mul
gelu p_hi p_split x2 s_ps s_max s_exp s_norm pt_ps pt_sb ao_ps ao_sb v_ps v_sb
rs_ps rs_sb ro_ps ro_sb rmu rxc r_sq r_ss r_ms r_sqrt mix_ret evac2 rg_done
ff_conv ff_gelu ff_mul ff_hi ff_split ff_done ff_seed x4 ple_gate ple_hi ple_op ple_ps ple_add""".split()


def program(nc, x_t, vecs, wts, c1, gate_w, rows, w_pool, keys, c2, ple_t, out):
    ctx = ExitStack()
    with ctx:
        s = {n: ctx.enter_context(nc.semaphore("s_" + n)) for n in SEMS}

        top = [-(-nc.sbuf_base // 32) * 32]
        slab = ctx.enter_context(nc.sbuf_tensor("slab", [P, (nc.sbuf_bytes_remaining - 64) // 4], F32))

        def place(name, shape, dt=F32, at=None):
            size = int(np.prod(shape)) * (2 if dt == BF16 else 4)
            size = -(-size // 32) * 32
            if at is None:
                at, top[0] = top[0], top[0] + size
            else:
                at[0], at = at[0] + size, at[0]
            return nc.alloc_sbuf_tensor_at(name, [P] + list(shape), dt, offset=at)

        raw = place("raw", [2, 2 * TW])
        whi = place("whi", [RING, TW], F32R)
        wlo = place("wlo", [RING, TW], F32R)
        ahi = place("ahi", [KT, T], F32R)
        alo = place("alo", [KT, T], F32R)
        ident = place("ident", [P])
        ones = place("ones", [P])
        vec = place("vec", [N_CV])
        small = top[0]
        x = place("x", [KT, T])
        pf = place("pf", [2, T])
        aux_end = top[0]
        phi = place("phi", [2, T], F32R)
        plo = place("plo", [2, T], F32R)
        aux = [small]
        kT = place("kT", [2, T], BF16, at=aux)
        gT = place("gT", [3, T], BF16, at=aux)
        iota = place("iota", [P, GT], BF16, at=aux)
        oh2 = place("oh2", [2, P, GT], BF16, at=aux)
        oheq = place("oheq", [2, N_EXP // 2, GT], BF16, at=aux)
        oh1 = place("oh1", [2, 3, N_EXP // 2, GT], BF16, at=aux)
        assert aux[0] <= aux_end
        arena = top[0]
        ea = place("ea", [N_EXP, T])
        end = top[0]
        assert end <= nc.sbuf_usable_end, end

        a = [arena]
        h32 = place("h32", [KT, T], at=a)
        sq = place("sq", [KT, T], at=a)
        rstd = place("rstd", [T], at=a)
        rtmp = place("rtmp", [T], at=a)
        common = a[0]
        cst = place("cst", [10 * P + PG * T], at=a)
        U1 = cst[:, 0:P]
        SL = cst[:, P:2 * P]
        LM0 = cst[:, 2 * P:3 * P]
        LMT = [cst[:, (3 + l) * P:(4 + l) * P] for l in range(7)]
        invc = cst[:, 10 * P:10 * P + PG * T].rearrange("p (g t) -> p g t", g=PG)
        gw = place("gw", [KT, 8], at=a)
        row = place("row", [8], at=a)
        wp = place("wp", [PG, P], at=a)
        keep = a[0]
        qraw = place("qraw", [12, T + 3], at=a)
        b = [keep]
        rn = place("rn", [8, T], at=b)
        qkv = place("qkv", [12, T], at=a)
        zs = place("zs", [DH, T], at=a)
        pp = place("pp", [PG, PAD + T], at=a)
        pa = place("pa", [PG, PAD + T], at=a)
        pb = place("pb", [PG, PAD + T], at=a)
        I8 = [NI, P]
        gbc = place("gbc", I8, at=a)
        AmT = gbc
        Dm = place("Dm", I8, at=a)
        Tm = Dm
        DT = place("DT", I8, at=a)
        X = place("X", I8, at=a)
        Us = X
        attnT = DT
        An = place("An", I8, at=a)
        AnT = place("AnT", I8, at=a)
        TT = place("TT", I8, at=a)
        eGb = place("eGb", [DH, P], at=a)
        kbg = place("kbg", [DH, P], at=a)
        kdec = place("kdec", [DH, P], at=a)
        vb = place("vb", I8, at=a)
        Wv = place("Wv", I8, at=a)
        kcdT = place("kcdT", [DH, P], at=a)
        S1 = place("S1", [DH, P], at=a)
        qd = kcdT_q = place("qd", [DH, P], at=a)
        tok = place("tok", [160], at=a)
        assert a[0] <= end, a[0] - end
        col = {}
        c = 0
        for n, w in (("ba", 16), ("beta", 8), ("nbeta", 8), ("t1", 8), ("t2", 8), ("e", 8), ("l", 8), ("ea", 4),
                     ("g", 8), ("gc", 8), ("egc", 4), ("bg", 4), ("kd", 4)):
            col[n] = tok[:, c:c + w]
            c += w
        a = [common]
        qs = place("qs", [4, T], at=a)
        kk = place("kk", [2 * NH, P], at=a)
        assert a[0] <= arena + 4 * T * N_EXP // 2
        a = [arena + 4 * T * N_EXP // 2]
        b = list(a)
        sc = place("sc", [TB, 2 * NH, P], at=a)
        eq0 = place("eq0", [TB * NH, TOPK, TOPK], at=b)
        eq1 = place("eq1", [TB * NH, TOPK, TOPK], at=b)
        cand = place("cand", [TB * NH, TOPK * TOPK], at=a)
        v16 = place("v16", [TB, 2 * NH, TOPK], at=a)
        i16 = place("i16", [TB, 2 * NH, TOPK], U32, at=a)
        i16f = place("i16f", [TB, 2 * NH, TOPK], at=a)
        cv = place("cv", [TB * NH, TOPK], at=a)
        ci = place("ci", [TB * NH, TOPK], U32, at=a)
        cj = place("cj", [2, TB * NH * TOPK], U32, at=a)
        cf = place("cf", [2, TB * NH * TOPK], at=a)
        gates = place("gates", [3, TB, P], at=a)
        gsum = place("gsum", [2, TB * NH], at=a)
        iota16 = place("iota16", [P], at=a)
        grest = place("grest", [T], at=a)
        assert a[0] <= end
        a = [common]
        qk2 = place("qk2", [16, T], at=a)
        rgs = place("rgs", [RH, T], at=a)
        vv = place("vv", [TB, D], at=a)
        cs2 = place("cs2", [RH * 3 * P + 3 * P], at=a)
        rdec = cs2[:, 0:RH * 3 * P].rearrange("p (r n) -> p r n", r=RH)
        dist = cs2[:, RH * 3 * P:]
        sS = place("sS", [2, 3 * P], at=a)
        pr = place("pr", [2, 3 * P], at=a)
        pT = place("pT", [2, 3 * P], at=a)
        mx = place("mx", [MH, 4], at=a)
        sums = place("sums", [MH, 4], at=a)
        rS = place("rS", [RH, 3 * P], at=a)
        ro = place("ro", [RH, T], at=a)
        rr = place("rr", [RH, T], at=a)
        mix2 = place("mix2", [KT, T], at=a)
        fu = place("fu", [2, T], at=a)
        fg = place("fg", [2, T], at=a)
        gs = place("gs", [KT, T], at=a)
        pt = place("pt", [2, T], at=a)
        pthi = place("pthi", [2, T], F32R, at=a)
        ptlo = place("ptlo", [2, T], F32R, at=a)
        assert a[0] <= end

        ps = ctx.enter_context(nc.psum_tensor("ps", [P, 8, 512], F32))
        flat = ps[:, :, :].rearrange("p b n -> p (b n)")

        def bank(b0, n, shape=None, base=0):
            v = flat[:, b0 * 512 + base:b0 * 512 + base + n]
            return v

        def vcol(name, j=0):
            return vec[:, CV[name] + j:CV[name] + j + 1]

        def b3(ap, n):
            return ap.unsqueeze(2).to_broadcast([P, ap.shape[1], n])

        def m3(ap, n):
            return ap.unsqueeze(1).to_broadcast([P, n, ap.shape[1]])

        block = ctx.enter_context(nc.Block())

        def raw_tile(half, k):
            return raw[:, half, k * TW:(k + 1) * TW]

        @block.sync
        def _(sp):
            sp.dma_start(x[:, :, :], x_t).then_inc(s["x_in"], 16)
            sp.dma_start(vec[:, :], vecs).then_inc(s["vec_in"], 16)
            rs = (s["raw0"], s["raw1"])
            for p in range(2):
                sp.dma_start(raw[:, p, :], wts[p]).then_inc(rs[p], 16)
            with sp.Fori(1, N_TILES // 4) as i:
                for p in range(2):
                    sp.wait_ge(s["w_hi"], i * 4 + (2 * p - 2))
                    sp.wait_ge(s["w_lo"], i * 4 + (2 * p - 2))
                    sp.dma_start(raw[:, p, :], wts[bass.ds(i * 2 + p, 1), :, :].rearrange("a p n -> p (a n)"))\
                      .then_inc(rs[p], 16)
            sp.wait_ge(s["norm_h"], 7)
            sp.dma_start(out, h32[:, :, :]).then_inc(s["out_done"], 16)
            sp.wait_ge(s["out_done"], 16)

        @block.gpsimd
        def _(pl):
            pl.dma_start(gw[:, :, :], gate_w).then_inc(s["gate_w_in"], 16)
            pl.dma_start(row[:, :], rows.partition_broadcast(P)).then_inc(s["row_in"], 16)
            pl.dma_start(ident[:, :], c1[:, 10 * P + PG * T:11 * P + PG * T]).then_inc(s["c1_in"], 16)
            pl.dma_start(cst[:, :], c1[:, 0:10 * P + PG * T]).then_inc(s["c1_in"], 16)
            pl.dma_start(wp[:, :, :], w_pool).then_inc(s["wpool_in"], 16)
            pl.wait_ge(s["operand"], 2)
            pl.dma_start(kk[:, :, :], keys).then_inc(s["keys_in"], 16)
            pl.dma_start(iota16[:, :], c1[:, 11 * P + PG * T:12 * P + PG * T]).then_inc(s["keys_in"], 16)
            pl.wait_ge(s["p_split"], N_EXP)
            pl.dma_start(cs2[:, :], c2).then_inc(s["c2_in"], 16)
            pl.dma_start(pt[:, :, :], ple_t).then_inc(s["ple_in"], 16)

        def split_hi(act, u, j, quad=None):
            if quad is None:
                if u >= N_TILES:
                    return
                act.wait_ge((s["raw0"], s["raw1"])[j // 2], 16 * (u // 4 + 1))
                if u >= RING:
                    act.wait_ge(s["w_used"], u - RING + 1)
            else:
                act.wait_ge((s["raw0"], s["raw1"])[j // 2], quad * 16 + 16)
                act.wait_ge(s["w_used"], quad * 4 + (j - RING + 1))
            nc.scalar.activation(whi[:, j, :], raw_tile(j // 2, j % 2), ACT.Copy).then_inc(s["w_hi"], 1)

        def split_lo(dve, u, j, quad=None):
            if quad is None:
                if u >= N_TILES:
                    return
                dve.wait_ge(s["w_hi"], u + 1)
                if u >= RING:
                    dve.wait_ge(s["w_used"], u - RING + 1)
            else:
                dve.wait_ge(s["w_hi"], quad * 4 + (j + 1))
                dve.wait_ge(s["w_used"], quad * 4 + (j - RING + 1))
            nc.vector.tensor_tensor(wlo[:, j, :], raw_tile(j // 2, j % 2), whi[:, j, :].bitcast(F32),
                                    ALU.subtract).then_inc(s["w_lo"], 1)

        def products(out_ap, wh, wl, xh, xl, first, last):
            nc.tensor.matmul(out_ap, wh, xh, start=first, stop=False, skip_group_check=True)
            nc.tensor.matmul(out_ap, wh, xl, start=False, stop=False, skip_group_check=True)
            return nc.tensor.matmul(out_ap, wl, xh, start=False, stop=last, skip_group_check=True)

        def w_k(j, k):
            return whi[:, j, k * P:(k + 1) * P], wlo[:, j, k * P:(k + 1) * P]

        def gemm_tile(pe, j, dst):
            for k in range(KT):
                m = products(dst, *w_k(j, k), ahi[:, k, :], alo[:, k, :], k == 0, k == KT - 1)
            m.then_inc(s["w_used"], 1)

        class Chain:

            def __init__(self, eng, sem):
                self.eng, self.sem, self.n = eng, sem, 0

            def __call__(self, ins):
                ins.then_inc(self.sem, 1)
                self.n += 1
                self.eng.wait_ge(self.sem, self.n)

        X_READY = [(s["x_in"], 16), (s["evac"], W_QUERY), (s["x2"], 1), (s["norm_h"], 3), (s["evac2"], N_PROJ2 + KT), (s["x4"], 1), (s["ple_add"], KT)]
        NORM_W = ["norm_mix", "norm_ffn", "norm_mid", "attn_norm", "ffn_norm", "ple_norm", "final_norm"]
        NORM_OP = [0, 2, None, 3, 5, 6, None]
        USED_BEFORE = [0, W_OUT1, W_QUERY, W_PROJ2, W_OUT2, W_FF, W_PLEG]

        def norm_act(act, i):
            act.wait_ge(*X_READY[i])
            if i == 4:
                act.wait_ge(s["mix_ret"], 1)
            nc.scalar.activation(sq[:, :, :], x[:, :, :], ACT.Square).then_inc(s["x_sq"], 1)
            act.wait_ge(s["norm_ms"], i + 1)
            nc.scalar.activation(rstd[:, :], rtmp[:, :], ACT.Sqrt).then_inc(s["norm_sqrt"], 1)
            if NORM_OP[i] is not None:
                operand_act(act, NORM_OP[i], h32)

        def norm_pe(pe, i):
            pe.wait_ge(s["x_sq"], i + 1)
            if i == 0:
                pe.wait_ge(s["pool"], 1)
            for k in range(KT):
                m = nc.tensor.matmul(bank(2, T), ones[:, :], sq[:, k, :], start=k == 0, stop=k == KT - 1)
            m.then_inc(s["ssq"], 1)

        def norm_dve(dve, ch, i):
            if i == 0:
                dve.wait_ge(s["x_in"], 16)
                dve.wait_ge(s["vec_in"], 16)
            dve.wait_ge(s["ssq"], i + 1)
            nc.vector.tensor_scalar(rtmp[:, :], bank(2, T), 1.0 / D, EPS, ALU.mult, ALU.add).then_inc(s["norm_ms"], 1)
            dve.wait_ge(s["norm_sqrt"], i + 1)
            ch(nc.vector.reciprocal(rtmp[:, :], rstd[:, :]))
            for k in range(KT):
                m = nc.vector.scalar_tensor_tensor((x if i == 2 else h32)[:, k, :], x[:, k, :], vcol(NORM_W[i], k), rtmp[:, :],
                                                   ALU.mult, ALU.mult)
            m.then_inc(s["norm_h"], 1)
            dve.wait_ge(s["norm_h"], i + 1)
            if NORM_OP[i] is not None:
                operand_dve(dve, NORM_OP[i], h32)

        def operand_act(act, n, src):
            if n in NORM_OP:
                act.wait_ge(s["norm_h"], NORM_OP.index(n) + 1)
            if n:
                act.wait_ge(s["w_used"], USED_BEFORE[n])
            nc.scalar.activation(ahi[:, :, :], src[:, :, :], ACT.Copy).then_inc(s["src_hi"], 1)

        def operand_dve(dve, n, src):
            dve.wait_ge(s["src_hi"], n + 1)
            nc.vector.tensor_tensor(alo[:, :, :], src[:, :, :], ahi[:, :, :].bitcast(F32), ALU.subtract)\
              .then_inc(s["operand"], 1)

        i4 = lambda b0, n=NI: bank(b0, n * P).rearrange("p (i n) -> p i n", n=P)

        @block.tensor
        def _(pe):
            tm = nc.tensor.matmul
            norm_pe(pe, 0)

            pe.wait_ge(s["operand"], 1)
            for u in range(2):
                pe.wait_ge(s["w_lo"], u + 1)
                gemm_tile(pe, u % RING, bank(u % 2, T))
            for u in range(2, 4):
                pe.wait_ge(s["w_lo"], u + 1)
                pe.wait_ge(s["evac"], u - 1)
                gemm_tile(pe, u % RING, bank(u % 2, T))
            with pe.Fori(1, N_PROJ1 // 4) as i:
                for j in range(4):
                    pe.wait_ge(s["w_lo"], i * 4 + (j + 1))
                    pe.wait_ge(s["evac"], i * 4 + (j - 1))
                    gemm_tile(pe, j, bank(j % 2, T))
            pe.wait_ge(s["gate_w_in"], 16)
            pe.wait_ge(s["norm_h"], 1)
            for n in range(TB):
                for k in range(KT):
                    m = tm(bank(3, 8, base=8 * n), h32[:, k, n * P:(n + 1) * P], gw[:, k, :],
                           start=k == 0, stop=k == KT - 1)
            m.then_inc(s["ba"], 1)
            pe.wait_ge(s["qk_sq"], 1)
            for b0 in range(4):
                m = tm(bank(4 + b0, 512), ones[:, :], sq[:, 2 * b0:2 * b0 + 2, :], start=True, stop=True)
            m.then_inc(s["qk_ss"], 1)
            pe.wait_ge(s["c1_in"], 32)
            pe.wait_ge(s["g_ready"], 1)
            for n in range(TB):
                tm(bank(3, DH, base=16 + DH * n), U1, col["g"][:, n * DH:(n + 1) * DH], start=True, stop=True)
            pe.wait_ge(s["evac"], N_PROJ1)
            for i in range(NI):
                m = tm(i4(0)[:, i, :], gbc[:, i, :], U1, start=True, stop=True)
            m.then_inc(s["gb"], 1)
            pe.wait_ge(s["qk_norm"], 1)
            for n in range(TB):
                for h in range(DH):
                    kc = qkv[:, DH + h, n * P:(n + 1) * P]
                    m = tm(i4(4)[:, n * DH + h, :], kc, kc, start=True, stop=True)
            m.then_inc(s["kk"], 1)
            for n in range(TB):
                for h in range(DH):
                    m = tm(i4(6)[:, n * DH + h, :], qkv[:, DH + h, n * P:(n + 1) * P],
                           qkv[:, h, n * P:(n + 1) * P], start=True, stop=True)
            m.then_inc(s["qkt"], 1)
            pe.wait_ge(s["gexp"], 1)
            for n in range(TB):
                for h in range(DH):
                    m = nc.tensor.transpose(i4(0)[:, n * DH + h, :], qkv[:, DH + h, n * P:(n + 1) * P], ident[:, :])
            m.then_inc(s["kvt"], 1)
            pe.wait_ge(s["norm_ms"], 1)
            pe.wait_ge(s["gate_l"], 1)
            pe.wait_ge(s["gsub"], 1)
            for n in range(TB):
                for h in range(DH):
                    m = nc.tensor.transpose(i4(2)[:, n * DH + h, :], qkv[:, 2 * DH + h, n * P:(n + 1) * P],
                                            ident[:, :])
            m.then_inc(s["kvt"], 1)
            pe.wait_ge(s["An_ready"], 1)
            for i in range(NI):
                m = nc.tensor.transpose(i4(4)[:, i, :], An[:, i, :], ident[:, :])
            m.then_inc(s["AnT"], 1)
            pe.wait_ge(s["kv_ready"], 1)
            for l in range(1, 7):
                pe.wait_ge(s["amt"], l)
                for i in range(NI):
                    m = tm(i4(0)[:, i, :], AmT[:, i, :], Tm[:, i, :], start=True, stop=True)
                m.then_inc(s["U"], 1)
                pe.wait_ge(s["U_sb"], l)
                for i in range(NI):
                    m = tm(i4(2)[:, i, :], Us[:, i, :], TT[:, i, :], start=True, stop=True)
                if l < 6:
                    for i in range(NI):
                        m = tm(i4(4)[:, i, :], TT[:, i, :], Us[:, i, :], start=True, stop=True)
                m.then_inc(s["Tp"], 1)
            pe.wait_ge(s["inverse"], 1)
            for i in range(NI):
                m = tm(i4(0)[:, i, :], TT[:, i, :], vb[:, i, :], start=True, stop=True)
            m.then_inc(s["w_ps"], 1)
            for h in range(DH):
                m = tm(i4(2)[:, h, :], kbg[:, h, :], TT[:, DH + h, :], start=True, stop=True)
            m.then_inc(s["kcd_ps"], 1)
            pe.wait_ge(s["w_sb"], 1)
            for h in range(DH):
                m = tm(i4(3)[:, h, :], kdec[:, h, :], Wv[:, h, :], start=True, stop=True)
            m.then_inc(s["s1_ps"], 1)
            pe.wait_ge(s["kcd_sb"], 1)
            pe.wait_ge(s["s1_sb"], 1)
            for h in range(DH):
                m = tm(i4(4)[:, h, :], kcdT[:, h, :], S1[:, h, :], start=True, stop=True)
            m.then_inc(s["vn_ps"], 1)
            pe.wait_ge(s["vn_sb"], 1)
            for h in range(DH):
                o = bank(6, T, base=h * T)
                tm(o[:, 0:P], Wv[:, h, :], attnT[:, h, :], start=True, stop=True)
                tm(o[:, P:T], S1[:, h, :], qd[:, h, :], start=True, stop=False)
                m = tm(o[:, P:T], Wv[:, DH + h, :], attnT[:, DH + h, :], start=False, stop=True)
            m.then_inc(s["o_ps"], 1)
            pe.wait_ge(s["o_sq"], 1)
            for b0 in range(2):
                m = tm(bank(4 + b0, 512), ones[:, :], sq[:, 2 * b0:2 * b0 + 2, :], start=True, stop=True)
            m.then_inc(s["o_ss"], 1)
            pe.wait_ge(s["wpool_in"], 16)
            pe.wait_ge(s["pooled"], 1)
            for g in range(PG):
                m = tm(bank(2, T, base=g * T), wp[:, g, :], pa[:, g, PAD:], start=True, stop=True)
            m.then_inc(s["pool_ps"], 1)

            pe.wait_ge(s["operand"], 2)
            def plain_stage(first, n, sem, base):
                assert first % 4 == 0
                for j in range(4):
                    pe.wait_ge(s["w_lo"], first + j + 1)
                    if base + j >= 2:
                        pe.wait_ge(sem, base + j - 1)
                    gemm_tile(pe, j, bank(j % 2, T))
                if n > 4:
                    with pe.Fori(1, n // 4) as i:
                        for j in range(4):
                            pe.wait_ge(s["w_lo"], i * 4 + (first + j + 1))
                            pe.wait_ge(sem, i * 4 + (base + j - 1))
                            gemm_tile(pe, j, bank(j % 2, T))
            plain_stage(W_OUT1, KT, s["evac"], N_PROJ1)
            norm_pe(pe, 1)

            pe.wait_ge(s["operand"], 3)
            pe.wait_ge(s["keys_in"], 32)

            def scores(m_idx, slot, key):
                for tb in range(TB):
                    m = tm(bank(2 + slot % 2, P, base=tb * P), qs[:, slot, tb * P:(tb + 1) * P], key,
                           start=True, stop=True)
                m.then_inc(s["sc_ps"], 1)

            for j in range(4):
                pe.wait_ge(s["w_lo"], W_QUERY + j + 1)
                pe.wait_ge(s["evac"], W_QUERY + j - 1)
                gemm_tile(pe, j, bank(j % 2, T))
                if j >= 1:
                    pe.wait_ge(s["evac"], W_QUERY + j)
                    if j >= 3:
                        pe.wait_ge(s["scores"], j - 2)
                    scores(j - 1, j - 1, kk[:, j - 1, :])
            with pe.Fori(1, N_QUERY // 4) as i:
                for j in range(4):
                    pe.wait_ge(s["w_lo"], i * 4 + (W_QUERY + j + 1))
                    pe.wait_ge(s["evac"], i * 4 + (W_QUERY + j - 1))
                    gemm_tile(pe, j, bank(j % 2, T))
                    pe.wait_ge(s["evac"], i * 4 + (W_QUERY + j))
                    pe.wait_ge(s["scores"], i * 4 + (j - 2))
                    scores(None, (j - 1) % 4, kk[:, bass.ds(i * 4 + (j - 1), 1), :].rearrange("p a n -> p (a n)"))
            pe.wait_ge(s["evac"], W_EXP)
            pe.wait_ge(s["scores"], N_QUERY - 2)
            scores(None, 3, kk[:, N_QUERY - 1, :])

            for b0 in range(4):
                m = tm(bank(4 + b0, 512), ident[:, :], x[:, 2 * b0:2 * b0 + 2, :],
                       start=True, stop=False, skip_group_check=True)
            m.then_inc(s["seeded"], 1)

            def hidden(j, r):
                gemm_tile(pe, j, bank(r, T))

            for n in range(4):
                pe.wait_ge(s["w_lo"], W_EXP + n + 1)
                if n >= 2:
                    pe.wait_ge(s["gelu"], n - 1)
                hidden(n, n % 2)
            with pe.Fori(1, N_EXP // 8) as i:
                for n in range(4):
                    pe.wait_ge(s["w_lo"], i * 4 + (W_EXP + n + 1))
                    pe.wait_ge(s["gelu"], i * 4 + (n - 1))
                    hidden(n, n % 2)
            half = N_EXP // 2

            def gate_group(j):
                for t in range(GT):
                    for part in range(3):
                        m = tm(bank(2 + j, half, base=t * half), oh2[:, j, :, t], oh1[:, j, part, :, t],
                               start=part == 0, stop=part == 2)
                m.then_inc(s["g_ps"], 1)

            for n in range(4):
                pe.wait_ge(s["w_lo"], W_EXP + half + n + 1)
                pe.wait_ge(s["gelu"], half + n - 1)
                hidden(n, n % 2)
                if n == 1:
                    pe.wait_ge(s["topk"], 1)
                    pe.wait_ge(s["scores"], N_QUERY)
                    for q in range(3):
                        for tb in range(TB):
                            m = nc.tensor.transpose(bank(2, P, base=q * T + tb * P), gates[:, q, tb, :], ident[:, :])
                    m.then_inc(s["idxT"], 1)
                    pe.wait_ge(s["gate_parts"], 1)
                for g in ((), (0, 1), (2,), (3,))[n]:
                    pe.wait_ge(s["oh1"], g + 1)
                    if g >= 2:
                        pe.wait_ge(s["g_mul"], g - 1)
                    gate_group(g % 2)
            with pe.Fori(1, N_EXP // 8) as i:
                for n in range(4):
                    pe.wait_ge(s["w_lo"], i * 4 + (W_EXP + half + n + 1))
                    pe.wait_ge(s["gelu"], i * 4 + (half + n - 1))
                    hidden(n, n % 2)
                    pe.wait_ge(s["oh1"], i * 4 + (n + 1))
                    pe.wait_ge(s["g_mul"], i * 4 + (n - 1))
                    gate_group(n % 2)

            def expert_out(j, r, last=False):
                for k in range(KT):
                    m = products(bank(4, T, base=k * T), *w_k(j, k), phi[:, r, :], plo[:, r, :], False, last)
                m.then_inc(s["w_used"], 1)

            with pe.Fori(0, N_EXP // 8) as i:
                for n in range(4):
                    pe.wait_ge(s["w_lo"], i * 4 + (W_UP + n + 1))
                    pe.wait_ge(s["p_split"], i * 4 + (n + 1))
                    expert_out(n, n % 2)
                    pe.wait_ge(s["oh1"], i * 4 + (N_GROUPS + n + 1))
                    pe.wait_ge(s["g_mul"], i * 4 + (N_GROUPS + n - 1))
                    gate_group(n % 2)
            with pe.Fori(0, N_EXP // 8) as i:
                for n in range(4):
                    pe.wait_ge(s["w_lo"], i * 4 + (W_UP + half + n + 1))
                    pe.wait_ge(s["p_split"], i * 4 + (half + n + 1))
                    expert_out(n, n % 2)
            norm_pe(pe, 2)
            norm_pe(pe, 3)

            pe.wait_ge(s["operand"], 4)
            plain_stage(W_PROJ2, N_PROJ2, s["evac2"], 0)
            for k in range(KT):
                u = W_V2 + k
                pe.wait_ge(s["w_lo"], u + 1)
                j = u % 4
                for tb in range(TB):
                    for half in range(2):
                        m = products(bank(4 + 2 * tb + half, 512), ahi[:, k, tb * P:(tb + 1) * P],
                                     alo[:, k, tb * P:(tb + 1) * P], whi[:, j, half * 512:(half + 1) * 512],
                                     wlo[:, j, half * 512:(half + 1) * 512], k == 0, k == KT - 1)
                m.then_inc(s["w_used"], 1)

            pe.wait_ge(s["evac2"], N_PROJ2)

            def att_scores(h):
                r0, jt = MD * (h % 2), h // 2
                rows_ = slice(r0, r0 + MD)
                if h >= 2:
                    pe.wait_ge(s["s_max"], h - 1)
                tm(bank(h % 2, P), qk2[rows_, jt, 0:P], qk2[rows_, 4 + jt, 0:P], start=True, stop=True)
                tm(bank(h % 2, T, base=P), qk2[rows_, jt, P:T], qk2[rows_, 4 + jt, 0:T], start=True, stop=True)\
                    .then_inc(s["s_ps"], 1)

            def att_transposed(h):
                pe.wait_ge(s["s_norm"], h + 1)
                if h >= 2:
                    pe.wait_ge(s["pt_sb"], h - 1)
                for q in range(3):
                    m = nc.tensor.transpose(bank(2 + h % 2, P, base=q * P), pr[:, h % 2, q * P:(q + 1) * P],
                                            ident[:, :])
                m.then_inc(s["pt_ps"], 1)

            def att_out(h):
                r0, jt = MD * (h % 2), h // 2
                pe.wait_ge(s["pt_sb"], h + 1)
                if h == 0:
                    pe.wait_ge(s["v_sb"], 1)
                if h >= 2:
                    pe.wait_ge(s["ao_sb"], h - 1)
                o = bank(4 + h % 2, T)[r0:r0 + MD, :]
                vh = lambda tb: vv[:, tb, h * MD:(h + 1) * MD]
                tm(o[:, 0:P], vh(0), pT[:, h % 2, 0:P], start=True, stop=True)
                tm(o[:, P:T], vh(0), pT[:, h % 2, P:2 * P], start=True, stop=False)
                tm(o[:, P:T], vh(1), pT[:, h % 2, 2 * P:3 * P], start=False, stop=True).then_inc(s["ao_ps"], 1)

            att_scores(0)
            for h in range(MH):
                if h + 1 < MH:
                    att_scores(h + 1)
                att_transposed(h)
                if h:
                    att_out(h - 1)
            att_out(MH - 1)

            pe.wait_ge(s["s_max"], MH)
            for r in range(RH):
                if r >= 2:
                    pe.wait_ge(s["rs_sb"], r - 1)
                tm(bank(r % 2, T), qk2[:, 12 + r, 0:P], qk2[:, 8 + r, 0:T], start=True, stop=True)
                tm(bank(r % 2, P, base=T), qk2[:, 12 + r, P:T], qk2[:, 8 + r, P:T], start=True, stop=True)\
                    .then_inc(s["rs_ps"], 1)
            for r in range(RH):
                pe.wait_ge(s["rs_sb"], r + 1)
                o = bank(6, T, base=r * T)
                vr = lambda tb: vv[:, tb, 512 + r * P:512 + (r + 1) * P]
                tm(o[:, 0:P], vr(0), rS[:, r, 0:P], start=True, stop=True)
                tm(o[:, P:T], vr(0), rS[:, r, P:T], start=True, stop=False)
                m = tm(o[:, P:T], vr(1), rS[:, r, T:T + P], start=False, stop=True)
            m.then_inc(s["ro_ps"], 1)
            pe.wait_ge(s["ro_sb"], 1)
            pe.wait_ge(s["pt_sb"], MH)
            for b0 in range(2):
                m = tm(bank(2 + b0, 512), ones[:, :], ro[:, 2 * b0:2 * b0 + 2, :], start=True, stop=True)
            m.then_inc(s["rmu"], 1)
            pe.wait_ge(s["r_sq"], 1)
            pe.wait_ge(s["ao_sb"], MH)
            for b0 in range(2):
                m = tm(bank(4 + b0, 512), ones[:, :], sq[:, 2 * b0:2 * b0 + 2, :], start=True, stop=True)
            m.then_inc(s["r_ss"], 1)

            pe.wait_ge(s["operand"], 5)
            plain_stage(W_OUT2, KT, s["evac2"], N_PROJ2)
            norm_pe(pe, 4)

            pe.wait_ge(s["operand"], 6)
            for b0 in range(4):
                tm(bank(4 + b0, 512), ident[:, :], x[:, 2 * b0:2 * b0 + 2, :],
                   start=True, stop=False, skip_group_check=True)
            for f in range(FF):
                u = W_FF + (3 * f - 1 if f else 0)
                v = f % 2
                for n in range(2):
                    pe.wait_ge(s["w_lo"], u + n + 1)
                    if f >= 2 and n == 0:
                        pe.wait_ge(s["ff_conv"], f - 1)
                    if f >= 2 and n == 1:
                        pe.wait_ge(s["ff_mul"], f - 1)
                    gemm_tile(pe, (u + n) % 4, bank(2 * n + v, T))
                if f:
                    pe.wait_ge(s["w_lo"], u + 3)
                    pe.wait_ge(s["ff_split"], f)
                    expert_out((u + 2) % 4, (f - 1) % 2)
            pe.wait_ge(s["w_lo"], W_PLEG)
            pe.wait_ge(s["ff_split"], FF)
            expert_out((W_PLEG - 1) % 4, (FF - 1) % 2, last=True)
            norm_pe(pe, 5)

            pe.wait_ge(s["operand"], 7)
            for n in range(KT):
                u = W_PLEG + n
                pe.wait_ge(s["w_lo"], u + 1)
                if n >= 2:
                    pe.wait_ge(s["ple_gate"], n - 1)
                gemm_tile(pe, u % 4, bank(n % 2, T))
            pe.wait_ge(s["ple_op"], 1)
            for n in range(KT):
                u = W_PLE + n // 4
                if n % 4 == 0:
                    pe.wait_ge(s["w_lo"], u + 1)
                if n >= 4:
                    pe.wait_ge(s["ple_add"], n - 3)
                for k in range(2):
                    m = products(bank(3 + n % 4, T), *w_k(u % 4, 2 * (n % 4) + k), pthi[:, k, :], ptlo[:, k, :],
                                 k == 0, k == 1)
                m.then_inc(s["ple_ps"], 1)
            norm_pe(pe, 6)

        @block.scalar
        def _(act):
            A = nc.scalar.activation
            for u in range(LEAD):
                split_hi(act, u, u % 4)
            norm_act(act, 0)

            def hi_for(u):
                split_hi(act, u + LEAD, (u + LEAD) % 4)

            for u in range(4):
                hi_for(u)
                act.wait_ge(s["w_used"], u + 1)
                A(qraw[:, u, 3:], bank(u % 2, T), ACT.Copy).then_inc(s["evac"], 1)
            with act.Fori(1, 3) as i:
                for j in range(4):
                    split_hi(act, None, (j + LEAD) % 4, i + (1 if j + LEAD >= 4 else 0))
                    act.wait_ge(s["w_used"], i * 4 + (j + 1))
                    A(qraw[:, bass.ds(i * 4 + j, 1), 3:], bank(j % 2, T).unsqueeze(1), ACT.Copy).then_inc(s["evac"], 1)
            for u in range(12, 16):
                hi_for(u)
                act.wait_ge(s["w_used"], u + 1)
                A(zs[:, u - 12, :], bank(u % 2, T), ACT.Silu).then_inc(s["evac"], 1)
            for u in range(16, 20):
                hi_for(u)
                act.wait_ge(s["w_used"], u + 1)
                A(pp[:, u - 16, PAD:], bank(u % 2, T), ACT.Copy).then_inc(s["evac"], 1)
            act.wait_ge(s["conv_done"], 12)
            A(qkv[:, :, :], qkv[:, :, :], ACT.Silu).then_inc(s["silu_done"], 1)
            act.wait_ge(s["silu_done"], 1)
            A(sq[:, :, :], qkv[:, 0:8, :], ACT.Square).then_inc(s["qk_sq"], 1)
            act.wait_ge(s["gate_in"], 1)
            A(col["beta"].rearrange("p (n h) -> p n h", n=TB), col["ba"].rearrange("p (n c) -> p n c", n=TB)[:, :, 0:4],
              ACT.Sigmoid).then_inc(s["gate_sig"], 1)
            act.wait_ge(s["gate_in"], 2)
            A(col["e"], col["t2"], ACT.Exp, scale=-1.0).then_inc(s["gate_e"], 1)
            act.wait_ge(s["gate_e"], 1)
            act.wait_ge(s["row_in"], 16)
            A(col["ea"], row[:, 4:8], ACT.Exp).then_inc(s["gate_ea"], 1)
            A(col["l"], col["e"], ACT.Ln, bias=1.0).then_inc(s["gate_l"], 1)
            act.wait_ge(s["qk_ms"], 1)
            A(rn[:, :, :], rn[:, :, :], ACT.Sqrt).then_inc(s["qk_sqrt"], 1)
            act.wait_ge(s["gsub"], 1)
            A(Dm[:, :, :], Dm[:, :, :], ACT.Exp)
            A(DT[:, :, :], DT[:, :, :], ACT.Exp)
            A(eGb[:, :, :], i4(0)[:, DH:NI, :], ACT.Exp)
            A(col["egc"], col["gc"][:, DH:NI], ACT.Exp)
            A(col["kd"], X[:, 0:DH, P - 1:P].rearrange("p h n -> p (h n)"), ACT.Exp).then_inc(s["gexp"], 1)
            act.wait_ge(s["AnT"], 1)
            A(AnT[:, :, :], i4(4), ACT.Copy).then_inc(s["AnT_sb"], 1)
            for l in range(1, 7):
                act.wait_ge(s["U"], l)
                A(Us[:, :, :], i4(0), ACT.Copy).then_inc(s["U_sb"], 1)
            act.wait_ge(s["w_ps"], 1)
            A(Wv[:, :, :], i4(0), ACT.Copy).then_inc(s["w_sb"], 1)
            act.wait_ge(s["kcd_ps"], 1)
            A(kcdT[:, :, :], i4(2)[:, 0:DH, :], ACT.Copy).then_inc(s["kcd_sb"], 1)
            act.wait_ge(s["s1_ps"], 1)
            A(S1[:, :, :], i4(3)[:, 0:DH, :], ACT.Copy).then_inc(s["s1_sb"], 1)
            act.wait_ge(s["o_ps"], 1)
            A(sq[:, 0:DH, :], bank(6, DH * T).rearrange("p (h t) -> p h t", h=DH), ACT.Square).then_inc(s["o_sq"], 1)
            act.wait_ge(s["o_ms"], 1)
            A(rn[:, 0:DH, :], rn[:, 0:DH, :], ACT.Sqrt).then_inc(s["o_sqrt"], 1)
            act.wait_ge(s["pool_ps"], 1)
            for g in range(PG):
                m = A(h32[:, DH + g, :], bank(2, T, base=g * T), ACT.Copy, scale=vcol("pool_scale", g))
            m.then_inc(s["mix_pool"], 1)
            act.wait_ge(s["mix_pool"], 1)
            act.wait_ge(s["mix_dn"], 1)
            operand_act(act, 1, h32)
            for u in range(W_OUT1, W_QUERY):
                hi_for(u)
            norm_act(act, 1)

            for j in range(4):
                hi_for(W_QUERY + j)
                act.wait_ge(s["w_used"], W_QUERY + j + 1)
                A(qs[:, j, :], bank(j % 2, T), ACT.Copy).then_inc(s["evac"], 1)
                if j:
                    act.wait_ge(s["sc_ps"], j)
                    A(sc[:, :, j - 1, :], bank(2 + (j - 1) % 2, T).rearrange("p (b n) -> p b n", b=TB), ACT.Copy)\
                        .then_inc(s["scores"], 1)
            with act.Fori(1, N_QUERY // 4) as i:
                for j in range(4):
                    split_hi(act, None, (j + LEAD) % 4, i + (W_QUERY // 4 + (1 if j + LEAD >= 4 else 0)))
                    act.wait_ge(s["w_used"], i * 4 + (W_QUERY + j + 1))
                    act.wait_ge(s["sc_ps"], i * 4 + (j - 3))
                    A(qs[:, j, :], bank(j % 2, T), ACT.Copy).then_inc(s["evac"], 1)
                    act.wait_ge(s["sc_ps"], i * 4 + j)
                    A(sc[:, :, bass.ds(i * 4 + (j - 1), 1), :].rearrange("p b a n -> p b (a n)"),
                      bank(2 + (j - 1) % 2, T).rearrange("p (b n) -> p b n", b=TB), ACT.Copy).then_inc(s["scores"], 1)
            act.wait_ge(s["sc_ps"], N_QUERY)
            A(sc[:, :, N_QUERY - 1, :], bank(3, T).rearrange("p (b n) -> p b n", b=TB), ACT.Copy).then_inc(s["scores"], 1)
            half = N_EXP // 2
            row_of = lambda e: ea[:, e, :] if isinstance(e, int) else \
                ea[:, bass.ds(e, 1), :].rearrange("p a t -> p (a t)")

            def gelu(n, quad=None, base=0):
                u = W_EXP + base + n + LEAD
                if quad is None:
                    split_hi(act, u, u % 4)
                    act.wait_ge(s["w_used"], W_EXP + base + n + 1)
                    A(row_of(base + n), bank(n % 2, T), ACT.Gelu).then_inc(s["gelu"], 1)
                else:
                    split_hi(act, None, u % 4, quad + u // 4)
                    act.wait_ge(s["w_used"], quad * 4 + (W_EXP + base + n + 1))
                    A(row_of(quad * 4 + (base + n)), bank(n % 2, T), ACT.Gelu).then_inc(s["gelu"], 1)

            with act.Fori(0, CV_AT // 4) as i:
                for n in range(4):
                    gelu(n, i)
            act.wait_ge(s["cv_ready"], 1)
            A(cv[:, :, :], cv[:, :, :], ACT.Exp).then_inc(s["cv_exp"], 1)
            with act.Fori(CV_AT // 4, N_EXP // 8) as i:
                for n in range(4):
                    gelu(n, i)
            split_hi(act, W_EXP + half + LEAD, (W_EXP + half + LEAD) % 4)
            act.wait_ge(s["seeded"], 1)
            act.wait_ge(s["idxT"], 1)
            A(kT[:, :, :], bank(2, 2 * T).rearrange("p (q t) -> p q t", q=2), ACT.Copy)
            A(gT[:, 0, :], bank(3, T), ACT.Copy).then_inc(s["idxT_sb"], 1)
            act.wait_ge(s["gate_parts"], 1)
            act.wait_ge(s["w_used"], W_EXP + half + 1)
            A(row_of(half), bank(0, T), ACT.Gelu).then_inc(s["gelu"], 1)
            for n in range(1, 4):
                gelu(n, None, half)
            with act.Fori(1, N_EXP // 8) as i:
                for n in range(4):
                    gelu(n, i, half)

            def p_hi(n, quad=None, base=0):
                u = W_UP + base + n + LEAD
                if quad is None:
                    if base + n >= 2:
                        act.wait_ge(s["w_used"], W_UP + base + n - 1)
                    A(phi[:, n % 2, :], row_of(base + n), ACT.Copy).then_inc(s["p_hi"], 1)
                    split_hi(act, u, u % 4)
                else:
                    act.wait_ge(s["w_used"], quad * 4 + (W_UP + base + n - 1))
                    A(phi[:, n % 2, :], row_of(quad * 4 + (base + n)), ACT.Copy).then_inc(s["p_hi"], 1)
                    split_hi(act, None, u % 4, quad + u // 4)

            act.wait_ge(s["g_mul"], N_GROUPS)
            for n in range(4):
                p_hi(n)
            with act.Fori(1, N_EXP // 8) as i:
                for n in range(4):
                    p_hi(n, i)
            act.wait_ge(s["g_mul"], 2 * N_GROUPS)
            with act.Fori(0, N_EXP // 8) as i:
                for n in range(4):
                    p_hi(n, i, half)
            act.wait_ge(s["w_used"], W_PROJ2)
            act.wait_ge(s["p_split"], N_EXP)
            for b0 in range(4):
                m = A(x[:, 2 * b0:2 * b0 + 2, :], bank(4 + b0, 512).rearrange("p (k t) -> p k t", k=2), ACT.Copy)
            m.then_inc(s["x2"], 1)
            norm_act(act, 2)
            norm_act(act, 3)

            for n in range(N_PROJ2):
                u = W_PROJ2 + n
                hi_for(u)
                act.wait_ge(s["w_used"], u + 1)
                if n < 16:
                    A(qk2[:, n, :], bank(n % 2, T), ACT.Copy).then_inc(s["evac2"], 1)
                else:
                    A(rgs[:, n - 16, :], bank(n % 2, T), ACT.Silu).then_inc(s["evac2"], 1)
            for u in range(W_V2, W_OUT2):
                hi_for(u)
            act.wait_ge(s["w_used"], W_OUT2)
            for b0 in range(4):
                m = A(vv[:, b0 // 2, (b0 % 2) * 512:(b0 % 2 + 1) * 512], bank(4 + b0, 512), ACT.Copy)
            m.then_inc(s["v_sb"], 1)
            def att_pt(h):
                act.wait_ge(s["pt_ps"], h + 1)
                if h >= 2:
                    act.wait_ge(s["ao_ps"], h - 1)
                A(pT[:, h % 2, :], bank(2 + h % 2, 3 * P), ACT.Copy).then_inc(s["pt_sb"], 1)

            for h in range(MH):
                act.wait_ge(s["s_max"], h + 1)
                if h >= 2:
                    act.wait_ge(s["pt_ps"], h - 1)
                A(pr[:, h % 2, 0:P], sS[:, h % 2, 0:P], ACT.Exp, bias=mx[:, h, 2:3], scale=MD ** -0.5,
                  accum_out=sums[:, h, 0:1])
                A(pr[:, h % 2, P:3 * P], sS[:, h % 2, P:3 * P], ACT.Exp, bias=mx[:, h, 3:4], scale=MD ** -0.5,
                  accum_out=sums[:, h, 1:2]).then_inc(s["s_exp"], 1)
                if h:
                    att_pt(h - 1)
            att_pt(MH - 1)
            act.wait_ge(s["ro_ps"], 1)
            A(ro[:, :, :], bank(6, RH * T).rearrange("p (r t) -> p r t", r=RH), ACT.Copy).then_inc(s["ro_sb"], 1)
            act.wait_ge(s["rxc"], 1)
            A(sq[:, 0:RH, :], ro[:, :, :], ACT.Square).then_inc(s["r_sq"], 1)
            act.wait_ge(s["r_ms"], 1)
            A(rr[:, :, :], rr[:, :, :], ACT.Sqrt).then_inc(s["r_sqrt"], 1)
            act.wait_ge(s["mix_ret"], 1)
            operand_act(act, 4, mix2)
            for u in range(W_OUT2, W_FF):
                hi_for(u)
            norm_act(act, 4)
            for f in range(FF):
                u = W_FF + (3 * f - 1 if f else 0)
                hi_for(u)
                act.wait_ge(s["ff_conv"], f + 1)
                if f >= 2:
                    act.wait_ge(s["ff_mul"], f - 1)
                A(fg[:, f % 2, :], fu[:, f % 2, :], ACT.Gelu_apprx_tanh).then_inc(s["ff_gelu"], 1)
                hi_for(u + 1)
                act.wait_ge(s["ff_mul"], f + 1)
                if f >= 2:
                    act.wait_ge(s["w_used"], W_FF + 3 * (f - 1) + 2)
                A(phi[:, f % 2, :], pf[:, f % 2, :], ACT.Copy).then_inc(s["ff_hi"], 1)
                if f:
                    hi_for(u + 2)
            hi_for(W_PLEG - 1)
            act.wait_ge(s["w_used"], W_PLEG)
            for b0 in range(4):
                m = A(x[:, 2 * b0:2 * b0 + 2, :], bank(4 + b0, 512).rearrange("p (k t) -> p k t", k=2), ACT.Copy)
            m.then_inc(s["x4"], 1)
            norm_act(act, 5)
            act.wait_ge(s["ple_in"], 16)
            A(pthi[:, :, :], pt[:, :, :], ACT.Copy).then_inc(s["ple_hi"], 1)
            for n in range(KT):
                hi_for(W_PLEG + n)
                act.wait_ge(s["w_used"], W_PLEG + n + 1)
                A(gs[:, n, :], bank(n % 2, T), ACT.Sigmoid).then_inc(s["ple_gate"], 1)
            norm_act(act, 6)

        @block.vector
        def _(dve):
            V = nc.vector
            ch = Chain(dve, s["dve"])
            V.memset(ones[:, :], 1.0).then_inc(s["pool"], 1)
            V.memset(qraw[:, :, 0:3], 0.0)
            ch(V.memset(pp[:, :, 0:PAD], 0.0))
            for u in range(LEAD):
                split_lo(dve, u, u % 4)
            norm_dve(dve, ch, 0)

            def lo_for(u):
                split_lo(dve, u + LEAD, (u + LEAD) % 4)

            for n in range(N_PROJ1):
                lo_for(n)
                if n < 12:
                    dve.wait_ge(s["evac"], n + 1)
                    ch(V.tensor_scalar(qkv[:, n, :], qraw[:, n, 3:3 + T], vcol("conv", 3 * 12 + n), None, ALU.mult))
                    for tap in (2, 1):
                        ch(V.scalar_tensor_tensor(qkv[:, n, :], qraw[:, n, tap:tap + T], vcol("conv", tap * 12 + n),
                                                  qkv[:, n, :], ALU.mult, ALU.add))
                    V.scalar_tensor_tensor(qkv[:, n, :], qraw[:, n, 0:T], vcol("conv", n), qkv[:, n, :],
                                           ALU.mult, ALU.add).then_inc(s["conv_done"], 1)
            bv = lambda n: col[n].rearrange("p (n h) -> p n h", n=TB)
            bav = col["ba"].rearrange("p (n c) -> p n c", n=TB)
            dve.wait_ge(s["ba"], 1)
            V.tensor_copy(col["ba"], bank(3, 16)).then_inc(s["gate_in"], 1)
            dve.wait_ge(s["gate_in"], 1)
            dve.wait_ge(s["row_in"], 16)
            ch(V.tensor_tensor(bv("t1"), bav[:, :, 4:8], m3(row[:, 0:4], TB), ALU.add))
            ch(V.tensor_scalar(col["t2"], col["t1"], -1.0, None, ALU.mult))
            V.tensor_tensor(col["t2"], col["t1"], col["t2"], ALU.max).then_inc(s["gate_in"], 1)
            dve.wait_ge(s["gate_l"], 1)
            dve.wait_ge(s["gate_ea"], 1)
            ch(V.scalar_tensor_tensor(col["l"], col["t1"], 0.0, col["l"], ALU.max, ALU.add))
            ch(V.scalar_tensor_tensor(bv("g"), bv("l"), -1.0, m3(col["ea"], TB), ALU.mult, ALU.mult))
            V.tensor_copy(gbc[:, :, :], b3(col["g"], P)).then_inc(s["g_ready"], 1)
            dve.wait_ge(s["gate_sig"], 1)
            ch(V.tensor_scalar(col["nbeta"], col["beta"], -1.0, None, ALU.mult))
            dve.wait_ge(s["qk_ss"], 1)
            dve.wait_ge(s["evac"], N_PROJ1)
            V.tensor_scalar(rn[:, 0:4, :], bank(4, 4 * T).rearrange("p (k t) -> p k t", k=4), EPS, float(P),
                            ALU.add, ALU.mult)
            V.tensor_scalar(rn[:, 4:8, :], bank(6, 4 * T).rearrange("p (k t) -> p k t", k=4), EPS, None,
                            ALU.add).then_inc(s["qk_ms"], 1)
            dve.wait_ge(s["gb"], 1)
            ch(V.tensor_copy(col["gc"], bank(3, NI, base=16)))
            ch(V.tensor_tensor(X[:, :, :], i4(0), b3(col["gc"], P), ALU.subtract))
            V.tensor_scalar(DT[:, :, :], X[:, :, :], 0.0, None, ALU.min)
            V.tensor_scalar(Dm[:, :, :], X[:, :, :], -1.0, 0.0, ALU.mult, ALU.min).then_inc(s["gsub"], 1)
            dve.wait_ge(s["qk_sqrt"], 1)
            ch(V.reciprocal(rn[:, :, :], rn[:, :, :]))
            V.tensor_tensor(qkv[:, 0:8, :], qkv[:, 0:8, :], rn[:, :, :], ALU.mult).then_inc(s["qk_norm"], 1)
            dve.wait_ge(s["gexp"], 1)
            dve.wait_ge(s["c1_in"], 32)
            dve.wait_ge(s["qk_norm"], 1)
            V.tensor_tensor(Dm[:, :, :], Dm[:, :, :], m3(SL, NI), ALU.mult)
            V.tensor_tensor(DT[:, :, :], DT[:, :, :], m3(U1, NI), ALU.mult)
            V.tensor_tensor(qd[:, :, :], qkv[:, 0:DH, P:T], eGb[:, :, :], ALU.mult)
            ch(V.tensor_tensor(col["bg"], col["beta"][:, DH:NI], col["egc"], ALU.mult))
            dve.wait_ge(s["kk"], 1)
            ch(V.tensor_tensor(An[:, :, :], i4(4), Dm[:, :, :], ALU.mult))
            V.tensor_tensor(An[:, :, :], An[:, :, :], b3(col["nbeta"], P), ALU.mult).then_inc(s["An_ready"], 1)
            dve.wait_ge(s["qkt"], 1)
            V.tensor_tensor(attnT[:, :, :], i4(6), DT[:, :, :], ALU.mult)
            dve.wait_ge(s["kvt"], 1)
            V.tensor_tensor(kdec[:, :, :], i4(0)[:, 0:DH, :], b3(col["kd"], P), ALU.mult)
            V.tensor_tensor(kbg[:, :, :], i4(0)[:, DH:NI, :], b3(col["bg"], P), ALU.mult)
            dve.wait_ge(s["kvt"], 2)
            V.tensor_tensor(vb[:, :, :], i4(2), b3(col["beta"], P), ALU.mult).then_inc(s["kv_ready"], 1)
            dve.wait_ge(s["An_ready"], 1)
            ch(V.tensor_tensor(Tm[:, :, :], An[:, :, :], m3(LM0, NI), ALU.mult))
            ch(V.tensor_tensor(Tm[:, :, :], Tm[:, :, :], m3(ident[:, :], NI), ALU.add))
            dve.wait_ge(s["AnT_sb"], 1)
            ch(V.tensor_tensor(TT[:, :, :], AnT[:, :, :], m3(LMT[0], NI), ALU.mult))
            ch(V.tensor_tensor(TT[:, :, :], TT[:, :, :], m3(ident[:, :], NI), ALU.add))
            V.tensor_tensor(AmT[:, :, :], AnT[:, :, :], m3(LMT[1], NI), ALU.mult).then_inc(s["amt"], 1)
            for l in range(1, 7):
                dve.wait_ge(s["Tp"], l)
                m = V.tensor_tensor(TT[:, :, :], TT[:, :, :], i4(2), ALU.add)
                if l < 6:
                    ch(V.tensor_tensor(Tm[:, :, :], Tm[:, :, :], i4(4), ALU.add))
                    V.tensor_tensor(AmT[:, :, :], AnT[:, :, :], m3(LMT[l + 1], NI), ALU.mult).then_inc(s["amt"], 1)
            m.then_inc(s["inverse"], 1)
            dve.wait_ge(s["vn_ps"], 1)
            V.tensor_tensor(Wv[:, DH:NI, :], Wv[:, DH:NI, :], i4(4)[:, 0:DH, :], ALU.subtract).then_inc(s["vn_sb"], 1)
            dve.wait_ge(s["evac"], N_PROJ1)
            N = PAD + T
            ch(V.tensor_tensor(pa[:, :, 1:N], pp[:, :, 1:N], pp[:, :, 0:N - 1], ALU.add))
            ch(V.tensor_tensor(pb[:, 1:, 3:N], pa[:, 1:, 3:N], pa[:, 1:, 1:N - 2], ALU.add))
            ch(V.tensor_tensor(pa[:, 2:, 7:N], pb[:, 2:, 7:N], pb[:, 2:, 3:N - 4], ALU.add))
            ch(V.tensor_tensor(pb[:, 3, 15:N], pa[:, 3, 15:N], pa[:, 3, 7:N - 8], ALU.add))
            for g in range(PG):
                m = V.tensor_tensor(pa[:, g, PAD:], (pa, pb)[g % 2][:, g, PAD:], invc[:, g, :], ALU.mult)
            ch(m)
            V.tensor_tensor(pa[:, :, PAD:], pa[:, :, PAD:], pp[:, :, PAD:], ALU.subtract).then_inc(s["pooled"], 1)
            dve.wait_ge(s["o_ss"], 1)
            V.tensor_scalar(rn[:, 0:DH, :], bank(4, DH * T).rearrange("p (h t) -> p h t", h=DH), 1.0 / P, EPS,
                            ALU.mult, ALU.add).then_inc(s["o_ms"], 1)
            dve.wait_ge(s["o_sqrt"], 1)
            ch(V.reciprocal(rn[:, 0:DH, :], rn[:, 0:DH, :]))
            ch(V.tensor_tensor(rn[:, 0:DH, :], rn[:, 0:DH, :], zs[:, :, :], ALU.mult))
            V.scalar_tensor_tensor(h32[:, 0:DH, :], bank(6, DH * T).rearrange("p (h t) -> p h t", h=DH),
                                   vcol("dn_norm"), rn[:, 0:DH, :], ALU.mult, ALU.mult).then_inc(s["mix_dn"], 1)
            dve.wait_ge(s["mix_dn"], 1)
            operand_dve(dve, 1, h32)
            for n in range(KT):
                u = W_OUT1 + n
                lo_for(u)
                dve.wait_ge(s["w_used"], u + 1)
                V.tensor_tensor(x[:, n, :], x[:, n, :], bank(n % 2, T), ALU.add).then_inc(s["evac"], 1)
            norm_dve(dve, ch, 1)
            for u in range(W_QUERY, W_EXP):
                lo_for(u)
            half = N_EXP // 2
            at = [0]

            def next_tile(n=1):
                for _ in range(n):
                    if at[0] < half:
                        lo_for(W_EXP + at[0])
                        at[0] += 1

            dve.wait_ge(s["scores"], N_QUERY)
            sets = [(tb, m) for tb in range(TB) for m in range(2 * NH)]

            def top16(vals, idx, data, keys_, every):
                def each(one):
                    for n, k in enumerate(keys_):
                        m = one(k)
                        if n % every == every - 1:
                            ch(m)
                            next_tile()
                    ch(m) if len(keys_) % every else None

                each(lambda k: V.max(out=vals(k)[:, 0:8], in_=data(k)))
                each(lambda k: V.max_index(out=idx(k)[:, 0:8], in_max=vals(k)[:, 0:8], in_values=data(k)))
                each(lambda k: V.match_replace(out=data(k), in_to_replace=vals(k)[:, 0:8], in_values=data(k),
                                               imm_value=NEG))
                each(lambda k: V.max(out=vals(k)[:, 8:16], in_=data(k)))
                each(lambda k: V.max_index(out=idx(k)[:, 8:16], in_max=vals(k)[:, 8:16], in_values=data(k)))

            top16(lambda k: v16[:, k[0], k[1], :], lambda k: i16[:, k[0], k[1], :], lambda k: sc[:, k[0], k[1], :],
                  sets, EVERY_A)
            V.tensor_copy(i16f[:, :, :, :], i16[:, :, :, :])
            v16s = v16[:, :, :, :].rearrange("p b (h c) k -> p (b h) c k", c=2)
            for k in range(TB * NH):
                m = V.tensor_tensor(cand[:, k, :].rearrange("p (a b) -> p a b", b=TOPK),
                                    b3(v16s[:, k, 0, :], TOPK), m3(v16s[:, k, 1, :], TOPK), ALU.add)
                if k % EVERY_B == EVERY_B - 1:
                    next_tile()
            ch(m)
            top16(lambda k: cv[:, k, :], lambda k: ci[:, k, :], lambda k: cand[:, k, :], range(TB * NH), EVERY_B)
            ch(V.tensor_copy(gsum[:, 0, :], cv[:, :, 0]))
            V.tensor_tensor(cv[:, :, :], cv[:, :, :], b3(gsum[:, 0, :], TOPK), ALU.subtract).then_inc(s["cv_ready"], 1)
            civ = ci[:, :, :].rearrange("p g k -> p (g k)")
            V.tensor_scalar(cj[:, 0, :], civ, 4, None, ALU.logical_shift_right)
            ch(V.tensor_scalar(cj[:, 1, :], civ, 15, None, ALU.bitwise_and))
            V.tensor_copy(cf[:, :, :], cj[:, :, :]).then_inc(s["cf_ready"], 1)
            i16s = i16f[:, :, :, :].rearrange("p b (h c) k -> p (b h) c k", c=2)
            dve.wait_ge(s["keys_in"], 32)
            dve.wait_ge(s["cf_ready"], 1)
            eqf = lambda e: e[:, :, :, :].rearrange("p g k j -> p (g k) j")
            next_tile()
            for half_, e in ((0, eq0), (1, eq1)):
                ch(V.tensor_tensor(eqf(e), b3(cf[:, half_, :], TOPK), m3(iota16[:, 0:TOPK], TB * NH * TOPK),
                                   ALU.is_equal))
                next_tile(2)
                ch(V.tensor_tensor(e[:, :, :, :], e[:, :, :, :],
                                   i16s[:, :, half_, :].unsqueeze(2).to_broadcast([P, TB * NH, TOPK, TOPK]), ALU.mult))
                next_tile(2)
                ch(V.tensor_reduce(out=gates[:, half_, :, :].rearrange("p b n -> p (b n)"), in_=eqf(e), op=ALU.add,
                                   axis=AX.X))
                next_tile(2)
            dve.wait_ge(s["cv_exp"], 1)
            ch(V.tensor_reduce(out=gsum[:, 0, :], in_=cv[:, :, :], op=ALU.add, axis=AX.X))
            ch(V.reciprocal(gsum[:, 1, :], gsum[:, 0, :]))
            V.tensor_tensor(gates[:, 2, :, :].rearrange("p b (g k) -> p (b g) k", k=TOPK), cv[:, :, :],
                            b3(gsum[:, 1, :], TOPK), ALU.mult).then_inc(s["topk"], 1)
            next_tile(half)
            assert at[0] == half

            def one_hots(t, j, h):
                v = [a_[:, q, bass.ds(t, GT)] if not isinstance(t, int) else a_[:, q, t:t + GT]
                     for a_, q in ((kT, 0), (kT, 1))]
                V.tensor_tensor(oh2[:, j, :, :], iota[:, :, :], m3(v[1], P), ALU.is_equal)
                V.tensor_tensor(oheq[:, j, :, :], iota[:, h * half:(h + 1) * half, :], m3(v[0], half),
                                ALU.is_equal).then_inc(s["oh_eq"], 1)

            def first_keys_gated(g, t, j):
                dve.wait_ge(s["oh_eq"], g + 1)
                v = gT[:, :, t:t + GT] if isinstance(t, int) else gT[:, :, bass.ds(t, GT)]
                V.tensor_tensor(oh1[:, j, :, :, :], oheq[:, j, :, :].unsqueeze(1).to_broadcast([P, 3, half, GT]),
                                v.unsqueeze(2).to_broadcast([P, 3, half, GT]), ALU.mult).then_inc(s["oh1"], 1)

            def apply_gates(g, t, j, h):
                dve.wait_ge(s["g_ps"], g + 1)
                v = ea[:, h * half:(h + 1) * half, :].rearrange("p e t -> p t e")
                v = v[:, t:t + GT, :] if isinstance(t, int) else v[:, bass.ds(t, GT), :]
                V.tensor_tensor(v, v, bank(2 + j, GT * half).rearrange("p (t e) -> p t e", t=GT), ALU.mult)\
                 .then_inc(s["g_mul"], 1)

            def lay_out(n, quad, h):
                g = n + h * N_GROUPS
                t = n * GT
                if quad is not None:
                    g, t = quad * 4 + g, quad * (4 * GT) + t
                if quad is not None or g >= 2:
                    dve.wait_ge(s["g_ps"], g - 1)
                one_hots(t, n % 2, h)
                first_keys_gated(g, t, n % 2)

            def apply(n, quad, h):
                g = n + h * N_GROUPS
                t = n * GT
                if quad is not None:
                    g, t = quad * 4 + g, quad * (4 * GT) + t
                apply_gates(g, t, n % 2, h)

            dve.wait_ge(s["idxT_sb"], 1)
            ch(V.tensor_tensor(grest[:, :], bank(3, T), gT[:, 0, :], ALU.subtract))
            ch(V.tensor_copy(gT[:, 1, :], grest[:, :]))
            ch(V.tensor_tensor(gT[:, 2, :], grest[:, :], gT[:, 1, :], ALU.subtract))
            V.tensor_copy(iota[:, :, :], b3(iota16[:, :], GT)).then_inc(s["gate_parts"], 1)
            dve.wait_ge(s["gate_parts"], 1)
            lay_out(0, None, 0)

            def hidden_step(n, quad=None):
                u = W_EXP + half + n + LEAD
                split_lo(dve, None, u % 4, quad + u // 4) if quad is not None else lo_for(u - LEAD)
                lay_out(n + 1, quad, 0) if n < half - 1 else lay_out(0, None, 1)
                if quad is not None or n:
                    apply(n - 1, quad, 0)

            dve.wait_ge(s["gelu"], half)
            for n in range(4):
                hidden_step(n)
            with dve.Fori(1, N_EXP // 8 - 1) as i:
                for n in range(4):
                    hidden_step(n, i)
            for n in range(half - 4, half):
                hidden_step(n)
            apply(half - 1, None, 0)

            def p_lo(e, r):
                dve.wait_ge(s["p_hi"], e + 1)
                src = ea[:, e, :] if isinstance(e, int) else ea[:, bass.ds(e, 1), :].rearrange("p a t -> p (a t)")
                V.tensor_tensor(plo[:, r, :], src, phi[:, r, :].bitcast(F32), ALU.subtract).then_inc(s["p_split"], 1)

            def output_step(n, quad=None, h=0):
                e = n + 1 + h * half
                u = W_UP + h * half + n + LEAD
                if quad is not None or n < half - 1:
                    p_lo(e if quad is None else quad * 4 + e, (n + 1) % 2)
                split_lo(dve, None, u % 4, quad + u // 4) if quad is not None else lo_for(u - LEAD)
                if h == 0:
                    if quad is not None or n < half - 1:
                        lay_out(n + 1, quad, 1)
                    if quad is not None or n:
                        apply(n - 1, quad, 1)

            p_lo(0, 0)
            dve.wait_ge(s["gelu"], N_EXP)
            for n in range(4):
                output_step(n)
            with dve.Fori(1, N_EXP // 8 - 1) as i:
                for n in range(4):
                    output_step(n, i)
            for n in range(half - 4, half):
                output_step(n)
            apply(half - 1, None, 1)
            p_lo(half, 0)
            with dve.Fori(0, N_EXP // 8 - 1) as i:
                for n in range(4):
                    output_step(n, i, 1)
            for n in range(half - 4, half):
                output_step(n, None, 1)
            norm_dve(dve, ch, 2)
            norm_dve(dve, ch, 3)

            for u in range(W_PROJ2, W_OUT2):
                lo_for(u)
            dve.wait_ge(s["c2_in"], 16)
            slopes = [2.0 ** (-8.0 * (h + 1) / MH) for h in range(MH)]
            norm_p = lambda h: (pr[:, h % 2, 0:P], pr[:, h % 2, P:3 * P])

            def att_norm(h):
                dve.wait_ge(s["s_exp"], h + 1)
                ch(V.reciprocal(sums[:, h, 2:4], sums[:, h, 0:2]))
                V.tensor_scalar(norm_p(h)[0], norm_p(h)[0], sums[:, h, 2:3], None, ALU.mult)
                V.tensor_scalar(norm_p(h)[1], norm_p(h)[1], sums[:, h, 3:4], None, ALU.mult).then_inc(s["s_norm"], 1)

            def att_evac(h):
                r0 = MD * (h % 2)
                dve.wait_ge(s["ao_ps"], h + 1)
                V.tensor_copy(mix2[r0:r0 + MD, h // 2, :], bank(4 + h % 2, T)[r0:r0 + MD, :]).then_inc(s["ao_sb"], 1)

            for h in range(MH):
                dve.wait_ge(s["s_ps"], h + 1)
                if h >= 2:
                    dve.wait_ge(s["s_exp"], h - 1)
                ch(V.scalar_tensor_tensor(sS[:, h % 2, :], dist, slopes[h] * MD ** 0.5, bank(h % 2, 3 * P),
                                          ALU.mult, ALU.add))
                V.tensor_reduce(out=mx[:, h, 0:1], in_=sS[:, h % 2, 0:P], op=ALU.max, axis=AX.X)
                ch(V.tensor_reduce(out=mx[:, h, 1:2], in_=sS[:, h % 2, P:3 * P], op=ALU.max, axis=AX.X))
                V.tensor_scalar(mx[:, h, 2:4], mx[:, h, 0:2], -(MD ** -0.5), None, ALU.mult).then_inc(s["s_max"], 1)
                if h:
                    att_norm(h - 1)
                if h >= 3:
                    att_evac(h - 3)
            att_norm(MH - 1)
            for h in range(MH - 3, MH):
                att_evac(h)
            for r in range(RH):
                dve.wait_ge(s["rs_ps"], r + 1)
                V.tensor_tensor(rS[:, r, :], bank(r % 2, 3 * P), rdec[:, r, :], ALU.mult).then_inc(s["rs_sb"], 1)
            dve.wait_ge(s["ro_sb"], 1)
            dve.wait_ge(s["rmu"], 1)
            V.scalar_tensor_tensor(ro[:, :, :], bank(2, RH * T).rearrange("p (r t) -> p r t", r=RH), -1.0 / P,
                                   ro[:, :, :], ALU.mult, ALU.add).then_inc(s["rxc"], 1)
            dve.wait_ge(s["r_ss"], 1)
            V.tensor_scalar(rr[:, :, :], bank(4, RH * T).rearrange("p (r t) -> p r t", r=RH), 1.0 / P, 1e-5,
                            ALU.mult, ALU.add).then_inc(s["r_ms"], 1)
            dve.wait_ge(s["r_sqrt"], 1)
            ch(V.reciprocal(rr[:, :, :], rr[:, :, :]))
            ch(V.tensor_tensor(rr[:, :, :], rr[:, :, :], rgs[:, :, :], ALU.mult))
            for r in range(RH):
                m = V.scalar_tensor_tensor(mix2[:, RH + r, :], ro[:, r, :], vcol("ret_norm", r), rr[:, r, :],
                                           ALU.mult, ALU.mult)
            m.then_inc(s["mix_ret"], 1)
            dve.wait_ge(s["mix_ret"], 1)
            operand_dve(dve, 4, mix2)
            for n in range(KT):
                u = W_OUT2 + n
                lo_for(u)
                dve.wait_ge(s["w_used"], u + 1)
                V.tensor_tensor(x[:, n, :], x[:, n, :], bank(n % 2, T), ALU.add).then_inc(s["evac2"], 1)
            norm_dve(dve, ch, 4)
            for f in range(FF):
                u = W_FF + (3 * f - 1 if f else 0)
                v = f % 2
                lo_for(u)
                dve.wait_ge(s["w_used"], u + 1)
                if f >= 2:
                    dve.wait_ge(s["ff_gelu"], f - 1)
                up = bank(v, T)
                ch(V.tensor_scalar(fu[:, v, :], up, vcol("conv2", 2 * FF + f), vcol("conv2_b", f), ALU.mult, ALU.add))
                ch(V.scalar_tensor_tensor(fu[:, v, 1:T], up[:, 0:T - 1], vcol("conv2", FF + f), fu[:, v, 1:T],
                                          ALU.mult, ALU.add))
                V.scalar_tensor_tensor(fu[:, v, 2:T], up[:, 0:T - 2], vcol("conv2", f), fu[:, v, 2:T],
                                       ALU.mult, ALU.add).then_inc(s["ff_conv"], 1)
                lo_for(u + 1)
                dve.wait_ge(s["w_used"], u + 2)
                dve.wait_ge(s["ff_gelu"], f + 1)
                if f >= 2:
                    dve.wait_ge(s["ff_split"], f - 1)
                V.tensor_tensor(pf[:, v, :], fg[:, v, :], bank(2 + v, T), ALU.mult).then_inc(s["ff_mul"], 1)
                if f:
                    dve.wait_ge(s["w_hi"], u + 2 + LEAD + 1)
                dve.wait_ge(s["ff_hi"], f + 1)
                V.tensor_tensor(plo[:, v, :], pf[:, v, :], phi[:, v, :].bitcast(F32), ALU.subtract)\
                 .then_inc(s["ff_split"], 1)
                if f:
                    lo_for(u + 2)
            lo_for(W_PLEG - 1)
            norm_dve(dve, ch, 5)
            dve.wait_ge(s["ple_hi"], 1)
            V.tensor_tensor(ptlo[:, :, :], pt[:, :, :], pthi[:, :, :].bitcast(F32), ALU.subtract).then_inc(s["ple_op"], 1)
            for n in range(KT):
                lo_for(W_PLEG + n)
            for n in range(KT):
                dve.wait_ge(s["ple_gate"], n + 1)
                dve.wait_ge(s["ple_ps"], n + 1)
                ch(V.tensor_tensor(gs[:, n, :], gs[:, n, :], bank(3 + n % 4, T), ALU.mult))
                V.tensor_tensor(x[:, n, :], x[:, n, :], gs[:, n, :], ALU.add).then_inc(s["ple_add"], 1)
            norm_dve(dve, ch, 6)


def columns(w):
    n = w.shape[1] // P
    return np.ascontiguousarray(w.reshape(KT, P, n, P).transpose(2, 1, 0, 3)).reshape(n, P, TW)


def rows_of(w):
    return w.reshape(-1, P, TW)


def interleaved(first, second, third=None):
    last = third if third is not None else second
    head = [first] if third is None else [first, second]
    out = []
    for e in range(len(first) + 1):
        if e < len(first):
            out += [h[e] for h in head]
        if e:
            out.append(last[e - 1])
    return np.stack(out)


def pack(v):
    return np.ascontiguousarray(v.reshape(-1, P).T)


def constants():
    i = np.arange(P)
    blk = lambda l: ((i[:, None] >> (l + 1)) == (i[None, :] >> (l + 1))) & (((i[:, None] >> l) & 1) == 1) \
        & (((i[None, :] >> l) & 1) == 0)
    c1 = [i[:, None] <= i[None, :], i[:, None] > i[None, :], blk(0)] + [blk(l).T for l in range(7)]
    t = np.arange(T)
    inv = [np.broadcast_to(np.float32(1) / np.minimum(t + 1, 2 << g).astype(np.float32), (P, T)) for g in range(PG)]
    c1 = np.concatenate([np.asarray(m, np.float32) for m in c1 + inv + [np.eye(P), np.broadcast_to(i, (P, P))]], axis=1)
    q, k = np.arange(T)[None, :], np.arange(T)[:, None]
    ret = []
    for r in range(RH):
        log_g = np.log(1.0 - 2.0 ** (-5.0 - r))
        d = np.where(q >= k, np.exp(log_g * np.maximum(q - k, 0)), 0.0) * P ** -0.5
        ret += [d[0:P, :], d[P:, P:]]
    dist = np.where(q <= k, (q - k).astype(np.float64), -1e30)
    c2 = np.concatenate(ret + [dist[0:P, 0:P], dist[P:, :]], axis=1).astype(np.float32)
    return c1, c2


def kernel(**a):
    import concourse.bacc as bacc
    from concourse.bass_utils import run_bass_kernel_spmd as run

    a = {k: np.asarray(v) for k, v in a.items()}
    w_in, w_in2 = a["w_in"][0], a["w_in_2"][0]
    c1, c2 = constants()
    m, r = 512, 512
    tiles = [
        columns(w_in[:, 0:4 * 512]), columns(w_in[:, 4 * 512 + 8:]),
        columns(a["w_out"][0]), columns(a["w_query"][0]),
        np.ascontiguousarray(a["expert_down"][0].reshape(N_EXP, P, KT, P).transpose(0, 3, 2, 1)).reshape(N_EXP, P, TW),
        rows_of(a["expert_up"][0]),
        columns(np.concatenate([w_in2[:, 0:2 * m], w_in2[:, 3 * m:3 * m + 2 * r], w_in2[:, 3 * m + 3 * r:]], axis=1)),
        rows_of(np.concatenate([w_in2[:, 2 * m:3 * m], w_in2[:, 3 * m + 2 * r:3 * m + 3 * r]], axis=1)),
        columns(a["w_out_2"][0]),
        interleaved(columns(a["w_up_2"][0]), columns(a["w_gate_2"][0]), rows_of(a["w_down_2"][0])),
        columns(a["w_ple_gate_2"][0]),
        a["w_ple_2"][0].reshape(2, P, 2, 4, P).transpose(2, 1, 3, 0, 4).reshape(2, P, TW),
    ]
    w = np.concatenate(tiles)
    assert w.shape[0] == N_TILES
    w = np.ascontiguousarray(w.reshape(N_TILES // 2, 2, P, TW).transpose(0, 2, 1, 3)).reshape(N_TILES // 2, P, 2 * TW)
    vecs = np.concatenate([
        pack(a["norm_mix_w"][0]), np.concatenate([pack(a["conv_w"][0, j]) for j in range(4)], axis=1),
        pack(a["dn_norm_w"][0]), pack(a["pool_scale"][0]), pack(a["norm_ffn_w"][0]), pack(a["norm_final_w"]), pack(a["attn_norm_2"][0]),
        pack(a["ret_norm_2"][0]), pack(a["ffn_norm_2"][0]),
        np.concatenate([pack(a["conv_w_2"][0, j]) for j in range(3)], axis=1), pack(a["conv_b_2"][0]),
        pack(a["ple_norm_2"][0]), pack(a["final_norm_2"])], axis=1)
    feature_major = lambda t: np.ascontiguousarray(t.T.reshape(-1, P, T).transpose(1, 0, 2))
    arrays = {
        "x_t": feature_major(a["x"][0]), "vecs": np.ascontiguousarray(vecs), "wts": w, "c1": c1,
        "gate_w": np.ascontiguousarray(w_in[:, 4 * 512:4 * 512 + 8].reshape(KT, P, 8).transpose(1, 0, 2)),
        "rows": np.concatenate([a["dt_bias"][0], a["a_log"][0]]),
        "w_pool": np.ascontiguousarray(a["w_pool"][0].transpose(1, 0, 2)),
        "keys": np.ascontiguousarray(a["sub_keys"][0].reshape(2 * NH, P, P).transpose(2, 0, 1)),
        "c2": c2, "ple_t": feature_major(a["p_2"][0, 0]),
    }
    nc = bacc.Bacc("TRN2", target_bir_lowering=False, num_devices=1)
    args = [nc.dram_tensor("in_" + n, v.shape, mybir.dt.from_np(v.dtype), kind="ExternalInput").ap()
            for n, v in arrays.items()]
    args.append(nc.dram_tensor("out_0_dram", (P, KT, T), F32, kind="ExternalOutput").ap())
    program(nc, *args)
    got = run(nc, [{"in_" + n: v for n, v in arrays.items()}], core_ids=[0]).results[0]["out_0_dram"]
    return np.ascontiguousarray(got.transpose(1, 0, 2).reshape(D, T).T).reshape(1, T, D)
```

```python
import concourse.bass as bass
from concourse import mybir
from contextlib import ExitStack
import numpy as np

F32 = mybir.dt.float32
F32R = mybir.dt.float32r
BF16 = mybir.dt.bfloat16
U32 = mybir.dt.uint32
ALU = mybir.AluOpType
ACT = mybir.ActivationFunctionType
AX = mybir.AxisListType

P = 128
T = 256
TB = T // P
D = 1024
KT = D // P
TW = KT * P
DH = 4
NI = TB * DH
PG = 4
NH = 8
TOPK = 16
NEG = -3.0e38
EPS = 1e-6
MH, MD = 8, 64
RH = 4
EVERY_A, EVERY_B = 8, 4
CHOSEN_AT = 60
CV_AT = 48
GT = 4
N_GROUPS = T // GT
FF = 2816 // P
PAD = 16

W_PROJ1 = 0
N_PROJ1 = 20
W_OUT1 = W_PROJ1 + N_PROJ1
W_QUERY = W_OUT1 + KT
N_QUERY = 2 * NH
W_EXP = W_QUERY + N_QUERY
N_EXP = P
W_UP = W_EXP + N_EXP
W_V2 = W_UP + N_EXP
W_QK2 = W_V2 + KT
N_QK2 = 8
W_RET2 = W_QK2 + N_QK2
N_RET2 = 12
W_OUT2 = W_RET2 + N_RET2
W_FF = W_OUT2 + KT
W_PLE = W_FF + 3 * FF
W_PLEG = W_PLE + 2
N_TILES = W_PLEG + KT
RING = 4
LEAD = 3
assert N_TILES % 4 == 0

CV = {}
_c = 0
for _n, _w in (("norm_mix", KT), ("conv", 48), ("dn_norm", 1), ("pool_scale", PG), ("norm_ffn", KT), ("norm_mid", KT),
               ("attn_norm", KT), ("ret_norm", RH), ("ffn_norm", KT), ("conv2", 3 * FF), ("conv2_b", FF),
               ("ple_norm", KT), ("final_norm", KT)):
    CV[_n] = _c
    _c += _w
N_CV = _c

SEMS = """ba_row ba_sb gw_hi gw_lo scale_ok sq_sum key_eq key_mul x_got r_norm rt_ps ident_in norm_r norm_bc qk_rn
qk_bc o_rn o_bc k_used tt_ok attn_ready x_in vec_in c1_in gate_w_in row_in wpool_in keys_in c2_in ple_in
out_done dve_step ones_ready w_hi w_lo w_used raw0 raw1 x_sq ssq norm_ms norm_sqrt norm_h src_hi operand
evac conv_done silu_done qk_sq qk_ss qk_ms qk_sqrt qk_norm ba gate_in gate_sig gate_e gate_l gate_ea
g_ready gb gsub gexp kk qkt kvt kv_ready An_ready AnT AnT_sb amt U U_sb Tp w_ps w_sb kcd_ps kcd_sb s1_ps
s1_sb vn_ps vn_sb o_ps o_sq o_ss o_ms o_sqrt mix_dn pooled pool_ps mix_pool sc_ps scores seeded cv_ready
cv_exp cf_ready topk idxT idxT_sb gate_parts oh_eq oh1 g_ps g_mul gelu p_hi p_split s_ps s_max s_exp
s_norm pt_ps pt_sb ao_ps ao_sb v_sb rs_ps rs_sb ro_ps rxc r_sq r_ms r_sqrt mix_ret evac2 rg_done ff_conv
ff_gelu ff_mul ff_hi ff_split ple_gate ple_hi ple_op ple_add""".split()


def program(nc, x_t, vecs, wts, c1, gate_w, rows, w_pool, keys, c2, ple_t, out):
    ctx = ExitStack()
    with ctx:
        s = {n: ctx.enter_context(nc.semaphore("s_" + n)) for n in SEMS}

        top = [-(-nc.sbuf_base // 32) * 32]
        slab = ctx.enter_context(nc.sbuf_tensor("slab", [P, (nc.sbuf_bytes_remaining - 64) // 4], F32))

        def place(name, shape, dt=F32, at=None):
            size = int(np.prod(shape)) * (2 if dt == BF16 else 4)
            size = -(-size // 32) * 32
            if at is None:
                at, top[0] = top[0], top[0] + size
            else:
                at[0], at = at[0] + size, at[0]
            return nc.alloc_sbuf_tensor_at(name, [P] + list(shape), dt, offset=at)

        raw = place("raw", [2, 2 * TW])
        whi = place("whi", [RING, TW], F32R)
        wlo = place("wlo", [RING, TW], F32R)
        ahi = place("ahi", [KT, T], F32R)
        alo = place("alo", [KT, T], F32R)
        ident = place("ident", [P])
        ones = place("ones", [P])
        vec = place("vec", [N_CV])
        warm = place("warm", [8])
        small = top[0]
        x = place("x", [KT, T])
        pf = place("pf", [2, T])
        aux_end = top[0]
        phi = place("phi", [2, T], F32R)
        plo = place("plo", [2, T], F32R)
        aux = [small]
        kT = place("kT", [2, T], BF16, at=aux)
        gT = place("gT", [3, T], BF16, at=aux)
        iota = place("iota", [P, GT], BF16, at=aux)
        oh2 = place("oh2", [2, P, GT], BF16, at=aux)
        oheq = place("oheq", [2, N_EXP // 2, GT], BF16, at=aux)
        oh1 = place("oh1", [2, 3, N_EXP // 2, GT], BF16, at=aux)
        assert aux[0] <= aux_end
        arena = top[0]
        ea = place("ea", [N_EXP, T])
        end = top[0]
        assert end <= nc.sbuf_usable_end, end

        a = [arena]
        h32 = place("h32", [KT, T], at=a)
        sq = place("sq", [KT, T], at=a)
        rstd = place("rstd", [TB], at=a)
        rms = place("rms", [TB], at=a)
        common = a[0]
        cst = place("cst", [11 * P + PG * T], at=a)
        U1 = cst[:, 0:P]
        CL = cst[:, P:2 * P]
        LM0 = cst[:, 2 * P:3 * P]
        LMT = [cst[:, (3 + l) * P:(4 + l) * P] for l in range(7)]
        invc = cst[:, 10 * P:10 * P + PG * T].rearrange("p (g t) -> p g t", g=PG)
        CU = cst[:, 10 * P + PG * T:]
        gw = place("gw", [KT, 8], at=a)
        row = place("row", [8], at=a)
        wp = place("wp", [PG, P], at=a)
        keep = a[0]
        qraw = place("qraw", [12, T + 3], at=a)
        b = [keep]
        AmT2 = place("AmT2", [NI, P], at=b)
        rn = place("rn", [DH, T], at=b)
        qkv = place("qkv", [12, T], at=a)
        zs = place("zs", [DH, T], at=a)
        pp = place("pp", [PG, PAD + T], at=a)
        pa = place("pa", [PG, PAD + T], at=a)
        pb = place("pb", [PG, PAD + T], at=a)
        I8 = [NI, P]
        gbc = place("gbc", I8, at=a)
        AmT = [AmT2, gbc]
        Dm = place("Dm", I8, at=a)
        Tm = Dm
        DT = place("DT", I8, at=a)
        X = place("X", I8, at=a)
        Us = X
        attnT = DT
        An = place("An", I8, at=a)
        AnT = place("AnT", I8, at=a)
        TT = place("TT", I8, at=a)
        eGb = place("eGb", [DH, P], at=a)
        kbg = place("kbg", [DH, P], at=a)
        kdec = place("kdec", [DH, P], at=a)
        vb = place("vb", I8, at=a)
        Wv = place("Wv", I8, at=a)
        kcdT = place("kcdT", [DH, P], at=a)
        S1 = place("S1", [DH, P], at=a)
        qd = place("qd", [DH, P], at=a)
        gw_hi = place("gw_hi", [KT, 8], F32R, at=a)
        gw_lo = place("gw_lo", [KT, 8], F32R, at=a)
        ba = place("ba", [T], at=a)
        tok = place("tok", [160], at=a)
        assert a[0] <= end, a[0] - end
        col = {}
        c = 0
        for n, w in (("ba", 16), ("beta", 8), ("nbeta", 8), ("t1", 8), ("t2", 8), ("e", 8), ("l", 8), ("ea", 4),
                     ("g", 8), ("gc", 8), ("egc", 4), ("bg", 4), ("kd", 4),
                     ("qk_ms", 16), ("qk_r", 16), ("o_ms", 8), ("o_r", 8)):
            col[n] = tok[:, c:c + w]
            c += w
        a = [common]
        qs = place("qs", [4, T], at=a)
        kk = place("kk", [2 * NH, P], at=a)
        assert a[0] <= arena + 4 * T * N_EXP // 2
        a = [arena + 4 * T * N_EXP // 2]
        b = list(a)
        sc = place("sc", [TB, 2 * NH, P], at=a)
        eq0 = place("eq0", [TB * NH, TOPK, TOPK], at=b)
        eq1 = place("eq1", [TB * NH, TOPK, TOPK], at=b)
        cand = place("cand", [TB * NH, TOPK * TOPK], at=a)
        v16 = place("v16", [TB, 2 * NH, TOPK], at=a)
        i16 = place("i16", [TB, 2 * NH, TOPK], U32, at=a)
        i16f = place("i16f", [TB, 2 * NH, TOPK], at=a)
        cv = place("cv", [TB * NH, TOPK], at=a)
        ci = place("ci", [TB * NH, TOPK], U32, at=a)
        cj = place("cj", [2, TB * NH * TOPK], U32, at=a)
        cf = place("cf", [2, TB * NH * TOPK], at=a)
        gates = place("gates", [3, TB, P], at=a)
        gsum = place("gsum", [2, TB * NH], at=a)
        iota16 = place("iota16", [P], at=a)
        grest = place("grest", [T], at=a)
        assert a[0] <= end
        a = [common]
        qk2 = place("qk2", [16, T], at=a)
        rgs = place("rgs", [RH, T], at=a)
        vv = place("vv", [TB, D], at=a)
        cs2 = place("cs2", [RH * 3 * P + 3 * P], at=a)
        rdec = cs2[:, 0:RH * 3 * P].rearrange("p (r n) -> p r n", r=RH)
        dist = cs2[:, RH * 3 * P:]
        sS = place("sS", [2, 3 * P], at=a)
        pr = place("pr", [2, 3 * P], at=a)
        pT = place("pT", [2, 3 * P], at=a)
        mx = place("mx", [MH, 4], at=a)
        sums = place("sums", [MH, 4], at=a)
        rS = place("rS", [RH, 3 * P], at=a)
        ro = place("ro", [RH * TB, P], at=a)
        rr = place("rr", [RH * TB, P], at=a)
        wm = place("wm", [KT], at=a)
        r_col = place("r_col", [2, TB], at=a)
        r_row = place("r_row", [T], at=a)
        rst = place("rst", [3, RH * TB], at=a)
        mix2 = place("mix2", [KT, T], at=a)
        fu = place("fu", [2, T], at=a)
        fg = place("fg", [2, T], at=a)
        gs = place("gs", [KT, T], at=a)
        pt = place("pt", [2, T], at=a)
        pthi = place("pthi", [2, T], F32R, at=a)
        ptlo = place("ptlo", [2, T], F32R, at=a)
        assert a[0] <= end

        ps = ctx.enter_context(nc.psum_tensor("ps", [P, 8, 512], F32))
        flat = ps[:, :, :].rearrange("p b n -> p (b n)")

        def bank(b0, n, base=0):
            return flat[:, b0 * 512 + base:b0 * 512 + base + n]

        i16s = i16f[:, :, :, :].rearrange("p b (h c) k -> p (b h) c k", c=2)

        def vcol(name, j=0):
            return vec[:, CV[name] + j:CV[name] + j + 1]

        def b3(ap, n):
            return ap.unsqueeze(2).to_broadcast([P, ap.shape[1], n])

        def m3(ap, n):
            return ap.unsqueeze(1).to_broadcast([P, n, ap.shape[1]])

        block = ctx.enter_context(nc.Block())

        def raw_tile(half, k):
            return raw[:, half, k * TW:(k + 1) * TW]

        @block.sync
        def _(sp):
            sp.dma_start(x[:, :, :], x_t).then_inc(s["x_in"], 16)
            sp.dma_start(vec[:, :], vecs).then_inc(s["vec_in"], 16)
            rs = (s["raw0"], s["raw1"])
            for p in range(2):
                sp.dma_start(raw[:, p, :], wts[p]).then_inc(rs[p], 16)
            with sp.Fori(1, N_TILES // 4) as i:
                for p in range(2):
                    sp.wait_ge(s["w_hi"], i * 4 + (2 * p - 2))
                    sp.wait_ge(s["w_lo"], i * 4 + (2 * p - 2))
                    sp.dma_start(raw[:, p, :], wts[bass.ds(i * 2 + p, 1), :, :].rearrange("a p n -> p (a n)"))\
                      .then_inc(rs[p], 16)
            for q in range(4):
                sp.wait_ge(s["norm_h"], 24 + q + 1)
                sp.dma_start(out[:, 2 * q:2 * q + 2, :], h32[:, 2 * q:2 * q + 2, :]).then_inc(s["out_done"], 16)
            sp.wait_ge(s["out_done"], 64)

        @block.gpsimd
        def _(pl):
            pl.dma_start(ident[:, :], c1[:, 11 * P + PG * T:12 * P + PG * T]).then_inc(s["ident_in"], 16)
            pl.dma_start(gw[:, :, :], gate_w).then_inc(s["gate_w_in"], 16)
            pl.dma_start(row[:, :], rows.partition_broadcast(P)).then_inc(s["row_in"], 16)
            pl.dma_start(cst[:, :], c1[:, 0:11 * P + PG * T]).then_inc(s["c1_in"], 16)
            pl.dma_start(wp[:, :, :], w_pool).then_inc(s["wpool_in"], 16)
            pl.wait_ge(s["operand"], 8)
            pl.dma_start(kk[:, :, :], keys).then_inc(s["keys_in"], 16)
            pl.dma_start(iota16[:, :], c1[:, 12 * P + PG * T:13 * P + PG * T]).then_inc(s["keys_in"], 16)
            for half_, e in ((0, eq0), (1, eq1)):
                pl.wait_ge(s["key_eq"], half_ + 1)
                nc.gpsimd.tensor_tensor(e[:, :, :, :], e[:, :, :, :],
                                        i16s[:, :, half_, :].unsqueeze(2).to_broadcast([P, TB * NH, TOPK, TOPK]),
                                        ALU.mult).then_inc(s["key_mul"], 1)
            pl.wait_ge(s["p_split"], N_EXP)
            pl.dma_start(cs2[:, :], c2).then_inc(s["c2_in"], 16)
            pl.dma_start(pt[:, :, :], ple_t).then_inc(s["ple_in"], 16)

        def split_hi(act, u, j, quad=None):
            if quad is None:
                if u >= N_TILES:
                    return
                act.wait_ge((s["raw0"], s["raw1"])[j // 2], 16 * (u // 4 + 1))
                if u >= RING:
                    act.wait_ge(s["w_used"], u - RING + 1)
            else:
                act.wait_ge((s["raw0"], s["raw1"])[j // 2], quad * 16 + 16)
                act.wait_ge(s["w_used"], quad * 4 + (j - RING + 1))
            nc.scalar.activation(whi[:, j, :], raw_tile(j // 2, j % 2), ACT.Copy).then_inc(s["w_hi"], 1)

        def split_lo(dve, u, j, quad=None):
            if quad is None:
                if u >= N_TILES:
                    return
                dve.wait_ge(s["w_hi"], u + 1)
                if u >= RING:
                    dve.wait_ge(s["w_used"], u - RING + 1)
            else:
                dve.wait_ge(s["w_hi"], quad * 4 + (j + 1))
                dve.wait_ge(s["w_used"], quad * 4 + (j - RING + 1))
            nc.vector.tensor_tensor(wlo[:, j, :], raw_tile(j // 2, j % 2), whi[:, j, :].bitcast(F32),
                                    ALU.subtract).then_inc(s["w_lo"], 1)

        def products(out_ap, wh, wl, xh, xl, first, last):
            nc.tensor.matmul(out_ap, wh, xh, start=first, stop=False, skip_group_check=True)
            nc.tensor.matmul(out_ap, wh, xl, start=False, stop=False, skip_group_check=True)
            return nc.tensor.matmul(out_ap, wl, xh, start=False, stop=last, skip_group_check=True)

        def w_k(j, k):
            return whi[:, j, k * P:(k + 1) * P], wlo[:, j, k * P:(k + 1) * P]

        def gemm_tile(pe, j, dst, content=None):
            for n in range(KT):
                if content is not None and n % 2 == 0:
                    pe.wait_ge(s["operand"], 4 * content + n // 2 + 1)
                k = 2 * QUARTERS[n // 2] + n % 2 if content == 1 else n
                m = products(dst, *w_k(j, k), ahi[:, k, :], alo[:, k, :], n == 0, n == KT - 1)
            m.then_inc(s["w_used"], 1)

        class Chain:

            def __init__(self, eng, sem):
                self.eng, self.sem, self.n = eng, sem, 0

            def __call__(self, ins):
                ins.then_inc(self.sem, 1)
                self.n += 1
                self.eng.wait_ge(self.sem, self.n)

        NORM_W = ["norm_mix", "norm_ffn", "norm_mid", "attn_norm", "ffn_norm", "ple_norm", "final_norm"]
        NORM_OP = [0, 2, 3, None, 5, 6, None]
        QUARTERS = (2, 3, 0, 1)
        FROM_PSUM = (2, 4, 5)
        NORM_BANK = [2, 2, 6, 6, 2, 2, 2]
        USED_BEFORE = [0, W_OUT1, W_QUERY, W_V2, W_OUT2, W_FF, W_PLE]

        def x_quarter(i, q):
            return [(s["x_in"], 16), (s["evac"], W_OUT1 + 2 * q + 2), (s["w_used"], W_V2), (s["norm_h"], 12 + q + 1),
                    (s["w_used"], W_FF), (s["w_used"], W_PLE), (s["ple_add"], 2 * q + 2)][i]

        def pair(buf, q):
            return buf[:, 2 * q:2 * q + 2, :]

        def accumulated(q):
            return bank(4 + q, 2 * T).rearrange("p (k t) -> p k t", k=2)

        def squares(act, i, q):
            act.wait_ge(*x_quarter(i, q))
            if i:
                act.wait_ge(s["ssq"], i)
            nc.scalar.activation(pair(sq, q), accumulated(q) if i in FROM_PSUM else pair(x, q), ACT.Square)\
              .then_inc(s["x_sq"], 1)

        def norm_act(act, i, first=0):
            if i == 0:
                act.wait_ge(s["ones_ready"], 1)
            nc.scalar.activation(warm[:, i:i + 1], ones[:, 0:1], ACT.Sqrt)
            for q in range(first, 4):
                squares(act, i, q)
            norm_root(act, i)
            if i == 0:
                split_hi(act, 0, 0)
            if NORM_OP[i] is not None:
                for q in range(4):
                    operand_act(act, NORM_OP[i], h32, q)

        def norm_root(act, i):
            act.wait_ge(s["norm_ms"], i + 1)
            nc.scalar.activation(rstd[:, :], rms[:, :], ACT.Sqrt).then_inc(s["norm_sqrt"], 1)

        def square_add(dve, ch, i, q):
            dve.wait_ge(s["x_sq"], 4 * i + q + 1)
            ch(nc.vector.tensor_tensor(pair(sq, 0), pair(sq, 0), pair(sq, q), ALU.add))
            if q == 3:
                nc.vector.tensor_tensor(sq[:, 0, :], sq[:, 0, :], sq[:, 1, :], ALU.add).then_inc(s["sq_sum"], 1)

        def square_sum(pe, i):
            pe.wait_ge(s["sq_sum"], i + 1)
            for tb in range(TB):
                m = nc.tensor.matmul(bank(NORM_BANK[i], 1, base=tb), sq[:, 0, tb * P:(tb + 1) * P], ones[:, 0:1],
                                     start=True, stop=True)
            m.then_inc(s["ssq"], 1)

        def norm_row(pe, i):
            if i == 0:
                pe.wait_ge(s["ident_in"], 16)
            pe.wait_ge(s["norm_r"], i + 1)
            for tb in range(TB):
                m = along_row(bank(NORM_BANK[i] + 1, P, base=tb * P), rms[:, tb:tb + 1])
            m.then_inc(s["norm_bc"], 1)

        def norm_pe(pe, i):
            if i == 0:
                pe.wait_ge(s["ones_ready"], 1)
            square_sum(pe, i)
            norm_row(pe, i)

        def along_row(dst, col_):
            return nc.tensor.matmul(dst, col_.to_broadcast([P, P]), ident[:, :], start=True, stop=True)

        def norm_dve(dve, ch, i, first=1):
            if i == 0:
                dve.wait_ge(s["x_in"], 16)
                dve.wait_ge(s["vec_in"], 16)
            for q in range(first, 4):
                square_add(dve, ch, i, q)

            def take(*quarters):
                for q in quarters if i in FROM_PSUM else ():
                    nc.vector.tensor_copy(pair(x, q), accumulated(q)).then_inc(s["x_got"], 1)

            take(0, 1)
            if i == 5:
                take(2, 3)
            dve.wait_ge(s["ssq"], i + 1)
            nc.vector.tensor_scalar(rms[:, :], bank(2, TB), 1.0 / D, EPS, ALU.mult, ALU.add).then_inc(s["norm_ms"], 1)
            if i != 5:
                take(2)
            dve.wait_ge(s["norm_sqrt"], i + 1)
            if i == 6:
                dve.wait_ge(s["operand"], 28)
            nc.vector.reciprocal(rms[:, :], rstd[:, :]).then_inc(s["norm_r"], 1)
            if i == 0:
                split_lo(dve, 0, 0)
            if i != 5:
                take(3)
            if i in FROM_PSUM:
                dve.wait_ge(s["x_got"], 4 * (FROM_PSUM.index(i) + 1))
            dve.wait_ge(s["norm_bc"], i + 1)
            for q in range(4):
                for k in (2 * q, 2 * q + 1):
                    m = nc.vector.scalar_tensor_tensor((x if i == 2 else h32)[:, k, :], x[:, k, :],
                                                       vcol(NORM_W[i], k), bank(3, T), ALU.mult, ALU.mult)
                m.then_inc(s["norm_h"], 1)
                if NORM_OP[i] is not None and q:
                    operand_dve(dve, NORM_OP[i], h32, q - 1)
            if NORM_OP[i] is not None:
                operand_dve(dve, NORM_OP[i], h32, 3)

        def operand_act(act, n, src, q):
            if n in NORM_OP:
                act.wait_ge(s["norm_h"], 4 * NORM_OP.index(n) + q + 1)
            if n:
                act.wait_ge(s["w_used"], USED_BEFORE[n])
            nc.scalar.activation(pair(ahi, q), pair(src, q), ACT.Copy).then_inc(s["src_hi"], 1)

        def operand_dve(dve, n, src, q):
            dve.wait_ge(s["src_hi"], 4 * n + q + 1)
            q = QUARTERS[q] if n == 1 else q
            nc.vector.tensor_tensor(pair(alo, q), pair(src, q), pair(ahi, q).bitcast(F32), ALU.subtract)\
              .then_inc(s["operand"], 1)

        def of(buf, c):
            return buf[:, c * DH:(c + 1) * DH, :]

        i4 = lambda b0, n=NI: bank(b0, n * P).rearrange("p (i n) -> p i n", n=P)

        @block.tensor
        def _(pe):
            tm = nc.tensor.matmul
            norm_pe(pe, 0)

            for u in range(N_PROJ1):
                pe.wait_ge(s["w_lo"], u + 1)
                if u >= 2:
                    pe.wait_ge(s["evac"], u - 1)
                gemm_tile(pe, u % RING, bank(u % 2, T), 0 if u == 0 else None)
                if u == 1:
                    pe.wait_ge(s["gw_lo"], 1)
                    for k in range(KT):
                        m = products(bank(3, T, base=T)[0:8, :], gw_hi[:, k, :], gw_lo[:, k, :], ahi[:, k, :],
                                     alo[:, k, :], k == 0, k == KT - 1)
                    m.then_inc(s["ba_row"], 1)
                if u == 2:
                    pe.wait_ge(s["ba_sb"], 1)
                    for n in range(TB):
                        m = nc.tensor.transpose(bank(3, 8, base=8 * n), ba[0:8, n * P:(n + 1) * P], ident[0:8, 0:8])
                    m.then_inc(s["ba"], 1)
                if u == 6:
                    pe.wait_ge(s["c1_in"], 16)
                    pe.wait_ge(s["g_ready"], 1)
                    for n in range(TB):
                        tm(bank(3, DH, base=16 + DH * n), U1, col["g"][:, n * DH:(n + 1) * DH], start=True, stop=True)
                    for i in range(NI):
                        m = tm(i4(6)[:, i, :], gbc[:, i, :], U1, start=True, stop=True)
                    m.then_inc(s["gb"], 1)
                if u in (8, 11):
                    kind = (u - 8) // 3
                    pe.wait_ge(s["qk_sq"], kind + 1)
                    for h in range(DH):
                        for n in range(TB):
                            m = tm(bank(2, 1, base=(kind * DH + h) * TB + n),
                                   sq[:, kind * DH + h, n * P:(n + 1) * P], ones[:, 0:1], start=True, stop=True)
                    m.then_inc(s["qk_ss"], 1)
                if u == 13:
                    pe.wait_ge(s["gexp"], 1)
                    pe.wait_ge(s["qk_rn"], 1)
                    for i in range(2 * NI):
                        m = along_row(bank(4, P, base=i * P), col["qk_r"][:, i:i + 1])
                    m.then_inc(s["qk_bc"], 1)
                if u == 14:
                    pe.wait_ge(s["qk_norm"], 1)
                    for n in range(TB):
                        for h in range(DH):
                            kc = qkv[:, h, n * P:(n + 1) * P]
                            m = tm(i4(4)[:, n * DH + h, :], kc, kc, start=True, stop=True)
                    m.then_inc(s["kk"], 1)
                    for n in range(TB):
                        for h in range(DH):
                            m = nc.tensor.transpose(i4(2)[:, n * DH + h, :], qkv[:, h, n * P:(n + 1) * P], ident[:, :])
                    m.then_inc(s["kvt"], 1)
                if u == 15:
                    pe.wait_ge(s["qk_norm"], 2)
                    for n in range(TB):
                        for h in range(DH):
                            m = tm(i4(6)[:, n * DH + h, :], qkv[:, h, n * P:(n + 1) * P],
                                   qkv[:, DH + h, n * P:(n + 1) * P], start=True, stop=True)
                    m.then_inc(s["qkt"], 1)
                if u == 17:
                    pe.wait_ge(s["An_ready"], 1)
                    for i in range(NI):
                        m = nc.tensor.transpose(i4(4)[:, i, :], An[:, i, :], ident[:, :])
                    m.then_inc(s["AnT"], 1)
                if u == 18:
                    pe.wait_ge(s["attn_ready"], 1)
                    pe.wait_ge(s["silu_done"], 3)
                    for n in range(TB):
                        for h in range(DH):
                            m = nc.tensor.transpose(i4(6)[:, n * DH + h, :], qkv[:, 2 * DH + h, n * P:(n + 1) * P],
                                                    ident[:, :])
                    m.then_inc(s["kvt"], 1)
            pe.wait_ge(s["k_used"], 1)
            for l in range(1, 7):
                for c in range(TB):
                    pe.wait_ge(s["amt"], 2 * l - 1 + c)
                    for i in range(c * DH, (c + 1) * DH):
                        m = tm(i4(2)[:, i, :], AmT[l % 2][:, i, :], Tm[:, i, :], start=True, stop=True)
                    m.then_inc(s["U"], 1)
                for c in range(TB):
                    pe.wait_ge(s["U_sb"], 2 * l - 1 + c)
                    pe.wait_ge(s["tt_ok"], 2 * l - 1 + c)
                    if l == 1:
                        pe.wait_ge(s["kv_ready"], 1)
                    if l < 6:
                        for i in range(c * DH, (c + 1) * DH):
                            m = tm(i4(4)[:, i, :], TT[:, i, :], Us[:, i, :], start=True, stop=True)
                    for i in range(c * DH, (c + 1) * DH):
                        m = tm(i4(6)[:, i, :], Us[:, i, :], TT[:, i, :], start=True, stop=True)
                    m.then_inc(s["Tp"], 1)
            pe.wait_ge(s["tt_ok"], 13)
            for i in range(DH):
                m = tm(i4(2)[:, i, :], TT[:, i, :], vb[:, i, :], start=True, stop=True)
            m.then_inc(s["w_ps"], 1)
            pe.wait_ge(s["tt_ok"], 14)
            for h in range(DH):
                m = tm(i4(4)[:, h, :], kbg[:, h, :], TT[:, DH + h, :], start=True, stop=True)
            m.then_inc(s["kcd_ps"], 1)
            for i in range(DH, NI):
                m = tm(i4(2)[:, i, :], TT[:, i, :], vb[:, i, :], start=True, stop=True)
            m.then_inc(s["w_ps"], 1)
            pe.wait_ge(s["w_sb"], 1)
            for h in range(DH):
                m = tm(i4(5)[:, h, :], kdec[:, h, :], Wv[:, h, :], start=True, stop=True)
            m.then_inc(s["s1_ps"], 1)
            def pooling(*groups):
                for g in groups:
                    m = tm(bank(0, T, base=g * T), wp[:, g, :], pa[:, g, PAD:], start=True, stop=True)
                m.then_inc(s["pool_ps"], 1)

            pe.wait_ge(s["wpool_in"], 16)
            pe.wait_ge(s["pooled"], 1)
            pe.wait_ge(s["evac"], N_PROJ1)
            pooling(0, 1)
            pe.wait_ge(s["kcd_sb"], 1)
            pe.wait_ge(s["s1_sb"], 1)
            for h in range(DH):
                m = tm(i4(4)[:, h, :], kcdT[:, h, :], S1[:, h, :], start=True, stop=True)
            m.then_inc(s["vn_ps"], 1)
            for h in range(DH):
                tm(bank(6, P, base=h * T), Wv[:, h, :], attnT[:, h, :], start=True, stop=True)
            pe.wait_ge(s["vn_sb"], 1)
            for h in range(DH):
                o = bank(6, P, base=h * T + P)
                tm(o, S1[:, h, :], qd[:, h, :], start=True, stop=False)
                tm(o, Wv[:, DH + h, :], attnT[:, DH + h, :], start=False, stop=True).then_inc(s["o_ps"], 1)
            pooling(2, 3)
            pe.wait_ge(s["w_sb"], 2)
            for h in range(DH):
                if h % 2 == 0:
                    pe.wait_ge(s["o_sq"], h // 2 + 1)
                for n in range(TB):
                    m = tm(bank(2, 1, base=h * TB + n), sq[:, h, n * P:(n + 1) * P], ones[:, 0:1],
                           start=True, stop=True)
            m.then_inc(s["o_ss"], 1)
            pe.wait_ge(s["o_rn"], 1)
            for i in range(NI):
                m = along_row(bank(4, P, base=i * P), col["o_r"][:, i:i + 1])
                if i % 4 == 3:
                    m.then_inc(s["o_bc"], 1)

            for n in range(KT):
                pe.wait_ge(s["w_lo"], W_OUT1 + n + 1)
                if n >= 2:
                    pe.wait_ge(s["evac"], W_OUT1 + n - 1)
                gemm_tile(pe, n % RING, bank(n % 2, T), 1 if n == 0 else None)
            def seed(*banks):
                for b0 in banks:
                    m = tm(bank(4 + b0, 512), ident[:, :], x[:, 2 * b0:2 * b0 + 2, :],
                           start=True, stop=False, skip_group_check=True)
                return m

            seed(0, 1)
            square_sum(pe, 1)
            seed(2)
            norm_row(pe, 1)
            seed(3).then_inc(s["seeded"], 1)

            pe.wait_ge(s["keys_in"], 32)

            def scores(slot, key):
                for tb in range(TB):
                    m = tm(bank(2 + slot % 2, P, base=tb * P), qs[:, slot, tb * P:(tb + 1) * P], key,
                           start=True, stop=True)
                m.then_inc(s["sc_ps"], 1)

            for j in range(4):
                pe.wait_ge(s["w_lo"], W_QUERY + j + 1)
                pe.wait_ge(s["evac"], W_QUERY + j - 1)
                gemm_tile(pe, j, bank(j % 2, T), 2 if j == 0 else None)
                if j >= 1:
                    pe.wait_ge(s["evac"], W_QUERY + j)
                    if j >= 3:
                        pe.wait_ge(s["scores"], j - 2)
                    scores(j - 1, kk[:, j - 1, :])
            with pe.Fori(1, N_QUERY // 4) as i:
                for j in range(4):
                    pe.wait_ge(s["w_lo"], i * 4 + (W_QUERY + j + 1))
                    pe.wait_ge(s["evac"], i * 4 + (W_QUERY + j - 1))
                    gemm_tile(pe, j, bank(j % 2, T))
                    pe.wait_ge(s["evac"], i * 4 + (W_QUERY + j))
                    pe.wait_ge(s["scores"], i * 4 + (j - 2))
                    scores((j - 1) % 4, kk[:, bass.ds(i * 4 + (j - 1), 1), :].rearrange("p a n -> p (a n)"))
            pe.wait_ge(s["evac"], W_EXP)
            pe.wait_ge(s["scores"], N_QUERY - 2)
            scores(3, kk[:, N_QUERY - 1, :])

            def hidden(j, r):
                gemm_tile(pe, j, bank(r, T))

            for n in range(4):
                pe.wait_ge(s["w_lo"], W_EXP + n + 1)
                if n >= 2:
                    pe.wait_ge(s["gelu"], n - 1)
                hidden(n, n % 2)
            with pe.Fori(1, CHOSEN_AT // 4) as i:
                for n in range(4):
                    pe.wait_ge(s["w_lo"], i * 4 + (W_EXP + n + 1))
                    pe.wait_ge(s["gelu"], i * 4 + (n - 1))
                    hidden(n, n % 2)
            for n in range(4):
                pe.wait_ge(s["w_lo"], W_EXP + CHOSEN_AT + n + 1)
                pe.wait_ge(s["gelu"], CHOSEN_AT + n - 1)
                hidden(n, n % 2)
                if n == 0:
                    pe.wait_ge(s["topk"], 1)
                    pe.wait_ge(s["scores"], N_QUERY)
                    for q in range(3):
                        for tb in range(TB):
                            m = nc.tensor.transpose(bank(2, P, base=q * T + tb * P), gates[:, q, tb, :], ident[:, :])
                    m.then_inc(s["idxT"], 1)
            half = N_EXP // 2

            def gate_group(j):
                for t in range(GT):
                    for part in range(3):
                        m = tm(bank(2 + j, half, base=t * half), oh2[:, j, :, t], oh1[:, j, part, :, t],
                               start=part == 0, stop=part == 2)
                m.then_inc(s["g_ps"], 1)

            for n in range(4):
                pe.wait_ge(s["w_lo"], W_EXP + half + n + 1)
                pe.wait_ge(s["gelu"], half + n - 1)
                hidden(n, n % 2)
                if n == 1:
                    pe.wait_ge(s["gate_parts"], 1)
                for g in ((), (0, 1), (2,), (3, 4))[n]:
                    pe.wait_ge(s["oh1"], g + 1)
                    if g >= 2:
                        pe.wait_ge(s["g_mul"], g - 1)
                    gate_group(g % 2)
            with pe.Fori(1, N_EXP // 8) as i:
                for n in range(4):
                    pe.wait_ge(s["w_lo"], i * 4 + (W_EXP + half + n + 1))
                    pe.wait_ge(s["gelu"], i * 4 + (half + n - 1))
                    hidden(n, n % 2)
                    pe.wait_ge(s["oh1"], i * 4 + (n + 2))
                    pe.wait_ge(s["g_mul"], i * 4 + n)
                    gate_group((n + 1) % 2)

            def add_outer(j, xh, xl):
                for k in range(KT):
                    m = products(bank(4, T, base=k * T), *w_k(j, k), xh, xl, False, False)
                m.then_inc(s["w_used"], 1)

            with pe.Fori(0, N_EXP // 8 - 1) as i:
                for n in range(4):
                    pe.wait_ge(s["w_lo"], i * 4 + (W_UP + n + 1))
                    pe.wait_ge(s["p_split"], i * 4 + (n + 1))
                    add_outer(n, phi[:, n % 2, :], plo[:, n % 2, :])
                    pe.wait_ge(s["oh1"], i * 4 + (N_GROUPS + n + 2))
                    pe.wait_ge(s["g_mul"], i * 4 + (N_GROUPS + n))
                    gate_group((n + 1) % 2)
            for n in range(half - 4, half):
                pe.wait_ge(s["w_lo"], W_UP + n + 1)
                pe.wait_ge(s["p_split"], n + 1)
                add_outer(n % 4, phi[:, n % 2, :], plo[:, n % 2, :])
                if n < half - 1:
                    pe.wait_ge(s["oh1"], N_GROUPS + n + 2)
                    pe.wait_ge(s["g_mul"], N_GROUPS + n)
                    gate_group((n + 1) % 2)
            with pe.Fori(0, N_EXP // 8) as i:
                for n in range(4):
                    pe.wait_ge(s["w_lo"], i * 4 + (W_UP + half + n + 1))
                    pe.wait_ge(s["p_split"], i * 4 + (half + n + 1))
                    add_outer(n, phi[:, n % 2, :], plo[:, n % 2, :])

            pe.wait_ge(s["gelu"], N_EXP)
            pe.wait_ge(s["g_mul"], 2 * N_GROUPS)
            for k in range(KT):
                u = W_V2 + k
                pe.wait_ge(s["w_lo"], u + 1)
                if k % 2 == 0:
                    pe.wait_ge(s["operand"], 4 * 3 + k // 2 + 1)
                j = u % 4
                for tb in range(TB):
                    for half in range(2):
                        m = products(bank(2 * tb + half, 512), ahi[:, k, tb * P:(tb + 1) * P],
                                     alo[:, k, tb * P:(tb + 1) * P], whi[:, j, half * 512:(half + 1) * 512],
                                     wlo[:, j, half * 512:(half + 1) * 512], k == 0, k == KT - 1)
                m.then_inc(s["w_used"], 1)
                if k == 3:
                    pe.wait_ge(s["x_got"], 4)
                    square_sum(pe, 2)
                if k == 4:
                    norm_row(pe, 2)
            for n in range(N_QK2):
                pe.wait_ge(s["w_lo"], W_QK2 + n + 1)
                if n >= 2:
                    pe.wait_ge(s["evac2"], n - 1)
                gemm_tile(pe, n % RING, bank(4 + n % 2, T))
                if n == 0:
                    square_sum(pe, 3)
                if n == 1:
                    norm_row(pe, 3)

            pe.wait_ge(s["evac2"], N_QK2)
            pe.wait_ge(s["v_sb"], 1)

            def att_scores(h):
                r0, jt = MD * (h % 2), h // 2
                rows_ = slice(r0, r0 + MD)
                if h >= 2:
                    pe.wait_ge(s["s_max"], h - 1)
                tm(bank(2 + h % 2, P), qk2[rows_, jt, 0:P], qk2[rows_, 4 + jt, 0:P], start=True, stop=True)
                tm(bank(2 + h % 2, T, base=P), qk2[rows_, jt, P:T], qk2[rows_, 4 + jt, 0:T], start=True, stop=True)\
                    .then_inc(s["s_ps"], 1)

            def att_transposed(h):
                pe.wait_ge(s["s_norm"], h + 1)
                if h >= 2:
                    pe.wait_ge(s["pt_sb"], h - 1)
                for q in range(3):
                    m = nc.tensor.transpose(bank(4 + h % 2, P, base=q * P), pr[:, h % 2, q * P:(q + 1) * P],
                                            ident[:, :])
                m.then_inc(s["pt_ps"], 1)

            def att_out(h):
                r0, jt = MD * (h % 2), h // 2
                pe.wait_ge(s["pt_sb"], h + 1)
                if h >= 2:
                    pe.wait_ge(s["ao_sb"], h - 1)
                o = bank(6 + h % 2, T)[r0:r0 + MD, :]
                vh = lambda tb: vv[:, tb, h * MD:(h + 1) * MD]
                tm(o[:, 0:P], vh(0), pT[:, h % 2, 0:P], start=True, stop=True)
                tm(o[:, P:T], vh(0), pT[:, h % 2, P:2 * P], start=True, stop=False)
                tm(o[:, P:T], vh(1), pT[:, h % 2, 2 * P:3 * P], start=False, stop=True).then_inc(s["ao_ps"], 1)

            def ret_scores(r):
                pe.wait_ge(s["evac2"], N_QK2 + 8)
                pe.wait_ge(s["s_max"], MH)
                if r >= 2:
                    pe.wait_ge(s["rs_sb"], r - 1)
                tm(bank(2 + r % 2, T), qk2[:, 12 + r, 0:P], qk2[:, 8 + r, 0:T], start=True, stop=True)
                tm(bank(2 + r % 2, P, base=T), qk2[:, 12 + r, P:T], qk2[:, 8 + r, P:T], start=True, stop=True)\
                    .then_inc(s["rs_ps"], 1)

            att_scores(0)
            for n in range(N_RET2):
                if n + 1 < MH:
                    att_scores(n + 1)
                pe.wait_ge(s["w_lo"], W_RET2 + n + 1)
                pe.wait_ge(s["evac2"], N_QK2 + n - 1)
                gemm_tile(pe, n % RING, bank(n % 2, T))
                if n < MH:
                    att_transposed(n)
                if 1 <= n <= MH:
                    att_out(n - 1)
                if n >= MH:
                    ret_scores(n - MH)

            pe.wait_ge(s["evac2"], N_QK2 + N_RET2)
            for r in range(RH):
                pe.wait_ge(s["rs_sb"], r + 1)
                vr = lambda tb: vv[:, tb, 512 + r * P:512 + (r + 1) * P]
                o = lambda tb: bank(0, P, base=(r * TB + tb) * P)
                tm(o(0), rS[:, r, 0:P], vr(0), start=True, stop=True)
                tm(o(1), rS[:, r, P:T], vr(0), start=True, stop=False)
                tm(o(1), rS[:, r, T:T + P], vr(1), start=False, stop=True).then_inc(s["ro_ps"], 1)
            pe.wait_ge(s["ao_sb"], MH)
            pe.wait_ge(s["pt_sb"], MH)
            seed(0, 1, 2, 3)
            for k in range(KT):
                pe.wait_ge(s["w_lo"], W_OUT2 + k + 1)
                pe.wait_ge(s["operand"], 4 * 4 + k // 2 + 1)
                add_outer(k % RING, ahi[:, k, :], alo[:, k, :])
                if k == 0:
                    pe.wait_ge(s["r_norm"], 1)
                    for i in range(RH * TB):
                        m = nc.tensor.transpose(bank(2, P, base=i * P), ro[:, i, :], ident[:, :])
                        if i % 4 == 3:
                            m.then_inc(s["rt_ps"], 1)
            norm_pe(pe, 4)

            for f in range(FF):
                u = W_FF + (3 * f - 1 if f else 0)
                v = f % 2
                for n in range(2):
                    pe.wait_ge(s["w_lo"], u + n + 1)
                    if f >= 2 and n == 0:
                        pe.wait_ge(s["ff_conv"], f - 1)
                    if f >= 2 and n == 1:
                        pe.wait_ge(s["ff_mul"], f - 1)
                    gemm_tile(pe, (u + n) % 4, bank(2 * n + v, T), 5 if f == 0 and n == 0 else None)
                if f:
                    pe.wait_ge(s["w_lo"], u + 3)
                    pe.wait_ge(s["ff_split"], f)
                    add_outer((u + 2) % 4, phi[:, (f - 1) % 2, :], plo[:, (f - 1) % 2, :])
            pe.wait_ge(s["w_lo"], W_PLE)
            pe.wait_ge(s["ff_split"], FF)
            add_outer((W_PLE - 1) % 4, phi[:, (FF - 1) % 2, :], plo[:, (FF - 1) % 2, :])

            def embedding(i):
                pe.wait_ge(s["w_lo"], W_PLE + i + 1)
                for n in range(4):
                    for k in range(2):
                        m = products(bank(4 + 2 * i, T, base=n * T), *w_k((W_PLE + i) % 4, 2 * n + k),
                                     pthi[:, k, :], ptlo[:, k, :], k == 0, k == 1)
                m.then_inc(s["w_used"], 1)

            square_sum(pe, 5)
            pe.wait_ge(s["ple_op"], 1)
            pe.wait_ge(s["x_got"], 12)
            embedding(0)
            norm_row(pe, 5)
            embedding(1)
            for n in range(KT):
                u = W_PLEG + n
                pe.wait_ge(s["w_lo"], u + 1)
                if n >= 2:
                    pe.wait_ge(s["ple_gate"], n - 1)
                gemm_tile(pe, u % 4, bank(n % 2, T), 6 if n == 0 else None)
            norm_pe(pe, 6)

        @block.scalar
        def _(act):
            A = nc.scalar.activation
            norm_act(act, 0)
            for u in range(1, LEAD):
                split_hi(act, u, u % 4)

            def hi_for(u):
                split_hi(act, u + LEAD, (u + LEAD) % 4)

            act.wait_ge(s["gate_w_in"], 16)
            A(gw_hi[:, :, :], gw[:, :, :], ACT.Copy).then_inc(s["gw_hi"], 1)
            for u in range(N_PROJ1):
                hi_for(u)
                act.wait_ge(s["w_used"], u + 1)
                if u < 12:
                    A(qkv[:, u, :], bank(u % 2, T), ACT.Copy, scale=vcol("conv", 3 * 12 + u))
                    A(qraw[:, u, 3:], bank(u % 2, T), ACT.Copy).then_inc(s["evac"], 1)
                elif u < 16:
                    A(zs[:, u - 12, :], bank(u % 2, T), ACT.Silu).then_inc(s["evac"], 1)
                else:
                    A(pp[:, u - 16, PAD:], bank(u % 2, T), ACT.Copy).then_inc(s["evac"], 1)
                if u == 3:
                    act.wait_ge(s["gate_in"], 1)
                    A(col["beta"].rearrange("p (n h) -> p n h", n=TB),
                      col["ba"].rearrange("p (n c) -> p n c", n=TB)[:, :, 0:4], ACT.Sigmoid).then_inc(s["gate_sig"], 1)
                    act.wait_ge(s["gate_in"], 2)
                    A(col["e"], col["t2"], ACT.Exp, scale=-1.0).then_inc(s["gate_e"], 1)
                    act.wait_ge(s["row_in"], 16)
                    A(col["ea"], row[:, 4:8], ACT.Exp).then_inc(s["gate_ea"], 1)
                    act.wait_ge(s["gate_e"], 1)
                    A(col["l"], col["e"], ACT.Ln, bias=1.0).then_inc(s["gate_l"], 1)
                if u in (6, 9):
                    kind = (u - 6) // 3
                    half = qkv[:, kind * DH:(kind + 1) * DH, :]
                    act.wait_ge(s["conv_done"], (kind + 1) * DH)
                    A(half, half, ACT.Silu).then_inc(s["silu_done"], 1)
                    act.wait_ge(s["silu_done"], kind + 1)
                    A(sq[:, kind * DH:(kind + 1) * DH, :], half, ACT.Square).then_inc(s["qk_sq"], 1)
                if u == 8:
                    act.wait_ge(s["gsub"], 1)
                    A(Dm[:, :, :], Dm[:, :, :], ACT.Exp)
                    A(DT[:, :, :], DT[:, :, :], ACT.Exp)
                    A(eGb[:, :, :], i4(6)[:, DH:NI, :], ACT.Exp)
                    A(col["egc"], col["gc"][:, DH:NI], ACT.Exp)
                    A(col["kd"], X[:, 0:DH, P - 1:P].rearrange("p h n -> p (h n)"), ACT.Exp).then_inc(s["gexp"], 1)
                if u == 11:
                    act.wait_ge(s["qk_ms"], 1)
                    A(col["qk_r"], col["qk_ms"], ACT.Sqrt).then_inc(s["qk_sqrt"], 1)
                if u == 13:
                    act.wait_ge(s["conv_done"], 12)
                    A(qkv[:, 2 * DH:, :], qkv[:, 2 * DH:, :], ACT.Silu).then_inc(s["silu_done"], 1)
                if u == 18:
                    act.wait_ge(s["AnT"], 1)
                    A(AnT[:, :, :], i4(4), ACT.Copy).then_inc(s["AnT_sb"], 1)
            for l in range(1, 7):
                for c in range(TB):
                    act.wait_ge(s["U"], 2 * l - 1 + c)
                    A(of(Us, c), of(i4(2), c), ACT.Copy).then_inc(s["U_sb"], 1)
            act.wait_ge(s["w_ps"], 1)
            A(of(Wv, 0), of(i4(2), 0), ACT.Copy).then_inc(s["w_sb"], 1)
            act.wait_ge(s["kcd_ps"], 1)
            A(kcdT[:, :, :], i4(4)[:, 0:DH, :], ACT.Copy).then_inc(s["kcd_sb"], 1)
            act.wait_ge(s["w_ps"], 2)
            A(of(Wv, 1), of(i4(2), 1), ACT.Copy).then_inc(s["w_sb"], 1)
            act.wait_ge(s["s1_ps"], 1)
            A(S1[:, :, :], i4(5)[:, 0:DH, :], ACT.Copy).then_inc(s["s1_sb"], 1)
            A(warm[:, 7:8], ones[:, 0:1], ACT.Sqrt)
            for p in range(2):
                act.wait_ge(s["o_ps"], 2 * p + 2)
                A(sq[:, 2 * p:2 * p + 2, :], bank(6 + p, 2 * T).rearrange("p (h t) -> p h t", h=2), ACT.Square)\
                    .then_inc(s["o_sq"], 1)
            act.wait_ge(s["pool_ps"], 2)
            for g in range(PG):
                m = A(h32[:, DH + g, :], bank(0, T, base=g * T), ACT.Copy, scale=vcol("pool_scale", g))
            m.then_inc(s["mix_pool"], 1)
            act.wait_ge(s["mix_pool"], 1)
            for q in QUARTERS[0:2]:
                operand_act(act, 1, h32, q)
            act.wait_ge(s["o_ms"], 1)
            A(col["o_r"], col["o_ms"], ACT.Sqrt).then_inc(s["o_sqrt"], 1)
            for q in QUARTERS[2:4]:
                act.wait_ge(s["mix_dn"], q + 1)
                operand_act(act, 1, h32, q)
            for n in range(KT):
                hi_for(W_OUT1 + n)
                if n in (2, 4, 6):
                    squares(act, 1, (n - 2) // 2)
            norm_act(act, 1, 3)

            for j in range(4):
                hi_for(W_QUERY + j)
                act.wait_ge(s["w_used"], W_QUERY + j + 1)
                A(qs[:, j, :], bank(j % 2, T), ACT.Copy).then_inc(s["evac"], 1)
                if j:
                    act.wait_ge(s["sc_ps"], j)
                    A(sc[:, :, j - 1, :], bank(2 + (j - 1) % 2, T).rearrange("p (b n) -> p b n", b=TB), ACT.Copy)\
                        .then_inc(s["scores"], 1)
            with act.Fori(1, N_QUERY // 4) as i:
                for j in range(4):
                    split_hi(act, None, (j + LEAD) % 4, i + (W_QUERY // 4 + (1 if j + LEAD >= 4 else 0)))
                    act.wait_ge(s["w_used"], i * 4 + (W_QUERY + j + 1))
                    act.wait_ge(s["sc_ps"], i * 4 + (j - 3))
                    A(qs[:, j, :], bank(j % 2, T), ACT.Copy).then_inc(s["evac"], 1)
                    act.wait_ge(s["sc_ps"], i * 4 + j)
                    A(sc[:, :, bass.ds(i * 4 + (j - 1), 1), :].rearrange("p b a n -> p b (a n)"),
                      bank(2 + (j - 1) % 2, T).rearrange("p (b n) -> p b n", b=TB), ACT.Copy).then_inc(s["scores"], 1)
            act.wait_ge(s["sc_ps"], N_QUERY)
            A(sc[:, :, N_QUERY - 1, :], bank(3, T).rearrange("p (b n) -> p b n", b=TB), ACT.Copy).then_inc(s["scores"], 1)
            half = N_EXP // 2
            row_of = lambda e: ea[:, e, :] if isinstance(e, int) else \
                ea[:, bass.ds(e, 1), :].rearrange("p a t -> p (a t)")

            def gelu(n, quad=None, base=0):
                u = W_EXP + base + n + LEAD
                if quad is None:
                    split_hi(act, u, u % 4)
                    act.wait_ge(s["w_used"], W_EXP + base + n + 1)
                    A(row_of(base + n), bank(n % 2, T), ACT.Gelu).then_inc(s["gelu"], 1)
                else:
                    split_hi(act, None, u % 4, quad + u // 4)
                    act.wait_ge(s["w_used"], quad * 4 + (W_EXP + base + n + 1))
                    A(row_of(quad * 4 + (base + n)), bank(n % 2, T), ACT.Gelu).then_inc(s["gelu"], 1)

            with act.Fori(0, CV_AT // 4) as i:
                for n in range(4):
                    gelu(n, i)
            act.wait_ge(s["cv_ready"], 1)
            A(cv[:, :, :], cv[:, :, :], ACT.Exp).then_inc(s["cv_exp"], 1)
            with act.Fori(CV_AT // 4, CHOSEN_AT // 4) as i:
                for n in range(4):
                    gelu(n, i)
            gelu(0, None, CHOSEN_AT)
            act.wait_ge(s["seeded"], 1)
            act.wait_ge(s["idxT"], 1)
            A(kT[:, :, :], bank(2, 2 * T).rearrange("p (q t) -> p q t", q=2), ACT.Copy)
            A(gT[:, 0, :], bank(3, T), ACT.Copy).then_inc(s["idxT_sb"], 1)
            for n in range(1, 4):
                gelu(n, None, CHOSEN_AT)
            act.wait_ge(s["gate_parts"], 1)
            for n in range(4):
                gelu(n, None, half)
            with act.Fori(1, N_EXP // 8) as i:
                for n in range(4):
                    gelu(n, i, half)

            def p_hi(n, quad=None, base=0):
                u = W_UP + base + n + LEAD
                if quad is None:
                    if base + n >= 2:
                        act.wait_ge(s["w_used"], W_UP + base + n - 1)
                    A(phi[:, n % 2, :], row_of(base + n), ACT.Copy).then_inc(s["p_hi"], 1)
                    split_hi(act, u, u % 4)
                else:
                    act.wait_ge(s["w_used"], quad * 4 + (W_UP + base + n - 1))
                    A(phi[:, n % 2, :], row_of(quad * 4 + (base + n)), ACT.Copy).then_inc(s["p_hi"], 1)
                    split_hi(act, None, u % 4, quad + u // 4)

            act.wait_ge(s["g_mul"], N_GROUPS)
            for n in range(4):
                p_hi(n)
            with act.Fori(1, N_EXP // 8) as i:
                for n in range(4):
                    p_hi(n, i)
            act.wait_ge(s["g_mul"], 2 * N_GROUPS)
            with act.Fori(0, N_EXP // 8) as i:
                for n in range(4):
                    p_hi(n, i, half)
            act.wait_ge(s["p_split"], N_EXP)
            for q in range(4):
                operand_act(act, 3, h32, q)
                squares(act, 2, q)
            hi_for(W_V2)
            A(warm[:, 2:3], ones[:, 0:1], ACT.Sqrt)
            for u in range(W_V2 + 1, W_V2 + 4):
                hi_for(u)
            norm_root(act, 2)
            hi_for(W_V2 + 4)
            for q in range(4):
                squares(act, 3, q)
            for u in range(W_V2 + 5, W_QK2):
                hi_for(u)
            norm_root(act, 3)
            hi_for(W_QK2)
            hi_for(W_QK2 + 1)
            act.wait_ge(s["w_used"], W_QK2)
            act.wait_ge(s["scale_ok"], 1)
            for b0 in range(4):
                m = A(vv[:, b0 // 2, (b0 % 2) * 512:(b0 % 2 + 1) * 512], bank(b0, 512), ACT.Copy,
                      scale=r_col[:, 0, b0 // 2:b0 // 2 + 1])
            m.then_inc(s["v_sb"], 1)
            for u in range(W_QK2 + 2, W_RET2):
                hi_for(u)
            def att_pt(h):
                act.wait_ge(s["pt_ps"], h + 1)
                if h >= 2:
                    act.wait_ge(s["ao_ps"], h - 1)
                A(pT[:, h % 2, :], bank(4 + h % 2, 3 * P), ACT.Copy).then_inc(s["pt_sb"], 1)

            def att_exp(h):
                act.wait_ge(s["s_max"], h + 1)
                if h >= 2:
                    act.wait_ge(s["pt_ps"], h - 1)
                A(pr[:, h % 2, 0:P], sS[:, h % 2, 0:P], ACT.Exp, bias=mx[:, h, 2:3], scale=MD ** -0.5,
                  accum_out=sums[:, h, 0:1])
                A(pr[:, h % 2, P:3 * P], sS[:, h % 2, P:3 * P], ACT.Exp, bias=mx[:, h, 3:4], scale=MD ** -0.5,
                  accum_out=sums[:, h, 1:2]).then_inc(s["s_exp"], 1)

            for n in range(N_RET2):
                u = W_RET2 + n
                hi_for(u)
                if n < MH:
                    att_exp(n)
                if n >= 8:
                    act.wait_ge(s["evac2"], N_QK2 + n + 1)
                    A(rgs[:, n - 8, :], rgs[:, n - 8, :], ACT.Silu).then_inc(s["rg_done"], 1)
                if n < MH:
                    att_pt(n)
            act.wait_ge(s["ao_sb"], MH)
            for q in range(2):
                operand_act(act, 4, mix2, q)
            for i in range(RH * TB):
                act.wait_ge(s["rxc"], i // 4 + 1)
                m = A(rr[:, i, :], ro[:, i, :], ACT.Square, accum_out=rst[:, 1, i:i + 1])
            m.then_inc(s["r_sq"], 1)
            hi_for(W_OUT2)
            act.wait_ge(s["r_ms"], 1)
            A(rst[:, 2, :], rst[:, 1, :], ACT.Sqrt).then_inc(s["r_sqrt"], 1)
            for u in range(W_OUT2 + 1, W_OUT2 + 4):
                hi_for(u)
            for q in range(2):
                act.wait_ge(s["mix_ret"], q + 1)
                operand_act(act, 4, mix2, 2 + q)
            for u in range(W_OUT2 + 4, W_FF):
                hi_for(u)
            norm_act(act, 4)
            for f in range(FF):
                u = W_FF + (3 * f - 1 if f else 0)
                hi_for(u)
                hi_for(u + 1)
                act.wait_ge(s["ff_conv"], f + 1)
                if f >= 2:
                    act.wait_ge(s["ff_mul"], f - 1)
                A(fg[:, f % 2, :], fu[:, f % 2, :], ACT.Gelu_apprx_tanh).then_inc(s["ff_gelu"], 1)
                if f:
                    hi_for(u + 2)
                act.wait_ge(s["ff_mul"], f + 1)
                if f >= 2:
                    act.wait_ge(s["w_used"], W_FF + 3 * (f - 1) + 2)
                A(phi[:, f % 2, :], pf[:, f % 2, :], ACT.Copy).then_inc(s["ff_hi"], 1)
                if f == 2:
                    act.wait_ge(s["ple_in"], 16)
                    A(pthi[:, :, :], pt[:, :, :], ACT.Copy).then_inc(s["ple_hi"], 1)
            hi_for(W_PLE - 1)
            norm_act(act, 5)
            hi_for(W_PLE)
            hi_for(W_PLE + 1)
            for n in range(KT):
                hi_for(W_PLEG + n)
                act.wait_ge(s["w_used"], W_PLEG + n + 1)
                A(gs[:, n, :], bank(n % 2, T), ACT.Sigmoid).then_inc(s["ple_gate"], 1)
                if n in (3, 5, 7):
                    squares(act, 6, (n - 3) // 2)
            norm_act(act, 6, 3)

        @block.vector
        def _(dve):
            V = nc.vector
            ch = Chain(dve, s["dve_step"])
            V.memset(ones[:, :], 1.0).then_inc(s["ones_ready"], 1)
            V.memset(qraw[:, :, 0:3], 0.0)
            ch(V.memset(pp[:, :, 0:PAD], 0.0))
            norm_dve(dve, ch, 0)
            for u in range(1, LEAD):
                split_lo(dve, u, u % 4)

            def lo_for(u):
                split_lo(dve, u + LEAD, (u + LEAD) % 4)

            bv = lambda n: col[n].rearrange("p (n h) -> p n h", n=TB)
            bav = col["ba"].rearrange("p (n c) -> p n c", n=TB)

            dve.wait_ge(s["gw_hi"], 1)
            V.tensor_tensor(gw_lo[:, :, :], gw[:, :, :], gw_hi[:, :, :].bitcast(F32), ALU.subtract).then_inc(s["gw_lo"], 1)
            for n in range(N_PROJ1):
                lo_for(n)
                if n < 12:
                    dve.wait_ge(s["evac"], n + 1)
                    for tap in (2, 1):
                        ch(V.scalar_tensor_tensor(qkv[:, n, :], qraw[:, n, tap:tap + T], vcol("conv", tap * 12 + n),
                                                  qkv[:, n, :], ALU.mult, ALU.add))
                    V.scalar_tensor_tensor(qkv[:, n, :], qraw[:, n, 0:T], vcol("conv", n), qkv[:, n, :],
                                           ALU.mult, ALU.add).then_inc(s["conv_done"], 1)
                if n == 1:
                    dve.wait_ge(s["ba_row"], 1)
                    V.tensor_copy(ba[0:8, :], bank(3, T, base=T)[0:8, :]).then_inc(s["ba_sb"], 1)
                if n == 2:
                    dve.wait_ge(s["ba"], 1)
                    V.tensor_copy(col["ba"], bank(3, 16)).then_inc(s["gate_in"], 1)
                    dve.wait_ge(s["gate_in"], 1)
                    dve.wait_ge(s["row_in"], 16)
                    ch(V.tensor_tensor(bv("t1"), bav[:, :, 4:8], m3(row[:, 0:4], TB), ALU.add))
                    ch(V.tensor_scalar(col["t2"], col["t1"], -1.0, None, ALU.mult))
                    V.tensor_tensor(col["t2"], col["t1"], col["t2"], ALU.max).then_inc(s["gate_in"], 1)
                if n == 4:
                    dve.wait_ge(s["gate_l"], 1)
                    dve.wait_ge(s["gate_ea"], 1)
                    ch(V.scalar_tensor_tensor(col["l"], col["t1"], 0.0, col["l"], ALU.max, ALU.add))
                    ch(V.scalar_tensor_tensor(bv("g"), bv("l"), -1.0, m3(col["ea"], TB), ALU.mult, ALU.mult))
                    V.tensor_copy(gbc[:, :, :], b3(col["g"], P)).then_inc(s["g_ready"], 1)
                    dve.wait_ge(s["gate_sig"], 1)
                    ch(V.tensor_scalar(col["nbeta"], col["beta"], -1.0, None, ALU.mult))
                if n == 7:
                    dve.wait_ge(s["gb"], 1)
                    ch(V.tensor_copy(col["gc"], bank(3, NI, base=16)))
                    ch(V.tensor_tensor(X[:, :, :], i4(6), b3(col["gc"], P), ALU.subtract))
                    V.tensor_tensor(DT[:, :, :], X[:, :, :], m3(CU, NI), ALU.min)
                    V.scalar_tensor_tensor(Dm[:, :, :], X[:, :, :], -1.0, m3(CL, NI), ALU.mult, ALU.min)\
                     .then_inc(s["gsub"], 1)
                if n == 11:
                    dve.wait_ge(s["qk_ss"], 2)
                    V.tensor_scalar(col["qk_ms"][:, 0:NI], bank(2, NI), EPS, None, ALU.add)
                    V.tensor_scalar(col["qk_ms"][:, NI:], bank(2, NI, base=NI), EPS, float(P), ALU.add, ALU.mult)\
                     .then_inc(s["qk_ms"], 1)
                if n == 12:
                    dve.wait_ge(s["qk_sqrt"], 1)
                    V.reciprocal(col["qk_r"], col["qk_r"]).then_inc(s["qk_rn"], 1)
                if n == 14:
                    dve.wait_ge(s["qk_bc"], 1)
                    for b0 in (0, DH):
                        V.tensor_tensor(qkv[:, b0:b0 + DH, :], qkv[:, b0:b0 + DH, :],
                                        bank(4, DH * T, base=b0 * T).rearrange("p (h t) -> p h t", h=DH), ALU.mult)\
                         .then_inc(s["qk_norm"], 1)
                if n == 15:
                    dve.wait_ge(s["gexp"], 1)
                    dve.wait_ge(s["qk_norm"], 2)
                    V.tensor_tensor(qd[:, :, :], qkv[:, DH:2 * DH, P:T], eGb[:, :, :], ALU.mult)
                    ch(V.tensor_tensor(col["bg"], col["beta"][:, DH:NI], col["egc"], ALU.mult))
                    dve.wait_ge(s["kk"], 1)
                    for i in range(NI):
                        m = V.scalar_tensor_tensor(An[:, i, :], i4(4)[:, i, :], col["nbeta"][:, i:i + 1], Dm[:, i, :],
                                                   ALU.mult, ALU.mult)
                    m.then_inc(s["An_ready"], 1)
                if n == 16:
                    dve.wait_ge(s["qkt"], 1)
                    V.tensor_tensor(attnT[:, :, :], i4(6), DT[:, :, :], ALU.mult).then_inc(s["attn_ready"], 1)
                    dve.wait_ge(s["An_ready"], 1)
                    ch(V.tensor_tensor(Tm[:, :, :], An[:, :, :], m3(LM0, NI), ALU.mult))
                    V.tensor_tensor(Tm[:, :, :], Tm[:, :, :], m3(ident[:, :], NI), ALU.add)
                if n == 17:
                    dve.wait_ge(s["kvt"], 1)
                    V.tensor_tensor(kdec[:, :, :], i4(2)[:, 0:DH, :], b3(col["kd"], P), ALU.mult)
                    V.tensor_tensor(kbg[:, :, :], i4(2)[:, DH:NI, :], b3(col["bg"], P), ALU.mult).then_inc(s["k_used"], 1)
                if n == 19:
                    dve.wait_ge(s["AnT_sb"], 1)
                    V.tensor_tensor(AmT[1][:, :, :], AnT[:, :, :], m3(LMT[1], NI), ALU.mult).then_inc(s["amt"], 2)
                    ch(V.tensor_tensor(TT[:, :, :], AnT[:, :, :], m3(LMT[0], NI), ALU.mult))
                    V.tensor_tensor(TT[:, :, :], TT[:, :, :], m3(ident[:, :], NI), ALU.add).then_inc(s["tt_ok"], 2)
                    dve.wait_ge(s["kvt"], 2)
                    V.tensor_tensor(vb[:, :, :], i4(6), b3(col["beta"], P), ALU.mult).then_inc(s["kv_ready"], 1)
                    dve.wait_ge(s["conv_done"], 12)
                    ch(V.tensor_tensor(AmT[0][:, :, :], AnT[:, :, :], m3(LMT[2], NI), ALU.mult))

            N = PAD + T
            dve.wait_ge(s["evac"], N_PROJ1)
            for l in range(1, 7):
                for c in range(TB):
                    dve.wait_ge(s["Tp"], 2 * l - 1 + c)
                    if l < 6:
                        V.tensor_tensor(of(Tm, c), of(Tm, c), of(i4(4), c), ALU.add).then_inc(s["amt"], 1)
                    V.tensor_tensor(of(TT, c), of(TT, c), of(i4(6), c), ALU.add).then_inc(s["tt_ok"], 1)
                    if l < 5:
                        ch(V.tensor_tensor(of(AmT[l % 2], c), of(AnT, c), m3(LMT[l + 2], DH), ALU.mult))
                if l == 1:
                    ch(V.tensor_tensor(pa[:, :, 1:N], pp[:, :, 1:N], pp[:, :, 0:N - 1], ALU.add))
                if l == 2:
                    ch(V.tensor_tensor(pb[:, 1:, 3:N], pa[:, 1:, 3:N], pa[:, 1:, 1:N - 2], ALU.add))
                if l == 3:
                    ch(V.tensor_tensor(pa[:, 2:, 7:N], pb[:, 2:, 7:N], pb[:, 2:, 3:N - 4], ALU.add))
                if l == 4:
                    ch(V.tensor_tensor(pb[:, 3, 15:N], pa[:, 3, 15:N], pa[:, 3, 7:N - 8], ALU.add))
                    for g in range(PG):
                        m = V.tensor_tensor(pa[:, g, PAD:], (pa, pb)[g % 2][:, g, PAD:], invc[:, g, :], ALU.mult)
                    ch(m)
                if l == 5:
                    V.tensor_tensor(pa[:, :, PAD:], pa[:, :, PAD:], pp[:, :, PAD:], ALU.subtract).then_inc(s["pooled"], 1)
            dve.wait_ge(s["vn_ps"], 1)
            dve.wait_ge(s["w_sb"], 2)
            V.tensor_tensor(of(Wv, 1), of(Wv, 1), i4(4)[:, 0:DH, :], ALU.subtract).then_inc(s["vn_sb"], 1)
            for q in range(2):
                operand_dve(dve, 1, h32, q)
            dve.wait_ge(s["o_ss"], 1)
            V.tensor_scalar(col["o_ms"], bank(2, NI), 1.0 / P, EPS, ALU.mult, ALU.add).then_inc(s["o_ms"], 1)
            dve.wait_ge(s["o_sqrt"], 1)
            V.reciprocal(col["o_r"], col["o_r"]).then_inc(s["o_rn"], 1)
            for p in range(2):
                two = lambda b0: bank(b0 + p, 2 * T).rearrange("p (h t) -> p h t", h=2)
                dve.wait_ge(s["o_bc"], p + 1)
                ch(V.tensor_tensor(pair(rn, p), two(4), pair(zs, p), ALU.mult))
                V.scalar_tensor_tensor(pair(h32, p), two(6), vcol("dn_norm"), pair(rn, p), ALU.mult, ALU.mult)\
                 .then_inc(s["mix_dn"], 1)
            for q in range(2):
                dve.wait_ge(s["mix_dn"], q + 1)
                operand_dve(dve, 1, h32, q + 2)
            for n in range(KT):
                u = W_OUT1 + n
                lo_for(u)
                dve.wait_ge(s["w_used"], u + 1)
                V.tensor_tensor(x[:, n, :], x[:, n, :], bank(n % 2, T), ALU.add).then_inc(s["evac"], 1)
                if n in (4, 6):
                    square_add(dve, ch, 1, n // 2 - 1)
            norm_dve(dve, ch, 1, 3)
            for u in range(W_QUERY, W_EXP):
                lo_for(u)
            half = N_EXP // 2
            at = [0]

            def next_tile(n=1):
                for _ in range(n):
                    if at[0] < half:
                        lo_for(W_EXP + at[0])
                        at[0] += 1

            dve.wait_ge(s["scores"], N_QUERY)
            sets = [(tb, m) for tb in range(TB) for m in range(2 * NH)]

            def top16(vals, idx, data, keys_, every):
                def each(one):
                    for n, k in enumerate(keys_):
                        m = one(k)
                        if n % every == every - 1:
                            ch(m)
                            next_tile()
                    ch(m) if len(keys_) % every else None

                each(lambda k: V.max(out=vals(k)[:, 0:8], in_=data(k)))
                each(lambda k: V.max_index(out=idx(k)[:, 0:8], in_max=vals(k)[:, 0:8], in_values=data(k)))
                each(lambda k: V.match_replace(out=data(k), in_to_replace=vals(k)[:, 0:8], in_values=data(k),
                                               imm_value=NEG))
                each(lambda k: V.max(out=vals(k)[:, 8:16], in_=data(k)))
                each(lambda k: V.max_index(out=idx(k)[:, 8:16], in_max=vals(k)[:, 8:16], in_values=data(k)))

            top16(lambda k: v16[:, k[0], k[1], :], lambda k: i16[:, k[0], k[1], :], lambda k: sc[:, k[0], k[1], :],
                  sets, EVERY_A)
            V.tensor_copy(i16f[:, :, :, :], i16[:, :, :, :])
            v16s = v16[:, :, :, :].rearrange("p b (h c) k -> p (b h) c k", c=2)
            for k in range(TB * NH):
                m = V.tensor_tensor(cand[:, k, :].rearrange("p (a b) -> p a b", b=TOPK),
                                    b3(v16s[:, k, 0, :], TOPK), m3(v16s[:, k, 1, :], TOPK), ALU.add)
                if k % EVERY_B == EVERY_B - 1:
                    next_tile()
            ch(m)
            top16(lambda k: cv[:, k, :], lambda k: ci[:, k, :], lambda k: cand[:, k, :], range(TB * NH), EVERY_B)
            ch(V.tensor_copy(gsum[:, 0, :], cv[:, :, 0]))
            V.tensor_tensor(cv[:, :, :], cv[:, :, :], b3(gsum[:, 0, :], TOPK), ALU.subtract).then_inc(s["cv_ready"], 1)
            civ = ci[:, :, :].rearrange("p g k -> p (g k)")
            V.tensor_scalar(cj[:, 0, :], civ, 4, None, ALU.logical_shift_right)
            ch(V.tensor_scalar(cj[:, 1, :], civ, 15, None, ALU.bitwise_and))
            V.tensor_copy(cf[:, :, :], cj[:, :, :]).then_inc(s["cf_ready"], 1)
            dve.wait_ge(s["keys_in"], 32)
            dve.wait_ge(s["cf_ready"], 1)
            eqf = lambda e: e[:, :, :, :].rearrange("p g k j -> p (g k) j")
            next_tile()
            nh = TB * NH * TOPK // 2
            for half_, e in ((0, eq0), (1, eq1)):
                for c in range(2):
                    m = V.tensor_tensor(eqf(e)[:, c * nh:(c + 1) * nh, :], b3(cf[:, half_, c * nh:(c + 1) * nh], TOPK),
                                        m3(iota16[:, 0:TOPK], nh), ALU.is_equal)
                    if c == 0:
                        next_tile()
                m.then_inc(s["key_eq"], 1)
                next_tile()
            dve.wait_ge(s["cv_exp"], 1)
            ch(V.tensor_reduce(out=gsum[:, 0, :], in_=cv[:, :, :], op=ALU.add, axis=AX.X))
            ch(V.reciprocal(gsum[:, 1, :], gsum[:, 0, :]))
            V.tensor_tensor(gates[:, 2, :, :].rearrange("p b (g k) -> p (b g) k", k=TOPK), cv[:, :, :],
                            b3(gsum[:, 1, :], TOPK), ALU.mult)
            for half_, e in ((0, eq0), (1, eq1)):
                next_tile(2)
                dve.wait_ge(s["key_mul"], half_ + 1)
                m = V.tensor_reduce(out=gates[:, half_, :, :].rearrange("p b n -> p (b n)"), in_=eqf(e), op=ALU.add,
                                    axis=AX.X)
            m.then_inc(s["topk"], 1)
            assert at[0] < CHOSEN_AT
            next_tile(CHOSEN_AT + 1 - at[0])

            def one_hots(t, j, h):
                v = [a_[:, q, bass.ds(t, GT)] if not isinstance(t, int) else a_[:, q, t:t + GT]
                     for a_, q in ((kT, 0), (kT, 1))]
                V.tensor_tensor(oh2[:, j, :, :], iota[:, :, :], m3(v[1], P), ALU.is_equal)
                V.tensor_tensor(oheq[:, j, :, :], iota[:, h * half:(h + 1) * half, :], m3(v[0], half),
                                ALU.is_equal).then_inc(s["oh_eq"], 1)

            def first_keys_gated(g, t, j):
                dve.wait_ge(s["oh_eq"], g + 1)
                v = gT[:, :, t:t + GT] if isinstance(t, int) else gT[:, :, bass.ds(t, GT)]
                V.tensor_tensor(oh1[:, j, :, :, :], oheq[:, j, :, :].unsqueeze(1).to_broadcast([P, 3, half, GT]),
                                v.unsqueeze(2).to_broadcast([P, 3, half, GT]), ALU.mult).then_inc(s["oh1"], 1)

            def apply_gates(g, t, j, h):
                dve.wait_ge(s["g_ps"], g + 1)
                v = ea[:, h * half:(h + 1) * half, :].rearrange("p e t -> p t e")
                v = v[:, t:t + GT, :] if isinstance(t, int) else v[:, bass.ds(t, GT), :]
                V.tensor_tensor(v, v, bank(2 + j, GT * half).rearrange("p (t e) -> p t e", t=GT), ALU.mult)\
                 .then_inc(s["g_mul"], 1)

            def lay_out(n, quad, h):
                g = n + h * N_GROUPS
                t = n * GT
                if quad is not None:
                    g, t = quad * 4 + g, quad * (4 * GT) + t
                if quad is not None or g >= 2:
                    dve.wait_ge(s["g_ps"], g - 1)
                one_hots(t, n % 2, h)
                first_keys_gated(g, t, n % 2)

            def apply(n, quad, h):
                g = n + h * N_GROUPS
                t = n * GT
                if quad is not None:
                    g, t = quad * 4 + g, quad * (4 * GT) + t
                apply_gates(g, t, n % 2, h)

            dve.wait_ge(s["idxT_sb"], 1)
            ch(V.tensor_tensor(grest[:, :], bank(3, T), gT[:, 0, :], ALU.subtract))
            ch(V.tensor_copy(gT[:, 1, :], grest[:, :]))
            ch(V.tensor_tensor(gT[:, 2, :], grest[:, :], gT[:, 1, :], ALU.subtract))
            V.tensor_copy(iota[:, :, :], b3(iota16[:, :], GT)).then_inc(s["gate_parts"], 1)
            dve.wait_ge(s["gate_parts"], 1)
            next_tile()
            lay_out(0, None, 0)
            next_tile(half)
            assert at[0] == half
            lay_out(1, None, 0)

            def hidden_step(n, quad=None):
                u = W_EXP + half + n + LEAD
                split_lo(dve, None, u % 4, quad + u // 4) if quad is not None else lo_for(u - LEAD)
                lay_out(n + 2, quad, 0) if n < half - 2 else lay_out(n + 2 - half, None, 1)
                apply(n, quad, 0)

            dve.wait_ge(s["gelu"], half)
            for n in range(4):
                hidden_step(n)
            with dve.Fori(1, N_EXP // 8 - 1) as i:
                for n in range(4):
                    hidden_step(n, i)
            for n in range(half - 4, half):
                hidden_step(n)

            def p_lo(e, r):
                dve.wait_ge(s["p_hi"], e + 1)
                src = ea[:, e, :] if isinstance(e, int) else ea[:, bass.ds(e, 1), :].rearrange("p a t -> p (a t)")
                V.tensor_tensor(plo[:, r, :], src, phi[:, r, :].bitcast(F32), ALU.subtract).then_inc(s["p_split"], 1)

            def output_step(n, quad=None, h=0):
                e = n + 1 + h * half
                u = W_UP + h * half + n + LEAD
                if quad is not None or n < half - 1:
                    p_lo(e if quad is None else quad * 4 + e, (n + 1) % 2)
                split_lo(dve, None, u % 4, quad + u // 4) if quad is not None else lo_for(u - LEAD)
                if h == 0:
                    if quad is not None or n < half - 2:
                        lay_out(n + 2, quad, 1)
                    apply(n, quad, 1)

            p_lo(0, 0)
            dve.wait_ge(s["gelu"], N_EXP)
            for n in range(4):
                output_step(n)
            with dve.Fori(1, N_EXP // 8 - 1) as i:
                for n in range(4):
                    output_step(n, i)
            for n in range(half - 4, half):
                output_step(n)
            p_lo(half, 0)
            with dve.Fori(0, N_EXP // 8 - 1) as i:
                for n in range(4):
                    output_step(n, i, 1)
            for n in range(half - 4, half):
                output_step(n, None, 1)

            dve.wait_ge(s["w_used"], W_V2)
            dve.wait_ge(s["g_mul"], 2 * N_GROUPS)
            ch(V.tensor_tensor(wm[:, :], vec[:, CV["norm_mid"]:CV["norm_mid"] + KT],
                               vec[:, CV["attn_norm"]:CV["attn_norm"] + KT], ALU.mult))
            for q in range(4):
                for k in (2 * q, 2 * q + 1):
                    m = V.tensor_scalar(h32[:, k, :], bank(4, T, base=k * T), wm[:, k:k + 1], None, ALU.mult)
                m.then_inc(s["norm_h"], 1)
                if q:
                    operand_dve(dve, 3, h32, q - 1)
            operand_dve(dve, 3, h32, 3)
            lo_for(W_V2)
            for q in range(1, 4):
                square_add(dve, ch, 2, q)
            for q in range(4):
                V.tensor_copy(pair(x, q), accumulated(q)).then_inc(s["x_got"], 1)
            for u in range(W_V2 + 1, W_V2 + 4):
                lo_for(u)

            def norm_inverse(i):
                dve.wait_ge(s["ssq"], i + 1)
                V.tensor_scalar(rms[:, :], bank(6, TB), 1.0 / D, EPS, ALU.mult, ALU.add).then_inc(s["norm_ms"], 1)
                dve.wait_ge(s["norm_sqrt"], i + 1)
                V.reciprocal(rms[:, :], rstd[:, :]).then_inc(s["norm_r"], 1)
                dve.wait_ge(s["norm_r"], i + 1)
                ch(V.tensor_copy(r_col[:, i - 2, :], rms[:, :]))

            norm_inverse(2)
            lo_for(W_V2 + 4)
            dve.wait_ge(s["norm_bc"], 3)
            dve.wait_ge(s["x_got"], 4)
            ch(V.tensor_copy(r_row[:, :], bank(7, T)))
            for q in range(4):
                for k in (2 * q, 2 * q + 1):
                    m = V.scalar_tensor_tensor(x[:, k, :], x[:, k, :], vcol("norm_mid", k), r_row[:, :],
                                               ALU.mult, ALU.mult)
                m.then_inc(s["norm_h"], 1)
            for q in range(1, 4):
                square_add(dve, ch, 3, q)
            for u in range(W_V2 + 5, W_QK2):
                lo_for(u)
            norm_inverse(3)
            ch(V.tensor_tensor(r_col[:, 0, :], r_col[:, 0, :], r_col[:, 1, :], ALU.mult))
            dve.wait_ge(s["norm_bc"], 4)
            V.tensor_tensor(r_row[:, :], r_row[:, :], bank(7, T), ALU.mult).then_inc(s["scale_ok"], 1)
            dve.wait_ge(s["scale_ok"], 1)

            def scaled(u, b0, dst):
                dve.wait_ge(s["w_used"], u + 1)
                V.tensor_tensor(dst, bank(b0, T), r_row[:, :], ALU.mult).then_inc(s["evac2"], 1)

            for n in range(N_QK2):
                lo_for(W_QK2 + n)
                scaled(W_QK2 + n, 4 + n % 2, qk2[:, n, :])
            dve.wait_ge(s["c2_in"], 16)
            slopes = [2.0 ** (-8.0 * (h + 1) / MH) for h in range(MH)]
            norm_p = lambda h: (pr[:, h % 2, 0:P], pr[:, h % 2, P:3 * P])

            def att_norm(h):
                dve.wait_ge(s["s_exp"], h + 1)
                ch(V.reciprocal(sums[:, h, 2:4], sums[:, h, 0:2]))
                V.tensor_scalar(norm_p(h)[0], norm_p(h)[0], sums[:, h, 2:3], None, ALU.mult)
                V.tensor_scalar(norm_p(h)[1], norm_p(h)[1], sums[:, h, 3:4], None, ALU.mult).then_inc(s["s_norm"], 1)

            def att_evac(h):
                r0 = MD * (h % 2)
                dve.wait_ge(s["ao_ps"], h + 1)
                V.tensor_copy(mix2[r0:r0 + MD, h // 2, :], bank(6 + h % 2, T)[r0:r0 + MD, :]).then_inc(s["ao_sb"], 1)

            def att_bias(h):
                dve.wait_ge(s["s_ps"], h + 1)
                if h >= 2:
                    dve.wait_ge(s["s_exp"], h - 1)
                ch(V.scalar_tensor_tensor(sS[:, h % 2, :], dist, slopes[h] * MD ** 0.5, bank(2 + h % 2, 3 * P),
                                          ALU.mult, ALU.add))
                V.tensor_reduce(out=mx[:, h, 0:1], in_=sS[:, h % 2, 0:P], op=ALU.max, axis=AX.X)
                ch(V.tensor_reduce(out=mx[:, h, 1:2], in_=sS[:, h % 2, P:3 * P], op=ALU.max, axis=AX.X))
                V.tensor_scalar(mx[:, h, 2:4], mx[:, h, 0:2], -(MD ** -0.5), None, ALU.mult).then_inc(s["s_max"], 1)

            def ret_decay(r):
                dve.wait_ge(s["rs_ps"], r + 1)
                V.tensor_tensor(rS[:, r, :], bank(2 + r % 2, 3 * P), rdec[:, r, :], ALU.mult).then_inc(s["rs_sb"], 1)

            att_bias(0)
            for n in range(N_RET2):
                if n + 1 < MH:
                    att_bias(n + 1)
                lo_for(W_RET2 + n)
                if n < MH:
                    att_norm(n)
                scaled(W_RET2 + n, n % 2, qk2[:, 8 + n, :] if n < 8 else rgs[:, n - 8, :])
                if 2 <= n < MH + 2:
                    att_evac(n - 2)
                if n > MH:
                    ret_decay(n - MH - 1)
            ret_decay(RH - 1)
            for p in range(2):
                of4 = lambda buf: buf[:, 4 * p:4 * p + 4, :]
                dve.wait_ge(s["ro_ps"], 2 * p + 2)
                o = bank(p, 512).rearrange("p (i n) -> p i n", n=P)
                ch(V.tensor_reduce(out=rst[:, 0, 4 * p:4 * p + 4], in_=o, op=ALU.add, axis=AX.X))
                ch(V.tensor_scalar(rst[:, 0, 4 * p:4 * p + 4], rst[:, 0, 4 * p:4 * p + 4], 1.0 / P, None, ALU.mult))
                V.tensor_tensor(of4(ro), o, b3(rst[:, 0, 4 * p:4 * p + 4], P), ALU.subtract).then_inc(s["rxc"], 1)
            for q in range(2):
                operand_dve(dve, 4, mix2, q)
            dve.wait_ge(s["r_sq"], 1)
            V.tensor_scalar(rst[:, 1, :], rst[:, 1, :], 1.0 / P, 1e-5, ALU.mult, ALU.add).then_inc(s["r_ms"], 1)
            lo_for(W_OUT2)
            dve.wait_ge(s["r_sqrt"], 1)
            ch(V.reciprocal(rst[:, 2, :], rst[:, 2, :]))
            V.tensor_tensor(ro[:, :, :], ro[:, :, :], b3(rst[:, 2, :], P), ALU.mult).then_inc(s["r_norm"], 1)
            for r in range(RH):
                dve.wait_ge(s["rt_ps"], r // 2 + 1)
                dve.wait_ge(s["rg_done"], r + 1)
                m = V.scalar_tensor_tensor(mix2[:, RH + r, :], bank(2, T, base=r * T), vcol("ret_norm", r),
                                           rgs[:, r, :], ALU.mult, ALU.mult)
                if r % 2:
                    m.then_inc(s["mix_ret"], 1)
            lo_for(W_OUT2 + 1)
            for q in range(2, 4):
                operand_dve(dve, 4, mix2, q)
            for u in range(W_OUT2 + 2, W_FF):
                lo_for(u)
            norm_dve(dve, ch, 4)
            for f in range(FF):
                u = W_FF + (3 * f - 1 if f else 0)
                v = f % 2
                lo_for(u)
                dve.wait_ge(s["w_used"], u + 1)
                if f >= 2:
                    dve.wait_ge(s["ff_gelu"], f - 1)
                up = bank(v, T)
                ch(V.tensor_scalar(fu[:, v, :], up, vcol("conv2", 2 * FF + f), vcol("conv2_b", f), ALU.mult, ALU.add))
                ch(V.scalar_tensor_tensor(fu[:, v, 1:T], up[:, 0:T - 1], vcol("conv2", FF + f), fu[:, v, 1:T],
                                          ALU.mult, ALU.add))
                V.scalar_tensor_tensor(fu[:, v, 2:T], up[:, 0:T - 2], vcol("conv2", f), fu[:, v, 2:T],
                                       ALU.mult, ALU.add).then_inc(s["ff_conv"], 1)
                lo_for(u + 1)
                dve.wait_ge(s["w_used"], u + 2)
                dve.wait_ge(s["ff_gelu"], f + 1)
                if f >= 2:
                    dve.wait_ge(s["ff_split"], f - 1)
                V.tensor_tensor(pf[:, v, :], fg[:, v, :], bank(2 + v, T), ALU.mult).then_inc(s["ff_mul"], 1)
                if f:
                    lo_for(u + 2)
                dve.wait_ge(s["ff_hi"], f + 1)
                V.tensor_tensor(plo[:, v, :], pf[:, v, :], phi[:, v, :].bitcast(F32), ALU.subtract)\
                 .then_inc(s["ff_split"], 1)
                if f == 2:
                    dve.wait_ge(s["ple_hi"], 1)
                    V.tensor_tensor(ptlo[:, :, :], pt[:, :, :], pthi[:, :, :].bitcast(F32), ALU.subtract)\
                     .then_inc(s["ple_op"], 1)
            lo_for(W_PLE - 1)
            norm_dve(dve, ch, 5)
            lo_for(W_PLE)
            lo_for(W_PLE + 1)
            for n in range(KT):
                lo_for(W_PLEG + n)
                dve.wait_ge(s["ple_gate"], n + 1)
                ch(V.tensor_tensor(gs[:, n, :], gs[:, n, :], bank(4, T, base=n * T), ALU.mult))
                V.tensor_tensor(x[:, n, :], x[:, n, :], gs[:, n, :], ALU.add).then_inc(s["ple_add"], 1)
                if n in (5, 7):
                    square_add(dve, ch, 6, n // 2 - 1)
            norm_dve(dve, ch, 6, 3)


def columns(w):
    n = w.shape[1] // P
    return np.ascontiguousarray(w.reshape(KT, P, n, P).transpose(2, 1, 0, 3)).reshape(n, P, TW)


def rows_of(w):
    return w.reshape(-1, P, TW)


def interleaved(first, second, third=None):
    last = third if third is not None else second
    head = [first] if third is None else [first, second]
    out = []
    for e in range(len(first) + 1):
        if e < len(first):
            out += [h[e] for h in head]
        if e:
            out.append(last[e - 1])
    return np.stack(out)


def pack(v):
    return np.ascontiguousarray(v.reshape(-1, P).T)


def constants():
    i = np.arange(P)
    low = np.float32(-1e30)
    blk = lambda l: ((i[:, None] >> (l + 1)) == (i[None, :] >> (l + 1))) & (((i[:, None] >> l) & 1) == 1) \
        & (((i[None, :] >> l) & 1) == 0)
    c1 = [i[:, None] <= i[None, :], np.where(i[:, None] > i[None, :], 0, low), blk(0)] + [blk(l).T for l in range(7)]
    t = np.arange(T)
    inv = [np.broadcast_to(np.float32(1) / np.minimum(t + 1, 2 << g).astype(np.float32), (P, T)) for g in range(PG)]
    c1 = np.concatenate([np.asarray(m, np.float32) for m in c1 + inv + [np.where(i[:, None] <= i[None, :], 0, low),
                                                                np.eye(P), np.broadcast_to(i, (P, P))]], axis=1)
    q, k = np.arange(T)[None, :], np.arange(T)[:, None]
    ret = []
    for r in range(RH):
        log_g = np.log(1.0 - 2.0 ** (-5.0 - r))
        d = np.where(q >= k, np.exp(log_g * np.maximum(q - k, 0)), 0.0) * P ** -0.5
        ret += [d[0:P, :], d[P:, P:]]
    dist = np.where(q <= k, (q - k).astype(np.float64), -1e30)
    c2 = np.concatenate(ret + [dist[0:P, 0:P], dist[P:, :]], axis=1).astype(np.float32)
    return c1, c2


def kernel(**a):
    import concourse.bacc as bacc
    from concourse.bass_utils import run_bass_kernel_spmd as run

    a = {k: np.asarray(v) for k, v in a.items()}
    w_in, w_in2 = a["w_in"][0], a["w_in_2"][0]
    c1, c2 = constants()
    m, r = 512, 512
    k_first = lambda w: np.concatenate([w[..., 512:1024], w[..., 0:512], w[..., 1024:]], axis=-1)
    tiles = [
        columns(k_first(w_in[:, 0:4 * 512])), columns(w_in[:, 4 * 512 + 8:]),
        columns(a["w_out"][0]), columns(a["w_query"][0]),
        np.ascontiguousarray(a["expert_down"][0].reshape(N_EXP, P, KT, P).transpose(0, 3, 2, 1)).reshape(N_EXP, P, TW),
        rows_of(a["expert_up"][0]),
        rows_of(np.concatenate([w_in2[:, 2 * m:3 * m], w_in2[:, 3 * m + 2 * r:3 * m + 3 * r]], axis=1)),
        columns(w_in2[:, 0:2 * m]),
        columns(np.concatenate([w_in2[:, 3 * m:3 * m + 2 * r], w_in2[:, 3 * m + 3 * r:]], axis=1)),
        rows_of(a["w_out_2"][0]),
        interleaved(columns(a["w_up_2"][0]), columns(a["w_gate_2"][0]), rows_of(a["w_down_2"][0])),
        a["w_ple_2"][0].reshape(2, P, 2, 4, P).transpose(2, 1, 3, 0, 4).reshape(2, P, TW),
        columns(a["w_ple_gate_2"][0]),
    ]
    w = np.concatenate(tiles)
    assert w.shape[0] == N_TILES
    w = np.ascontiguousarray(w.reshape(N_TILES // 2, 2, P, TW).transpose(0, 2, 1, 3)).reshape(N_TILES // 2, P, 2 * TW)
    vecs = np.concatenate([
        pack(a["norm_mix_w"][0]), np.concatenate([pack(k_first(a["conv_w"][0, j])) for j in range(4)], axis=1),
        pack(a["dn_norm_w"][0]), pack(a["pool_scale"][0]), pack(a["norm_ffn_w"][0]), pack(a["norm_final_w"]),
        pack(a["attn_norm_2"][0]),
        pack(a["ret_norm_2"][0]), pack(a["ffn_norm_2"][0]),
        np.concatenate([pack(a["conv_w_2"][0, j]) for j in range(3)], axis=1), pack(a["conv_b_2"][0]),
        pack(a["ple_norm_2"][0]), pack(a["final_norm_2"])], axis=1)
    feature_major = lambda t: np.ascontiguousarray(t.T.reshape(-1, P, T).transpose(1, 0, 2))
    arrays = {
        "x_t": feature_major(a["x"][0]), "vecs": np.ascontiguousarray(vecs), "wts": w, "c1": c1,
        "gate_w": np.ascontiguousarray(w_in[:, 4 * 512:4 * 512 + 8].reshape(KT, P, 8).transpose(1, 0, 2)),
        "rows": np.concatenate([a["dt_bias"][0], a["a_log"][0]]),
        "w_pool": np.ascontiguousarray(a["w_pool"][0].transpose(1, 0, 2)),
        "keys": np.ascontiguousarray(a["sub_keys"][0].reshape(2 * NH, P, P).transpose(2, 0, 1)),
        "c2": c2, "ple_t": feature_major(a["p_2"][0, 0]),
    }
    nc = bacc.Bacc("TRN2", target_bir_lowering=False, num_devices=1)
    args = [nc.dram_tensor("in_" + n, v.shape, mybir.dt.from_np(v.dtype), kind="ExternalInput").ap()
            for n, v in arrays.items()]
    args.append(nc.dram_tensor("out_0_dram", (P, KT, T), F32, kind="ExternalOutput").ap())
    program(nc, *args)
    got = run(nc, [{"in_" + n: v for n, v in arrays.items()}], core_ids=[0]).results[0]["out_0_dram"]
    return np.ascontiguousarray(got.transpose(1, 0, 2).reshape(D, T).T).reshape(1, T, D)
```
